# Optimizing a Trainium2 kernel written in Bass

```python
import math
import jax, jax.numpy as jnp
from jax import lax
import numpy as np

D_MODEL = 1024
BATCH = 1
SEQ = 256
DEPTH = 2

N_EVEN = (DEPTH + 1) // 2
N_ODD = DEPTH // 2
RMS_EPS = 1e-6

GDN_HEADS = 4
GDN_DK = 128
GDN_DV = 128
GDN_CONV = 4
GDN_CHUNK = 64
GDN_QK = GDN_HEADS * GDN_DK
GDN_VD = GDN_HEADS * GDN_DV
GDN_SPLITS = (GDN_QK, GDN_QK, GDN_VD, GDN_VD, GDN_HEADS, GDN_HEADS)
GDN_COLS = sum(GDN_SPLITS)

RWKV_HEADS = 8
RWKV_HEAD = 64
RWKV_DIM = RWKV_HEADS * RWKV_HEAD
DECAY_LORA = 32
AAA_LORA = 32
MV_LORA = 32
GATE_LORA = 96
RWKV_LN_EPS = 64e-5
RWKV_SPLITS = (RWKV_DIM, RWKV_DIM, RWKV_DIM, DECAY_LORA, AAA_LORA, GATE_LORA)
RWKV_COLS = sum(RWKV_SPLITS)

EV_COLS = GDN_COLS + RWKV_COLS
MIX_WIDTH_EVEN = GDN_VD + RWKV_DIM

DIL_PATTERNS = ((128, 1), (512, 4), (2048, 16))
N_DIL_GROUPS = len(DIL_PATTERNS)
DIL_HEADS = 8
DIL_HEAD_DIM = 64
DIL_WIDTH = DIL_HEADS * DIL_HEAD_DIM
DIL_QKV = N_DIL_GROUPS * DIL_WIDTH
OD_COLS = 3 * DIL_QKV
ATT_BLOCK = 128
ROPE_THETA = 10000.0

N_GROUPS = 4
EXPERTS_PER_GROUP = 4
N_EXPERTS = N_GROUPS * EXPERTS_PER_GROUP
EXPERT_FF = 256
TOP_K_INNER = 2

kernel_name = "hybrid_gdn_rwkv7_dilated_hmoe"

def rmsnorm(x, gain):
    xf = x.astype(jnp.float32)
    y = xf * lax.rsqrt(jnp.mean(xf * xf, axis=-1, keepdims=True) + RMS_EPS)
    return (y * gain.astype(jnp.float32)).astype(x.dtype)

def l2norm(t):
    return t * lax.rsqrt(jnp.sum(t * t, axis=-1, keepdims=True) + 1e-6)

def split_cols(h, sizes):
    return jnp.split(h, np.cumsum(sizes)[:-1].tolist(), axis=-1)

def token_shift(h):
    return jnp.pad(h, ((0, 0), (1, 0), (0, 0)))[:, :-1]

def causal_depthwise_conv(x, w):
    K = w.shape[0]
    S = x.shape[1]
    xp = jnp.pad(x, ((0, 0), (K - 1, 0), (0, 0)))
    return sum(xp[:, i:i + S] * w[i] for i in range(K))

def gated_delta_rule_chunked(q, k, v, g, beta):
    B, S, H, Dk = q.shape
    Dv = v.shape[-1]
    C = GDN_CHUNK
    N = S // C

    def to_chunks(t):
        return jnp.moveaxis(t.reshape(B, N, C, H, *t.shape[3:]), 3, 1)

    q, k, v, g, beta = (to_chunks(t) for t in (q, k, v, g, beta))
    gc = jnp.cumsum(g, axis=-1)
    causal = jnp.tril(jnp.ones((C, C), bool))
    strict = jnp.tril(jnp.ones((C, C), bool), -1)
    diff = gc[..., :, None] - gc[..., None, :]
    decay = jnp.where(causal, jnp.exp(jnp.where(causal, diff, 0.0)), 0.0)
    kb = k * beta[..., None]
    vb = v * beta[..., None]
    L = jnp.where(strict, jnp.einsum('bhnik,bhnjk->bhnij', kb, k) * decay, 0.0)
    eye = jnp.eye(C, dtype=q.dtype)
    rhs = jnp.concatenate([vb, kb * jnp.exp(gc)[..., None]], axis=-1)
    sol = lax.linalg.triangular_solve(L + eye, rhs, left_side=True, lower=True, unit_diagonal=True)
    u, w = sol[..., :Dv], sol[..., Dv:]
    aqk = jnp.einsum('bhnik,bhnjk->bhnij', q, k) * decay
    q_dec = q * jnp.exp(gc)[..., None]
    g_last = gc[..., -1]
    k_dec = k * jnp.exp(g_last[..., None] - gc)[..., None]

    def step(state, inp):
        u_n, w_n, aqk_n, qd_n, kd_n, gl_n = inp
        v_new = u_n - jnp.einsum('bhck,bhkv->bhcv', w_n, state)
        o = jnp.einsum('bhck,bhkv->bhcv', qd_n, state) + jnp.einsum('bhij,bhjv->bhiv', aqk_n, v_new)
        state = state * jnp.exp(gl_n)[..., None, None] + jnp.einsum('bhck,bhcv->bhkv', kd_n, v_new)
        return state, o

    xs = tuple(jnp.moveaxis(t, 2, 0) for t in (u, w, aqk, q_dec, k_dec, g_last))
    s0 = jnp.zeros((B, H, Dk, Dv), q.dtype)
    _, o = lax.scan(step, s0, xs)
    return jnp.transpose(o, (1, 0, 3, 2, 4)).reshape(B, S, H, Dv)

def gdn_mixer(hA, conv_w, A_log, dt_bias, norm_w):
    B, S, _ = hA.shape
    f32 = jnp.float32
    q, k, v, z, a, b = split_cols(hA, GDN_SPLITS)
    qkv = jax.nn.silu(causal_depthwise_conv(jnp.concatenate([q, k, v], axis=-1), conv_w)).astype(f32)
    q, k, v = split_cols(qkv, (GDN_QK, GDN_QK, GDN_VD))
    q = l2norm(q.reshape(B, S, GDN_HEADS, GDN_DK)) * (GDN_DK ** -0.5)
    k = l2norm(k.reshape(B, S, GDN_HEADS, GDN_DK))
    v = v.reshape(B, S, GDN_HEADS, GDN_DV)
    beta = jax.nn.sigmoid(b.astype(f32))
    g = -jnp.exp(A_log.astype(f32)) * jax.nn.softplus(a.astype(f32) + dt_bias.astype(f32))
    o = gated_delta_rule_chunked(q, k, v, g, beta)
    o = rmsnorm(o, norm_w) * jax.nn.silu(z.astype(f32).reshape(B, S, GDN_HEADS, GDN_DV))
    return o.reshape(B, S, GDN_VD)

def rwkv7_scan(r, w, k, v, a, b):
    B, S, H, N = r.shape

    def step(state, inp):
        r_t, w_t, k_t, v_t, a_t, b_t = inp
        sa = jnp.einsum('bhvk,bhk->bhv', state, a_t)
        state = state * w_t[:, :, None, :] + sa[..., None] * b_t[:, :, None, :] + v_t[..., None] * k_t[:, :, None, :]
        return state, jnp.einsum('bhvk,bhk->bhv', state, r_t)

    xs = tuple(jnp.moveaxis(t, 1, 0) for t in (r, w, k, v, a, b))
    s0 = jnp.zeros((B, H, N, N), r.dtype)
    _, y = lax.scan(step, s0, xs)
    return jnp.moveaxis(y, 0, 1)

def rwkv7_mixer(hB, mu, w0, w2, a0, a2, g2, k_k, k_a, r_k, ln_w, ln_b, v_first, vres):
    B, S, _ = hB.shape
    f32 = jnp.float32
    hB = hB.astype(f32)
    hB = hB + mu * (token_shift(hB) - hB)
    r, k, v, hw, ha, hg = split_cols(hB, RWKV_SPLITS)
    w_log = -jax.nn.softplus(-(w0 + jnp.tanh(hw) @ w2)) - 0.5
    decay = jnp.exp(-jnp.exp(w_log))
    a = jax.nn.sigmoid(a0 + ha @ a2)
    g = jax.nn.sigmoid(hg) @ g2
    if vres is None:
        v_first = v
    else:
        hv, vres_mu, v0, v2 = vres
        hv = hv.astype(f32)
        hv = hv + vres_mu * (token_shift(hv) - hv)
        v = v + (v_first - v) * jax.nn.sigmoid(v0 + hv @ v2)

    def heads(t):
        return t.reshape(B, S, RWKV_HEADS, RWKV_HEAD)

    kk = l2norm(heads(k * k_k))
    k = k * (1.0 + (a - 1.0) * k_a)
    r_h, k_h, v_h, a_h = heads(r), heads(k), heads(v), heads(a)
    y = rwkv7_scan(r_h, heads(decay), k_h, v_h, -kk, kk * a_h)
    mean = jnp.mean(y, axis=-1, keepdims=True)
    var = jnp.mean(jnp.square(y - mean), axis=-1, keepdims=True)
    y = ((y - mean) * lax.rsqrt(var + RWKV_LN_EPS)).reshape(B, S, RWKV_DIM) * ln_w + ln_b
    bonus = jnp.sum(r_h * k_h * r_k, axis=-1, keepdims=True) * v_h
    y = y + bonus.reshape(B, S, RWKV_DIM)
    return y * g, v_first

def rope(x, positions):
    half = x.shape[-1] // 2
    inv_freq = ROPE_THETA ** (-jnp.arange(half, dtype=jnp.float32) * 2.0 / x.shape[-1])
    ang = positions.astype(jnp.float32)[..., None] * inv_freq
    cos, sin = jnp.cos(ang)[:, :, None, :], jnp.sin(ang)[:, :, None, :]
    x1, x2 = x[..., :half], x[..., half:]
    return jnp.concatenate([x1 * cos - x2 * sin, x2 * cos + x1 * sin], axis=-1)

def dilated_window_attention(q, k, v, window, dilation):
    B, S, H, Dh = q.shape
    span = window // dilation
    L = S // dilation
    nb = -(-L // ATT_BLOCK)
    Lp = nb * ATT_BLOCK

    def to_blocks(t):
        t = t.reshape(B, L, dilation, H, Dh)
        t = jnp.pad(t, ((0, 0), (0, Lp - L), (0, 0), (0, 0), (0, 0)))
        return jnp.transpose(t.reshape(B, nb, ATT_BLOCK, dilation, H, Dh), (0, 3, 4, 1, 2, 5))

    def with_prev(t):
        prev = jnp.pad(t, ((0, 0), (0, 0), (0, 0), (1, 0), (0, 0), (0, 0)))[:, :, :, :-1]
        return jnp.concatenate([prev, t], axis=-2)

    qb = to_blocks(q)
    kw = with_prev(to_blocks(k))
    vw = with_prev(to_blocks(v))
    s = jnp.einsum('brhnqd,brhnkd->brhnqk', qb, kw) * (Dh ** -0.5)
    qi = jnp.arange(ATT_BLOCK)[:, None]
    kj = jnp.arange(2 * ATT_BLOCK)[None, :]
    rel = ATT_BLOCK + qi - kj
    blk = jnp.arange(nb)[:, None, None]
    valid = (rel >= 0) & (rel <= span) & ((blk > 0) | (kj >= ATT_BLOCK))
    s = jnp.where(valid, s, -jnp.inf)
    m = jnp.max(s, axis=-1, keepdims=True)
    p = jnp.exp(s - m)
    l = jnp.sum(p, axis=-1, keepdims=True)
    o = jnp.einsum('brhnqk,brhnkd->brhnqd', p, vw) / l
    lse = (m + jnp.log(l))[..., 0]

    def from_blocks(t):
        t = jnp.moveaxis(t, (3, 4), (1, 2))
        t = t.reshape(B, Lp, dilation, H, *t.shape[5:])[:, :L]
        return t.reshape(B, S, H, *t.shape[4:])

    return from_blocks(o), from_blocks(lse)

def dilated_mixer(h, positions):
    B, S, _ = h.shape
    q, k, v = split_cols(h.astype(jnp.float32), (DIL_QKV, DIL_QKV, DIL_QKV))
    shp = (B, S, N_DIL_GROUPS * DIL_HEADS, DIL_HEAD_DIM)
    q = rope(q.reshape(shp), positions)
    k = rope(k.reshape(shp), positions)
    v = v.reshape(shp)
    outs, lses = [], []
    for gi, (window, dilation) in enumerate(DIL_PATTERNS):
        sl = slice(gi * DIL_HEADS, (gi + 1) * DIL_HEADS)
        o, lse = dilated_window_attention(q[:, :, sl], k[:, :, sl], v[:, :, sl], window, dilation)
        outs.append(o)
        lses.append(lse)
    wts = jax.nn.softmax(jnp.stack(lses), axis=0)
    o = jnp.sum(wts[..., None] * jnp.stack(outs), axis=0)
    return o.reshape(B, S, DIL_WIDTH)

def hierarchical_moe(x, w_group, w_expert, w1, w3, w2):
    B, S, D = x.shape
    t = x.reshape(B * S, D)
    f32 = jnp.float32
    group_logits = (t @ w_group).astype(f32)
    group_prob = jax.nn.softmax(group_logits, axis=-1)
    g_sel = jnp.argmax(group_logits, axis=-1)
    p_group = jnp.take_along_axis(group_prob, g_sel[:, None], axis=-1)
    exp_logits = jnp.einsum('td,gde->tge', t, w_expert).astype(f32)
    sel_logits = jnp.take_along_axis(exp_logits, g_sel[:, None, None], axis=1)[:, 0]
    top_val, top_idx = lax.top_k(sel_logits, TOP_K_INNER)
    inner = jax.nn.softmax(top_val, axis=-1) * p_group
    expert_id = g_sel[:, None] * EXPERTS_PER_GROUP + top_idx
    gates = jnp.sum(jax.nn.one_hot(expert_id, N_EXPERTS, dtype=f32) * inner[..., None], axis=1)
    h = jax.nn.silu(jnp.einsum('td,edf->tef', t, w1)) * jnp.einsum('td,edf->tef', t, w3)
    y = jnp.einsum('tef,efd->td', h * gates[..., None].astype(h.dtype), w2)
    return y.reshape(B, S, D)

def setup_inputs(seed: int = 0) -> dict:
    key = jax.random.key(seed)
    ks = iter(jax.random.split(key, 48))
    f32 = jnp.float32

    def nrm(shape, scale):
        return jax.random.normal(next(ks), shape, f32) * scale

    def uni(shape, lo, hi):
        return jax.random.uniform(next(ks), shape, f32, lo, hi)

    NE, NO = N_EVEN, N_ODD
    res_scale = (2 * DEPTH) ** -0.5
    dt = jnp.exp(uni((NE, GDN_HEADS), math.log(1e-3), math.log(1e-1)))
    return {
        'x': nrm((BATCH, SEQ, D_MODEL), 1.0),
        'positions': jnp.broadcast_to(jnp.arange(SEQ, dtype=jnp.int32), (BATCH, SEQ)),
        'ev_norm': 1.0 + nrm((NE, D_MODEL), 0.02),
        'ev_w_in': nrm((NE, D_MODEL, EV_COLS), D_MODEL ** -0.5),
        'rwkv_vres_down': nrm((NE - 1, D_MODEL, MV_LORA), D_MODEL ** -0.5),
        'ev_w_out': nrm((NE, MIX_WIDTH_EVEN, D_MODEL), MIX_WIDTH_EVEN ** -0.5 * res_scale),
        'gdn_conv_w': nrm((NE, GDN_CONV, 2 * GDN_QK + GDN_VD), GDN_CONV ** -0.5),
        'gdn_A_log': jnp.log(uni((NE, GDN_HEADS), 1.0, 16.0)),
        'gdn_dt_bias': dt + jnp.log(-jnp.expm1(-dt)),
        'gdn_norm': 1.0 + nrm((NE, GDN_DV), 0.02),
        'rwkv_mu': uni((NE, RWKV_COLS), 0.0, 1.0),
        'rwkv_w0': uni((NE, RWKV_DIM), -6.5, -1.5),
        'rwkv_w2': nrm((NE, DECAY_LORA, RWKV_DIM), 0.1),
        'rwkv_a0': nrm((NE, RWKV_DIM), 0.1),
        'rwkv_a2': nrm((NE, AAA_LORA, RWKV_DIM), AAA_LORA ** -0.5),
        'rwkv_g2': nrm((NE, GATE_LORA, RWKV_DIM), GATE_LORA ** -0.5),
        'rwkv_k_k': 0.85 + nrm((NE, RWKV_DIM), 0.02),
        'rwkv_k_a': 1.0 + nrm((NE, RWKV_DIM), 0.02),
        'rwkv_r_k': nrm((NE, RWKV_HEADS, RWKV_HEAD), 0.1),
        'rwkv_ln_w': 1.0 + nrm((NE, RWKV_DIM), 0.02),
        'rwkv_ln_b': nrm((NE, RWKV_DIM), 0.02),
        'rwkv_vres_mu': uni((NE - 1, MV_LORA), 0.0, 1.0),
        'rwkv_v0': 1.0 + nrm((NE - 1, RWKV_DIM), 0.1),
        'rwkv_v2': nrm((NE - 1, MV_LORA, RWKV_DIM), MV_LORA ** -0.5),
        'od_norm': 1.0 + nrm((NO, D_MODEL), 0.02),
        'od_w_in': nrm((NO, D_MODEL, OD_COLS), D_MODEL ** -0.5),
        'od_w_out': nrm((NO, DIL_WIDTH, D_MODEL), DIL_WIDTH ** -0.5 * res_scale),
        'ffn_norm': 1.0 + nrm((DEPTH, D_MODEL), 0.02),
        'moe_w_group': nrm((DEPTH, D_MODEL, N_GROUPS), D_MODEL ** -0.5),
        'moe_w_expert': nrm((DEPTH, N_GROUPS, D_MODEL, EXPERTS_PER_GROUP), D_MODEL ** -0.5),
        'moe_w1': nrm((DEPTH, N_EXPERTS, D_MODEL, EXPERT_FF), D_MODEL ** -0.5),
        'moe_w3': nrm((DEPTH, N_EXPERTS, D_MODEL, EXPERT_FF), D_MODEL ** -0.5),
        'moe_w2': nrm((DEPTH, N_EXPERTS, EXPERT_FF, D_MODEL), EXPERT_FF ** -0.5 * res_scale),
        'final_norm': 1.0 + nrm((D_MODEL,), 0.02),
    }

def reference(x, positions, ev_norm, ev_w_in, rwkv_vres_down, ev_w_out,
              gdn_conv_w, gdn_A_log, gdn_dt_bias, gdn_norm,
              rwkv_mu, rwkv_w0, rwkv_w2, rwkv_a0, rwkv_a2, rwkv_g2, rwkv_k_k, rwkv_k_a, rwkv_r_k,
              rwkv_ln_w, rwkv_ln_b, rwkv_vres_mu, rwkv_v0, rwkv_v2,
              od_norm, od_w_in, od_w_out,
              ffn_norm, moe_w_group, moe_w_expert, moe_w1, moe_w3, moe_w2,
              final_norm):
    v_first = None
    for layer in range(DEPTH):
        if layer % 2 == 0:
            i = layer // 2
            h = rmsnorm(x, ev_norm[i])
            if i == 0:
                w_in = ev_w_in[0]
            else:
                w_in = jnp.concatenate([ev_w_in[i], rwkv_vres_down[i - 1]], axis=-1)
            proj = h @ w_in
            hA = proj[..., :GDN_COLS]
            hB = proj[..., GDN_COLS:EV_COLS]
            yA = gdn_mixer(hA, gdn_conv_w[i], gdn_A_log[i], gdn_dt_bias[i], gdn_norm[i])
            vres = None if i == 0 else (proj[..., EV_COLS:], rwkv_vres_mu[i - 1], rwkv_v0[i - 1], rwkv_v2[i - 1])
            yB, v_first = rwkv7_mixer(hB, rwkv_mu[i], rwkv_w0[i], rwkv_w2[i], rwkv_a0[i], rwkv_a2[i], rwkv_g2[i],
                                      rwkv_k_k[i], rwkv_k_a[i], rwkv_r_k[i], rwkv_ln_w[i], rwkv_ln_b[i],
                                      v_first, vres)
            mixed = jnp.concatenate([yA, yB], axis=-1).astype(x.dtype) @ ev_w_out[i]
        else:
            i = layer // 2
            h = rmsnorm(x, od_norm[i])
            mixed = dilated_mixer(h @ od_w_in[i], positions).astype(x.dtype) @ od_w_out[i]
        x = x + mixed
        x = x + hierarchical_moe(rmsnorm(x, ffn_norm[layer]), moe_w_group[layer], moe_w_expert[layer],
                                 moe_w1[layer], moe_w3[layer], moe_w2[layer])
    return rmsnorm(x, final_norm)


_drawn_inputs = setup_inputs


def setup_inputs(seed=0):
    import zlib

    import numpy as np

    out = dict(_drawn_inputs(seed))
    spreads = {}
    factors = {'ev_norm': 2.937,
     'gdn_norm': 8.0,
     'rwkv_w2': 8.0,
     'rwkv_a0': 4.221,
     'rwkv_k_k': 6.3,
     'rwkv_k_a': 4.736,
     'rwkv_ln_w': 6.754,
     'rwkv_ln_b': 8.0,
     'od_norm': 8.0,
     'ffn_norm': 2.729,
     'final_norm': 2.742}
    for name, (base, spread) in spreads.items():
        noise = np.random.default_rng([zlib.crc32(name.encode()), seed]).standard_normal(out[name].shape)
        drawn = base * np.exp(spread * noise) if base else spread * noise
        out[name] = __import__('jax').numpy.asarray(drawn.astype(out[name].dtype))
    for name, factor in factors.items():
        out[name] = (out[name] * factor).astype(out[name].dtype)
    return out
```

```python
from contextlib import ExitStack

import numpy as np

import concourse.bass as bass
from concourse import mybir

P = 128
F32 = mybir.dt.float32
I32 = mybir.dt.int32
U32 = mybir.dt.uint32
ALU = mybir.AluOpType
ACT = mybir.ActivationFunctionType
AX = mybir.AxisListType
ADD, SUB, MUL, MAX, EQ = ALU.add, ALU.subtract, ALU.mult, ALU.max, ALU.is_equal

SMALL_DMAS = 23
D = 1024
S = 256
NT = S // P
KC = D // P
RMS_EPS = 1e-6
GH, GD = 4, 128
CONV = 4
RH, RD = 8, 64
RT = RH * RD // P
LORA_W, LORA_A, LORA_G = 32, 32, 96
LN_EPS = 64e-5
NG, NEG_ = 4, 4
NE = NG * NEG_
FF = 256
AH, AD, AG = 8, 64, 3
DILATIONS = (1, 4, 16)
SPAN = 128
ROPE_THETA = 10000.0
CH = 128
LEVELS = 7
DECAY = float(np.exp(-0.5))
FAR = -1.0e30
BANKS = 8

C_Q, C_K, C_V, C_Z, C_AB, C_R, C_RK, C_RV, C_LORA = 0, 512, 1024, 1536, 2048, 2056, 2568, 3080, 3592


def constants():
    i = np.arange(P)[:, None]
    j = np.arange(P)[None, :]
    incl = (i <= j).astype(np.float32)
    strict = (i < j).astype(np.float32)
    parts = {"ident": np.eye(P, dtype=np.float32), "incl": incl, "strict": strict,
             "far": np.where(i <= j, 0.0, FAR).astype(np.float32),
             "heads64": (i // RD == j // RD).astype(np.float32)}
    for l in range(LEVELS):
        b = 1 << l
        parts[f"level{l}"] = ((i // (2 * b) == j // (2 * b)) & (i // b % 2 == 1) & (j // b % 2 == 0)).astype(np.float32)
    parts["causal4"] = np.concatenate([strict, incl, strict, incl], 1)
    parts["invf"] = np.tile((ROPE_THETA ** (-np.arange(AD // 2, dtype=np.float32) * 2.0 / AD)).astype(np.float32), (P, 1))
    parts["rank4"] = np.tile(np.array([4, 3, 2, 1], np.float32), (P, 1))
    place, at = {}, 0
    for name, m in parts.items():
        place[name] = (at, m.shape[1])
        at += m.shape[1]
    masks = []
    for t in range(NT):
        keys = np.arange((t + 1) * P)[None, :]
        rel = (t * P + i) - keys
        masks.append(np.concatenate([np.where((rel >= 0) & (rel % d == 0) & (rel <= SPAN * d), 0.0, FAR)
                                     for d in DILATIONS], 1).astype(np.float32))
    return np.concatenate(list(parts.values()), 1), place, np.concatenate(masks, 1)


P_CONV, P_MU, P_MUL, P_W0, P_A0, P_KK, P_KA, P_RK = 0, 48, 60, 62, 66, 70, 74, 78
P_ROWS = 82


class PsumPlan:

    def __init__(self, sems):
        self.sems = sems
        self.jobs = []
        self.index = {}
        self.first = 0

    def segment(self):
        self.first = len(self.jobs)

    def add(self, name, reader):
        assert name not in self.index, name
        self.index[name] = len(self.jobs)
        self.jobs.append((name, reader, self.first))

    def bank(self, name):
        n = self.index[name]
        return (n - self.jobs[n][2]) % BANKS

    def made(self, name):
        return self.index[name] + 1

    def emptied(self, name):
        n = self.index[name]
        reader = self.jobs[n][1]
        return self.sems[reader], sum(1 for job in self.jobs[:n + 1] if job[1] == reader)

    def must_be_empty(self, name):
        n = self.index[name]
        upto = n - BANKS + 1 if n - self.jobs[n][2] >= BANKS else self.jobs[n][2]
        for reader in ("act", "dve"):
            count = sum(1 for job in self.jobs[:upto] if job[1] == reader)
            if count:
                yield self.sems[reader], count


def trunk(nc, x, positions, ev_norm, ev_w_in, ev_w_out, gdn_conv_w, gdn_A_log, gdn_dt_bias, gdn_norm, rwkv_mu,
          rwkv_w0, rwkv_w2, rwkv_a0, rwkv_a2, rwkv_g2, rwkv_k_k, rwkv_k_a, rwkv_r_k, rwkv_ln_w, rwkv_ln_b,
          od_norm, od_w_in, od_w_out, ffn_norm, moe_w_group, moe_w_expert, moe_w1, moe_w3, moe_w2, final_norm,
          const_mats, attn_masks, out):
    _, CP, _ = constants()
    ctx = ExitStack()

    def sb(name, shape, dt=F32):
        return ctx.enter_context(nc.sbuf_tensor(name, shape, dt))

    def sem(name):
        return ctx.enter_context(nc.semaphore(name))

    consts = sb("consts", [P, const_mats.shape[1]])

    def const(name):
        a, w = CP[name]
        return consts[:, a:a + w]

    ident = const("ident")
    ones = sb("ones", [P, P])
    X = sb("X", [P, NT, D])
    hn = sb("hn", [P, NT, D])
    hT = sb("hT", [P, KC, S])
    strips = sb("strips", [P, 2, KC, 512])
    downs = sb("downs", [P, 2, 2, D])
    work = sb("work", [P, 27648])
    prow = sb("prow", [P, P])
    par = sb("par", [P, P_ROWS])
    npar = sb("npar", [P, 8])
    omka = sb("omka", [P, RT])
    gains = sb("gains", [P, 4, KC])
    loraw = sb("loraw", [LORA_W + LORA_A, 512])
    g2sb = sb("g2sb", [LORA_G, 512])
    lnw = sb("lnw", [P, 512])
    lnb = sb("lnb", [P, 512])
    gnw = sb("gnw", [P, GD])
    gab = sb("gab", [P, 2, GH])
    router = sb("router", [P, 2, KC, NG + NE])
    possb = sb("possb", [P, NT], I32)
    small = sb("small", [P, 512])
    sgate = sb("sgate", [LORA_G, S])
    psum = ctx.enter_context(nc.psum_tensor("psum", [P, BANKS, 512], F32))

    def w_(a, n):
        return work[:, a:a + n]

    dflat = downs[:, :, :, :].rearrange("p a b c -> p (a b c)")
    m4 = w_(0, 8192).rearrange("p (q n) -> p q n", n=512)
    tinv = w_(8192, 6144).rearrange("p (q s n) -> p q s n", s=2, n=P)
    AR = w_(14336, 2048).rearrange("p (t c s n) -> p t c s n", t=RT, c=2, s=2)
    Bt = w_(16384, 1024).rearrange("p (t n) -> p t n", t=RT)
    Kt = w_(17408, 1024).rearrange("p (t n) -> p t n", t=RT)
    KQ = w_(18432, 2048).rearrange("p (h c s n) -> p h c s n", h=GH, c=2, s=2)
    GM = w_(20480, 2048).rearrange("p (q s n) -> p q s n", s=2, n=P)
    zr = w_(22528, 1024).rearrange("p (t n) -> p t n", t=NT)
    UG = w_(23552, 1024).rearrange("p (q n) -> p q n", n=P)
    kbT = w_(24576, 1024).rearrange("p (s n) -> p s n", s=2)
    kdec = w_(25600, 512)
    Gb = w_(26112, 1536).rearrange("p (b n) -> p b n", b=3)
    vrow = hn[:, 0, :].rearrange("p (t n) -> p t n", t=NT)
    gvrow = hn[:, 1, :].rearrange("p (t n) -> p t n", t=NT)
    rawB = w_(0, 12 * 257).rearrange("p (t n) -> p t n", n=257)
    rawA = w_(3084, 12 * 259).rearrange("p (t n) -> p t n", n=259)
    rawL = w_(6192, 514).rearrange("p (t n) -> p t n", n=257)
    convv = w_(6706, 1024).rearrange("p (t n) -> p t n", t=4)
    fk, fr, fsg, fal, fd, fdx = [w_(8192 + 1024 * n, 1024).rearrange("p (t n) -> p t n", t=RT) for n in range(6)]
    fv, fe2, fkk, ft = [dflat[:, 1024 * n:1024 * (n + 1)].rearrange("p (t n) -> p t n", t=RT) for n in range(4)]
    gtmp = w_(20480, 2048)

    def gtmp_h(n):
        return gtmp[:, 1024 * (n % 2):1024 * (n % 2) + 1024].rearrange("p (h c n) -> p h c n", h=GH, c=2)

    conv_out = [KQ[:, :, :, 0, :], KQ[:, :, :, 1, :], convv.rearrange("p h (c n) -> p h c n", c=2)]
    wsb = dflat[:, 0:512]
    un = dflat[:, 512:1024]
    state_r = dflat[:, 1024:1536].rearrange("p (t n) -> p t n", t=RT)
    vnew = dflat[:, 1536:2048]
    r1 = dflat[:, 2048:2560]
    state_g = dflat[:, 2560:3072].rearrange("p (h n) -> p h n", h=GH)
    tmpd = dflat[:, 3072:3584]
    ycat = hT[:, :, :].rearrange("p c n -> p (c n)").rearrange("p (t n) -> p t n", t=NT)
    yT = w_(14336, 2048).rearrange("p (c n) -> p c n", c=KC)
    qkv = w_(0, 2 * 4608).rearrange("p (t n) -> p t n", t=NT)
    qkT = w_(9216, 6144).rearrange("p (i n) -> p i n", n=S)
    masks = w_(15360, 1152)
    probs = w_(16512, 1536).rearrange("p (b n) -> p b n", b=2)
    pT = w_(18048, 1536).rearrange("p (b n) -> p b n", b=2)
    scs = w_(19584, 1536).rearrange("p (b n) -> p b n", b=2)
    rtmp = w_(21120, 2048).rearrange("p (b s n) -> p b s n", b=2, s=2)
    trig = w_(23168, 512)
    arow = w_(23680, 1024).rearrange("p (t n) -> p t n", t=NT)
    aT = w_(24704, 1024).rearrange("p (c n) -> p c n", c=4)
    moes = w_(26112, 512).rearrange("p (t n) -> p t n", t=NT)
    moeg = w_(26624, 512).rearrange("p (t n) -> p t n", t=NT)
    moegT = w_(27136, 512).rearrange("p (t k n) -> p t k n", t=NT, k=2)
    sm = {}
    at = GC0 = 0
    for name, n in (("ssq", 2), ("rstd", 2), ("ab", 16), ("beta", 8), ("gx", 8), ("ga", 8), ("gg", 8), ("gc", 8),
                    ("glast", 8), ("egc", 8), ("kd", 8), ("fs", 4), ("bonus", 16), ("stat", 16), ("stat2", 16),
                    ("logits", 40), ("gm", 2), ("gt", 8), ("gt2", 2), ("goh", 8), ("ge", 8), ("gs", 2), ("pg", 2),
                    ("sel", 8), ("v1", 2), ("v2", 2), ("oh1", 8), ("oh2", 8), ("s2", 8), ("dv", 2), ("i1", 2),
                    ("i2", 2), ("inn", 8), ("gates", 32), ("mx", 2), ("nmx", 2), ("den", 2), ("rden", 2), ("eal", 4), ("mark", 2)):
        sm[name] = small[:, at:at + n]
        GC0 = at if name == "gc" else GC0
        at += n
    assert at <= 512
    sm["gc2"] = small[:, GC0:GC0 + 16]
    gates = sm["gates"].rearrange("p (t e) -> p t e", t=NT)

    made, act_read, dve_read = sem("made"), sem("act_read"), sem("dve_read")
    s_act, s_dve, s_pool = sem("act_steps"), sem("dve_steps"), sem("pool_steps")
    d_const, d_x, d_par, d_small, d_mask = sem("d_const"), sem("d_x"), sem("d_par"), sem("d_small"), sem("d_mask")
    d_fin, d_out = sem("d_fin"), sem("d_out")
    d_strip = [sem(f"d_strip{b}") for b in range(2)]
    d_down = [sem(f"d_down{b}") for b in range(2)]
    ones_set, pads_set, m4_zero = sem("ones_set"), sem("pads_set"), sem("m4_zero")
    sq_done, hn_ready = sem("sq_done"), sem("hn_ready")
    mixl_ready, lorain_ready, sgate_ready = sem("mixl_ready"), sem("lorain_ready"), sem("sgate_ready")
    npar_ready = sem("npar_ready")
    kksq_ready, rkr_ready, cols_ready, decay_in, decay_out = (sem("kksq_ready"), sem("rkr_ready"), sem("cols_ready"),
                                                               sem("decay_in"), sem("decay_out"))
    fv_ready, convv_ready, conv_done, silu_in, silu_exp = (sem("fv_ready"), sem("convv_ready"), sem("conv_done"),
                                                           sem("silu_in"), sem("silu_exp"))
    silu_out, rden_ready = sem("silu_out"), sem("rden_ready")
    gsq_ready, kq_ready = sem("gsq_ready"), sem("kq_ready")
    gate_in, gate_exp, g_ready, ug_ready, dt_in, dt_exp, gc_exp = (sem("gate_in"), sem("gate_exp"), sem("g_ready"),
                                                                   sem("ug_ready"), sem("dt_in"), sem("dt_exp"),
                                                                   sem("gc_exp"))
    early_done, tinv_set = sem("early_done"), sem("tinv_set")
    r1_ready, z_exp, ycat_ready = sem("r1_ready"), sem("z_exp"), sem("ycat_ready")
    x_ready = sem("x_ready")
    route_in, route_exp, gates_ready = sem("route_in"), sem("route_exp"), sem("gates_ready")
    root_in, root_out = sem("root_in"), sem("root_out")
    h_made, silu_done, g_made, gT_made, gT_copied, y_made = (sem("h_made"), sem("silu_done"), sem("g_made"),
                                                             sem("gT_made"), sem("gT_copied"), sem("y_made"))
    trig_in, trig_done, rope_ready, roped = sem("trig_in"), sem("trig_done"), sem("rope_ready"), sem("roped")
    scores_ready, probs_ready, out_ready = sem("scores_ready"), sem("probs_ready"), sem("out_ready")

    plan = PsumPlan({"act": act_read, "dve": dve_read})

    def plan_norm(tag):
        for n in range(4):
            plan.add(f"{tag}nt{n}", "dve")

    INV0 = [(l, g) for l in range(LEVELS) for g in range(6)]
    plan.add("params", "dve")
    plan_norm("a")
    for n in ("lora", "ab", "k0", "k1", "r0", "r1", "v0", "v1"):
        plan.add(n, "act")
    for n in ("wz0", "wz1", "az0", "az1"):
        plan.add(n, "act")
    for n in ("gk0", "gk1", "gq0", "gq1", "gv0", "gv1", "z0", "z1"):
        plan.add(n, "act")
    for n in ("ss0", "ss1", "bon"):
        plan.add(n, "dve")
    for n in ("vt0", "vt1"):
        plan.add(n, "act")
    for n in ("gss0", "gss1", "gss2", "gss3", "gc", "gb0", "gb1"):
        plan.add(n, "dve")
    for n in ("gvt0", "gvt1", "kt0", "bt0"):
        plan.add(n, "act")
    plan.add("gkt", "dve")
    for n in range(4):
        plan.add(f"ga{n}", "dve")
    for q in range(16):
        plan.add(f"m{q}", "dve")
    for n, (l, g) in enumerate(INV0):
        if n == 0:
            plan.add(f"i1_{l}_{g}", "dve")
        if n + 1 < len(INV0):
            l1, g1 = INV0[n + 1]
            plan.add(f"i1_{l1}_{g1}", "dve")
        plan.add(f"i2_{l}_{g}", "dve")
        plan.add(f"i3_{l}_{g}", "dve")
    for n, e in (("w0", "act"), ("gz0", "dve"), ("u0", "act"), ("gs1", "act"), ("st", "dve"), ("y0", "act"),
                 ("gp1", "dve"), ("go0", "act"), ("w1", "act"), ("gz1", "dve"), ("u1", "act"), ("go1", "act"),
                 ("gos", "dve"), ("y1", "act"), ("lg0", "dve"), ("lg1", "dve")):
        plan.add(n, e)
    for n in range(4):
        plan.add(f"yt{n}", "act")
    for t in range(NT):
        for half in range(2):
            plan.add(f"op{t}{half}", "dve")
    plan_norm("b")
    plan.add("brl", "dve")
    plan.segment()
    plan_norm("c")
    for s in range(9):
        for t in range(NT):
            plan.add(f"s{s}{t}", "dve" if s < 6 else "act")
            if s < 6 and (s, t) != (0, 0):
                sp_, tp = (s, t - 1) if t else (s - 1, 1)
                plan.add(f"qt{sp_}{tp}", "act")
            if (s, t) == (6, 0):
                plan.add("qt51", "act")
    HT_ = [(h, t) for h in range(AH) for t in range(NT)]

    def plan_scores(h, t):
        plan.add(f"sc{h}{t}a", "dve")
        if t:
            plan.add(f"sc{h}{t}b", "dve")

    plan_scores(0, 0)
    for n, (h, t) in enumerate(HT_):
        if n + 1 < len(HT_):
            plan_scores(*HT_[n + 1])
        plan.add(f"pt{h}{t}a", "act")
        if t:
            plan.add(f"pt{h}{t}b", "act")
        plan.add(f"pv{h}{t}", "act")
    for n in range(2):
        plan.add(f"at{n}", "act")
    for t in range(NT):
        for half in range(2):
            plan.add(f"ao{t}{half}", "dve")
    plan_norm("d")
    plan.add("drl", "dve")

    EV = [("small", 0), ("ev", C_RK), ("ev", C_R), ("ev", C_RV), ("ev", C_K), ("ev", C_Q), ("ev", C_V), ("ev", C_Z),
          ("evo", 0), ("evo", 512)]
    OD = [("od", 512 * n) for n in range(9)] + [("odo", 0)]
    MOE0 = len(EV)
    ODB = MOE0 + NE
    MOE1 = ODB + len(OD)
    last_use = {0: "ab", 1: "k1", 2: "r1", 3: "v1", 4: "gk1", 5: "gq1", 6: "gv1", 7: "z1", 8: "op10", 9: "op11"}
    for n in range(9):
        last_use[ODB + n] = f"s{n}1"
    last_use[ODB + 9] = "ao11"

    def strip_landed(n):
        return d_strip[n % 2], 32 * (n // 2 + 1)

    ev_k = ev_w_in[0].rearrange("(p c) n -> p c n", c=KC)
    od_k = od_w_in[0].rearrange("(p c) n -> p c n", c=KC)
    evo_k = ev_w_out[0].rearrange("(c p) n -> p c n", p=P)
    odo_k = od_w_out[0].rearrange("(c p) n -> p c n", p=P)

    block = ctx.enter_context(nc.Block())

    @block.sync
    def _(sp):
        xr = x[0].rearrange("(t p) n -> p t n", p=P)
        for t in range(NT):
            sp.dma_start(X[:, t, :], xr[:, t, :]).then_inc(d_x, 16)
        sp.dma_start(consts[:, :], const_mats).then_inc(d_const, 16)
        rows = [(P_CONV, gdn_conv_w[0].rearrange("k (t p) -> (k t) p", p=P), 48),
                (P_MU, rwkv_mu[:, 0:1536].rearrange("o (t p) -> (o t) p", p=P), 12),
                (P_W0, rwkv_w0.rearrange("o (t p) -> (o t) p", p=P), 4),
                (P_A0, rwkv_a0.rearrange("o (t p) -> (o t) p", p=P), 4),
                (P_KK, rwkv_k_k.rearrange("o (t p) -> (o t) p", p=P), 4),
                (P_KA, rwkv_k_a.rearrange("o (t p) -> (o t) p", p=P), 4),
                (P_RK, rwkv_r_k[0].rearrange("(t h) d -> t (h d)", h=2), 4)]
        sp.wait_ge(pads_set, 1)
        for r, src, n in rows:
            sp.dma_start(prow[r:r + n, :], src).then_inc(d_par, 16)
        sp.dma_start(prow[P_MUL:P_MUL + 1, 0:64], rwkv_mu[:, 1536:1600]).then_inc(d_par, 16)
        sp.dma_start(prow[P_MUL + 1:P_MUL + 2, 0:96], rwkv_mu[:, 1600:1696]).then_inc(d_par, 16)
        for n, src in enumerate((ev_norm[0], ffn_norm[0], od_norm[0], ffn_norm[1])):
            sp.dma_start(gains[:, n, :], src.rearrange("(p c) -> p c", c=KC)).then_inc(d_small, 16)

        def strip(n, kind, arg):
            slot = strips[:, n % 2]
            if n - 2 in last_use:
                sp.wait_ge(made, plan.made(last_use[n - 2]))
            elif n >= 2:
                sp.wait_ge(h_made, 3 + 2 * (n - 2 - MOE0 + 1))
            if kind == "small":
                sp.dma_start(slot[:, :, 0:8], ev_k[:, :, C_AB:C_AB + 8]).then_inc(d_strip[n % 2], 16)
                sp.dma_start(slot[:, :, 8:168], ev_k[:, :, C_LORA:C_LORA + 160]).then_inc(d_strip[n % 2], 16)
                return
            src = {"ev": ev_k, "od": od_k, "evo": evo_k, "odo": odo_k}[kind]
            if kind == "odo":
                dst = slot.rearrange("p (c a) n -> p c (a n)", a=2)
                for c in (0, 2):
                    sp.dma_start(dst[:, c:c + 2, :], src[:, c:c + 2, :]).then_inc(d_strip[n % 2], 16)
                return
            for c in (0, 4):
                sp.dma_start(slot[:, c:c + 4, :], src[:, c:c + 4, arg:arg + 512]).then_inc(d_strip[n % 2], 16)

        strip(0, *EV[0])
        strip(1, *EV[1])
        small_dmas = [(loraw[0:32, :], rwkv_w2[0]), (loraw[32:64, :], rwkv_a2[0]), (g2sb[:, :], rwkv_g2[0]),
                      (lnw[:, :], rwkv_ln_w[0].partition_broadcast(P)), (lnb[:, :], rwkv_ln_b[0].partition_broadcast(P)),
                      (gnw[:, :], gdn_norm[0].partition_broadcast(P)),
                      (gab[:, 0, :], gdn_A_log[0].partition_broadcast(P)),
                      (gab[:, 1, :], gdn_dt_bias[0].partition_broadcast(P)),
                      (possb[:, :], positions[0].rearrange("(t p) -> p t", p=P))]
        for l in range(2):
            small_dmas.append((router[:, l, :, 0:NG], moe_w_group[l].rearrange("(p c) g -> p c g", c=KC)))
            for g in range(NG):
                small_dmas.append((router[:, l, :, NG + 4 * g:NG + 4 * g + 4],
                                   moe_w_expert[l, g].rearrange("(p c) e -> p c e", c=KC)))
        assert 4 + len(small_dmas) == SMALL_DMAS
        for dst, src in small_dmas:
            sp.dma_start(dst, src, allow_slow_non_contiguous=True).then_inc(d_small, 16)
        for n in range(2, len(EV)):
            strip(n, *EV[n])

        def experts(layer, first):
            with sp.Fori(0, NE // 2) as i:
                for u in range(2):
                    sp.wait_ge(h_made, i * 4 + ((2 * NE + 3) * layer + 2 * u + 1))
                    n = first + u
                    w1 = moe_w1[layer, bass.ds(i * 2 + u, 1)].rearrange("o (p c) f -> p (o c) f", c=KC)
                    w3 = moe_w3[layer, bass.ds(i * 2 + u, 1)].rearrange("o (p c) f -> p (o c) f", c=KC)
                    sp.dma_start(strips[:, n % 2, :, 0:FF], w1).then_inc(d_strip[n % 2], 16)
                    sp.dma_start(strips[:, n % 2, :, FF:2 * FF], w3).then_inc(d_strip[n % 2], 16)
                    sp.wait_ge(y_made, i * 2 + ((NE + 2) * layer + u + 1))
                    w2 = moe_w2[layer, bass.ds(i * 2 + u, 1)].rearrange("o (c p) n -> p (o c) n", p=P)
                    sp.dma_start(downs[:, u, :, :], w2).then_inc(d_down[u], 16)

        sp.wait_ge(made, plan.made("op11"))
        experts(0, MOE0)
        sp.dma_start(masks, attn_masks).then_inc(d_mask, 16)
        for n, (kind, arg) in enumerate(OD):
            strip(ODB + n, kind, arg)
        sp.wait_ge(made, plan.made("ao11"))
        experts(1, MOE1)
        sp.dma_start(w_(0, D), final_norm.partition_broadcast(P)).then_inc(d_fin, 16)
        outr = out[0].rearrange("(t p) n -> p t n", p=P)
        for t in range(NT):
            sp.wait_ge(out_ready, t + 1)
            sp.dma_start(outr[:, t, :], hn[:, t, :]).then_inc(d_out, 16)
        sp.wait_ge(d_out, 16 * NT)

    @block.gpsimd
    def _(pool):
        nc.gpsimd.memset(prow[:, :], 0.0).then_inc(pads_set, 1)
        nc.gpsimd.memset(ones[:, :], 1.0).then_inc(ones_set, 1)
        nc.gpsimd.memset(rawB[:, :, 0:1], 0.0)
        nc.gpsimd.memset(rawL[:, :, 0:1], 0.0)
        nc.gpsimd.memset(rawA[:, :, 0:3], 0.0).then_inc(pads_set, 1)
        pool.wait_ge(early_done, 1)
        pool.wait_ge(*plan.emptied("gvt1"))
        nc.gpsimd.memset(w_(0, 8192), 0.0).then_inc(m4_zero, 1)
        pool.wait_ge(d_const, 16)
        nc.gpsimd.tensor_copy(w_(8192, 6144).rearrange("p (q n) -> p q n", n=P),
                              ident.unsqueeze(1).broadcast_to([P, 48, P])).then_inc(tinv_set, 1)
        for s in range(6):
            for t in range(NT):
                n = NT * s + t
                pool.wait_ge(rope_ready, n + 1)
                nc.gpsimd.tensor_tensor(qkv[:, t, 512 * s:512 * s + 512], rtmp[:, n % 2, 0, 0:512],
                                        rtmp[:, n % 2, 1, 0:512], ADD).then_inc(roped, 1)

    @block.scalar
    def _(act):
        steps = [0]

        def step(ins):
            steps[0] += 1
            ins.then_inc(s_act, 1)
            act.wait_ge(s_act, steps[0])

        def take(name):
            act.wait_ge(made, plan.made(name))
            return psum[:, plan.bank(name), :]

        roots = [0]

        def root(m):
            roots[0] += 1
            act.wait_ge(root_in, roots[0])
            nc.scalar.activation(m, m, ACT.Sqrt).then_inc(root_out, 1)

        def norm_squares(k):
            for t in range(NT):
                act.wait_ge(*((d_x, 16 * NT) if k == 0 else (x_ready, NT * (k - 1) + t + 1)))
                nc.scalar.activation(hn[:, t, :], X[:, t, :], ACT.Square,
                                     accum_out=sm["ssq"][:, t:t + 1]).then_inc(sq_done, 1)
            root(sm["rstd"])

        norm_squares(0)
        act.wait_ge(pads_set, 2)
        b = take("lora")
        nc.scalar.copy(rawL[0:64, 0, 1:257], b[0:64, 0:256])
        nc.scalar.copy(rawL[0:96, 1, 1:257], b[0:96, 256:512]).then_inc(act_read, 1)
        b = take("ab")
        nc.scalar.copy(sm["ab"], b[:, 0:16]).then_inc(act_read, 1)
        for n, name in enumerate(("k0", "k1", "r0", "r1", "v0", "v1")):
            b = take(name)
            nc.scalar.copy(rawB[:, 2 * n:2 * n + 2, 1:257], b.rearrange("p (t n) -> p t n", t=2)).then_inc(act_read, 1)
        act.wait_ge(mixl_ready, 2)
        nc.scalar.activation(fe2[0:32, 0, :], fe2[0:32, 0, :], ACT.Tanh).then_inc(lorain_ready, 1)
        nc.scalar.activation(sgate[:, :], fe2[0:96, 1, :], ACT.Exp, scale=-1.0).then_inc(lorain_ready, 1)
        act.wait_ge(npar_ready, 1)
        for k, (name, dst) in enumerate((("wz0", fsg), ("wz1", fsg), ("az0", fal), ("az1", fal))):
            b = take(name)
            for j in range(2):
                t = 2 * (k % 2) + j
                ins = nc.scalar.activation(dst[:, t, :], b[:, 256 * j:256 * j + 256], ACT.Exp, scale=-1.0,
                                           bias=npar[:, 4 * (k // 2) + t:4 * (k // 2) + t + 1])
            ins.then_inc(act_read, 1)
        for n, name in enumerate(("gk0", "gk1", "gq0", "gq1", "gv0", "gv1")):
            b = take(name)
            nc.scalar.copy(rawA[:, 2 * n:2 * n + 2, 3:259], b.rearrange("p (t n) -> p t n", t=2)).then_inc(act_read, 1)
        for t in range(NT):
            b = take(f"z{t}")
            nc.scalar.copy(zr[:, t, :], b).then_inc(act_read, 1)
        act.wait_ge(decay_in, 1)
        nc.scalar.activation(fe2, fd, ACT.Exp, scale=-DECAY).then_inc(decay_out, 1)
        act.wait_ge(decay_out, 1)
        nc.scalar.activation(fd, fd, ACT.Exp, scale=DECAY).then_inc(decay_out, 1)
        nc.scalar.activation(fdx, fdx, ACT.Exp, scale=-DECAY).then_inc(decay_out, 1)
        act.wait_ge(decay_in, 2)
        nc.scalar.activation(sm["fs"], sm["fs"], ACT.Exp, scale=-DECAY).then_inc(decay_out, 1)
        root(ft)
        for t in range(NT):
            b = take(f"vt{t}")
            nc.scalar.copy(vrow[:, t, :], b).then_inc(act_read, 1)
        for n in range(3):
            act.wait_ge(silu_in, n + 1)
            if n == 2:
                act.wait_ge(silu_out, 1)
            nc.scalar.activation(gtmp_h(n), conv_out[n], ACT.Exp, scale=-1.0).then_inc(silu_exp, 1)
        act.wait_ge(*plan.emptied("ab"))
        abv = sm["ab"].rearrange("p (c s h) -> p c s h", c=2, s=2)
        nc.scalar.activation(sm["beta"].rearrange("p (c h) -> p c h", c=2), abv[:, :, 1, :], ACT.Exp,
                             scale=-1.0).then_inc(gate_exp, 1)
        act.wait_ge(d_small, 16 * SMALL_DMAS)
        nc.scalar.activation(sm["eal"], gab[:, 0, :], ACT.Exp).then_inc(gate_exp, 1)
        act.wait_ge(gate_in, 1)
        nc.scalar.activation(sm["ga"], sm["gg"], ACT.Exp, scale=-1.0).then_inc(gate_exp, 1)
        act.wait_ge(gate_exp, 3)
        nc.scalar.activation(sm["ga"], sm["ga"], ACT.Ln, bias=1.0).then_inc(gate_exp, 1)
        root(gtmp)
        act.wait_ge(dt_in, 1)
        nc.scalar.activation(GM[:, :, 1, :], GM[:, :, 1, :], ACT.Exp).then_inc(dt_exp, 1)
        nc.scalar.activation(sm["egc"], sm["gc"], ACT.Exp).then_inc(gc_exp, 1)
        nc.scalar.activation(sm["kd"], sm["kd"], ACT.Exp).then_inc(gc_exp, 1)
        for t in range(NT):
            b = take(f"gvt{t}")
            nc.scalar.copy(gvrow[:, t, :], b).then_inc(act_read, 1)
        for s, name in enumerate(("kt0", "bt0")):
            b = take(name)
            nc.scalar.copy(kbT[:, s, :], b).then_inc(act_read, 1)
        nc.scalar.activation(UG.rearrange("p (t q) n -> p t (q n)", t=NT), zr, ACT.Exp, scale=-1.0).then_inc(z_exp, 1)
        b = take("w0")
        nc.scalar.copy(wsb, b).then_inc(act_read, 1)
        b = take("u0")
        nc.scalar.mul(un, b, -1.0).then_inc(act_read, 1)
        b = take("gs1")
        nc.scalar.copy(state_g.rearrange("p h n -> p (h n)"), b).then_inc(act_read, 1)
        b = take("y0")
        nc.scalar.copy(ycat[:, 0, 512:1024], b).then_inc(act_read, 1)
        b = take("go0")
        nc.scalar.copy(ycat[:, 0, 0:512], b).then_inc(act_read, 1)
        b = take("w1")
        nc.scalar.copy(wsb, b).then_inc(act_read, 1)
        b = take("u1")
        nc.scalar.mul(un, b, -1.0).then_inc(act_read, 1)
        b = take("go1")
        nc.scalar.copy(ycat[:, 1, 0:512], b).then_inc(act_read, 1)
        b = take("y1")
        nc.scalar.copy(ycat[:, 1, 512:1024], b).then_inc(act_read, 1)
        root(sm["stat"][:, 0:8])
        root(sm["stat2"])
        for n in range(4):
            b = take(f"yt{n}")
            nc.scalar.copy(yT[:, 2 * n:2 * n + 2, :], b.rearrange("p (c n) -> p c n", c=2)).then_inc(act_read, 1)

        def moe(layer):
            act.wait_ge(route_in, 2 * layer + 1)
            nc.scalar.activation(sm["ge"], sm["ge"], ACT.Exp).then_inc(route_exp, 1)
            act.wait_ge(route_in, 2 * layer + 2)
            nc.scalar.activation(sm["dv"], sm["dv"], ACT.Exp).then_inc(route_exp, 1)
            for k in range(2):
                nc.scalar.copy(sm["gs"][:, k:k + 1], ident[:, 0:1]).then_inc(gT_copied, 1)
            with act.Fori(0, NE) as e:
                for t in range(NT):
                    act.wait_ge(h_made, e * 2 + ((2 * NE + 3) * layer + 3 + t + 1))
                    act.wait_ge(g_made, e * 2 + ((2 * NE + 2) * layer + t + 1))
                    nc.scalar.activation(moes[:, t, :], psum[:, 4 + t, 0:FF], ACT.Silu).then_inc(silu_done, 1)
                for t in range(NT):
                    act.wait_ge(gT_made, e * 2 + (2 * NE * layer + t + 1))
                    nc.scalar.copy(moegT[:, t, :, :], psum[:, 6 + t, 0:2 * P].rearrange("p (k n) -> p k n", k=2)
                                   ).then_inc(gT_copied, 1)

        norm_squares(1)
        moe(0)
        norm_squares(2)
        act.wait_ge(trig_in, 1)
        nc.scalar.activation(trig[:, 128:256], trig[:, 128:256], ACT.Sin).then_inc(trig_done, 1)

        def copy_qkT(s, t):
            b = take(f"qt{s}{t}")
            nc.scalar.copy(qkT[:, 4 * s:4 * s + 4, P * t:P * t + P],
                           b.rearrange("p (j n) -> p j n", j=4)).then_inc(act_read, 1)

        for s in range(9):
            for t in range(NT):
                if s >= 6:
                    b = take(f"s{s}{t}")
                    nc.scalar.copy(qkv[:, t, 512 * s:512 * s + 512], b).then_inc(act_read, 1)
                if s < 6 and (s, t) != (0, 0):
                    copy_qkT(*((s, t - 1) if t else (s - 1, 1)))
                if (s, t) == (6, 0):
                    copy_qkT(5, 1)
        for n, (h, t) in enumerate(HT_):
            keys = AG * P * (t + 1)
            act.wait_ge(scores_ready, n + 1)
            nc.scalar.activation(probs[:, n % 2, 0:keys], scs[:, n % 2, 0:keys], ACT.Exp,
                                 bias=sm["nmx"][:, n % 2:n % 2 + 1],
                                 accum_out=sm["den"][:, n % 2:n % 2 + 1]).then_inc(probs_ready, 1)
            b = take(f"pt{h}{t}a")
            w = 384 if t == 0 else 512
            nc.scalar.copy(pT[:, n % 2, 0:w], b[:, 0:w]).then_inc(act_read, 1)
            if t:
                b = take(f"pt{h}{t}b")
                nc.scalar.copy(pT[:, n % 2, 512:768], b[:, 0:256]).then_inc(act_read, 1)
            b = take(f"pv{h}{t}")
            act.wait_ge(rden_ready, n + 1)
            nc.scalar.activation(arow[:, t, AD * h:AD * h + AD], b[:, 0:AD], ACT.Copy,
                                 scale=sm["rden"][:, n % 2:n % 2 + 1]).then_inc(act_read, 1)
        for n in range(2):
            b = take(f"at{n}")
            nc.scalar.copy(aT[:, 2 * n:2 * n + 2, :], b.rearrange("p (c n) -> p c n", c=2)).then_inc(act_read, 1)
        norm_squares(3)
        moe(1)
        norm_squares(4)

    @block.tensor
    def _(pe):
        seen = {}

        def fill(name):
            for s_, v in plan.must_be_empty(name):
                if v > seen.get(id(s_), 0):
                    seen[id(s_)] = v
                    pe.wait_ge(s_, v)
            return psum[:, plan.bank(name), :]

        def mm(out_, lhsT, rhs, start=True, stop=True, shared=False):
            return nc.tensor.matmul(out_, lhsT, rhs, start=start, stop=stop, skip_group_check=shared)

        def norm_columns(tag, k):
            pe.wait_ge(hn_ready, k + 1)
            for n in range(4):
                b = fill(f"{tag}nt{n}")
                for j in range(2):
                    for t in range(NT):
                        c = 2 * n + j
                        ins = nc.tensor.transpose(b[:, 256 * j + P * t:256 * j + P * t + P],
                                                  hn[:, t, P * c:P * c + P], ident)
                ins.then_inc(made, 1)

        def col_pair(name, n, j0):
            b = fill(name)
            for j in range(2):
                for c in range(KC):
                    ins = mm(b[:, 256 * j:256 * j + 256], strips[:, n % 2, c, P * (j0 + j):P * (j0 + j) + P],
                             hT[:, c, :], c == 0, c == KC - 1)
            ins.then_inc(made, 1)

        def rows_of(name, n, t, lhs, kc, rhs_of):
            b = fill(name)
            for c in range(kc):
                ins = mm(b, lhs[:, c, P * t:P * t + P], rhs_of(c), c == 0, c == kc - 1)
            ins.then_inc(made, 1)

        pe.wait_ge(d_const, 16)
        pe.wait_ge(d_par, 16 * 9)
        b = fill("params")
        nc.tensor.transpose(b[:, 0:P], prow[:, :], ident).then_inc(made, 1)
        norm_columns("a", 0)
        pe.wait_ge(*plan.emptied("ant3"))
        pe.wait_ge(*strip_landed(0))
        b = fill("lora")
        for j, (a0, w) in enumerate(((8, 64), (72, 96))):
            for c in range(KC):
                ins = mm(b[0:w, 256 * j:256 * j + 256], strips[:, 0, c, a0:a0 + w], hT[:, c, :], c == 0, c == KC - 1)
        ins.then_inc(made, 1)
        b = fill("ab")
        for t in range(NT):
            for c in range(KC):
                ins = mm(b[:, 8 * t:8 * t + 8], hT[:, c, P * t:P * t + P], strips[:, 0, c, 0:8], c == 0, c == KC - 1)
        ins.then_inc(made, 1)
        for n, name in ((1, "k"), (2, "r"), (3, "v")):
            pe.wait_ge(*strip_landed(n))
            col_pair(f"{name}0", n, 0)
            col_pair(f"{name}1", n, 2)
        pe.wait_ge(d_small, 16 * SMALL_DMAS)
        pe.wait_ge(lorain_ready, 1)
        for name, lo, hi in (("wz", 0, 32), ("az", 32, 64)):
            for k in range(2):
                b = fill(f"{name}{k}")
                for j in range(2):
                    c0 = P * (2 * k + j)
                    ins = mm(b[:, 256 * j:256 * j + 256], loraw[lo:hi, c0:c0 + P], fe2[lo:hi, 0, :])
                ins.then_inc(made, 1)
        for n, name in ((4, "gk"), (5, "gq"), (6, "gv")):
            pe.wait_ge(*strip_landed(n))
            col_pair(f"{name}0", n, 0)
            col_pair(f"{name}1", n, 2)
        pe.wait_ge(*strip_landed(7))
        for t in range(NT):
            rows_of(f"z{t}", 7, t, hT, KC, lambda c: strips[:, 1, c, :])
        pe.wait_ge(kksq_ready, 1)
        for k in range(2):
            b = fill(f"ss{k}")
            for j in range(2):
                ins = mm(b[:, 256 * j:256 * j + 256], const("heads64"), ft[:, 2 * k + j, :])
            ins.then_inc(made, 1)
        pe.wait_ge(rkr_ready, 1)
        b = fill("bon")
        for t in range(NT):
            for j in range(RT):
                ins = mm(b[:, 8 * t + 2 * j:8 * t + 2 * j + 2], fr[:, j, P * t:P * t + P],
                         const("heads64")[:, 0:P:RD])
        ins.then_inc(made, 1)

        def four_transposes(name, of):
            b_ = fill(name)
            for j in range(4):
                ins_ = nc.tensor.transpose(b_[:, P * j:P * j + P], of(j), ident)
            ins_.then_inc(made, 1)

        for t in range(NT):
            four_transposes(f"vt{t}", lambda j: fv[:, j, P * t:P * t + P])
        pe.wait_ge(ones_set, 1)
        pe.wait_ge(gsq_ready, 1)
        for m in range(4):
            b = fill(f"gss{m}")
            mm(b, ones[:, :], gtmp[:, 512 * m:512 * m + 512]).then_inc(made, 1)
        pe.wait_ge(g_ready, 1)
        b = fill("gc")
        mm(b[:, 0:8], const("incl"), sm["gx"])
        mm(b[:, 8:16], ones[:, :], sm["gx"]).then_inc(made, 1)
        pe.wait_ge(ug_ready, 1)
        for m in range(2):
            b = fill(f"gb{m}")
            mm(b, ones[:, :], UG[:, 4 * m:4 * m + 4, :]).then_inc(made, 1)
        for t in range(NT):
            four_transposes(f"gvt{t}", lambda j: convv[:, j, P * t:P * t + P])
        pe.wait_ge(cols_ready, 1)
        four_transposes("kt0", lambda j: Kt[:, j, 0:P])
        four_transposes("bt0", lambda j: Bt[:, j, 0:P])
        pe.wait_ge(kq_ready, 1)
        four_transposes("gkt", lambda j: KQ[:, j, 0, 0, :])
        for n in range(4):
            b = fill(f"ga{n}")
            for j in range(2):
                q = 2 * n + j
                c, h = q // GH, q % GH
                ins = mm(b[:, 256 * j:256 * j + 256], KQ[:, h, c, 0, :], KQ[:, h, c, :, :])
            ins.then_inc(made, 1)
        for q in range(16):
            c, h = q // RH, q % RH
            j, lo = h // 2, RD * (h % 2)
            b = fill(f"m{q}")
            mm(b[:, 0:256], Bt[lo:lo + RD, j, P * c:P * c + P], AR[lo:lo + RD, j, c, :, :])
            mm(b[:, 256:512], Kt[lo:lo + RD, j, P * c:P * c + P], AR[lo:lo + RD, j, c, :, :]).then_inc(made, 1)

        def lt(q):
            return m4[:, q, 0:P] if q < 16 else GM[:, q - 16, 0, :]

        def inv1(n):
            l, g = INV0[n]
            if l:
                pe.wait_ge(*plan.emptied(f"i3_{l - 1}_{g}"))
            b_ = fill(f"i1_{l}_{g}")
            for j in range(4):
                q = 4 * g + j
                ins_ = mm(b_[:, P * j:P * j + P], lt(q), tinv[:, q, 0, :])
            ins_.then_inc(made, 1)

        pe.wait_ge(tinv_set, 1)
        pe.wait_ge(*plan.emptied("m15"))
        inv1(0)
        for n, (l, g) in enumerate(INV0):
            if n + 1 < len(INV0):
                inv1(n + 1)
            pe.wait_ge(*plan.emptied(f"i1_{l}_{g}"))
            for k, name in enumerate(("i2", "i3")):
                b = fill(f"{name}_{l}_{g}")
                for j in range(2):
                    q = 4 * g + 2 * k + j
                    gm = Gb[:, n % 3, P * (2 * k + j):P * (2 * k + j) + P]
                    mm(b[:, 256 * j:256 * j + P], tinv[:, q, 1, :], gm)
                    ins = mm(b[:, 256 * j + P:256 * j + 256], gm, tinv[:, q, 1, :])
                ins.then_inc(made, 1)

        pe.wait_ge(*plan.emptied(f"i3_{LEVELS - 1}_5"))

        def hcol(h):
            return slice(RD * h, RD * h + RD)

        def rw_w(c):
            b_ = fill(f"w{c}")
            if c:
                pe.wait_ge(*plan.emptied("st"))
            for h in range(RH):
                if c and h % 2 == 0:
                    mm(b_[:, P * (h // 2):P * (h // 2) + P], AR[:, h // 2, 1, 0, :], state_r[:, h // 2, :], True, False,
                       True)
                ins_ = mm(b_[:, hcol(h)], m4[:, 8 * c + h, 256:384], vrow[:, c, hcol(h)], c == 0, True, c == 1)
            ins_.then_inc(made, 1)

        def rw_u(c):
            pe.wait_ge(*plan.emptied(f"w{c}"))
            b_ = fill(f"u{c}")
            for h in range(RH):
                ins_ = mm(b_[:, hcol(h)], tinv[:, 8 * c + h, 1, :], wsb[:, hcol(h)])
            ins_.then_inc(made, 1)

        def rw_y(c):
            b_ = fill(f"y{c}")
            pe.wait_ge(*plan.emptied(f"u{c}"))
            for h in range(RH):
                if c and h % 2 == 0:
                    mm(b_[:, P * (h // 2):P * (h // 2) + P], AR[:, h // 2, 1, 1, :], state_r[:, h // 2, :], True, False,
                       True)
                mm(b_[:, hcol(h)], m4[:, 8 * c + h, 384:512], vrow[:, c, hcol(h)], c == 0, False, c == 1)
                ins_ = mm(b_[:, hcol(h)], m4[:, 8 * c + h, 128:256], un[:, hcol(h)], False, True, c == 1)
            ins_.then_inc(made, 1)

        def gcol(h):
            return slice(GD * h, GD * h + GD)

        def gd(name, lhs, rhs):
            b_ = fill(name)
            for h in range(GH):
                ins_ = mm(b_[:, gcol(h)], lhs(h), rhs(h))
            ins_.then_inc(made, 1)

        rw_w(0)
        gd("gz0", lambda h: tinv[:, 16 + h, 1, :], lambda h: gvrow[:, 0, gcol(h)])
        rw_u(0)
        pe.wait_ge(*plan.emptied("gz0"))
        gd("gs1", lambda h: kdec[:, gcol(h)], lambda h: vnew[:, gcol(h)])
        b = fill("st")
        pe.wait_ge(*plan.emptied("u0"))
        for j in range(RT):
            mm(b[:, P * j:P * j + P], kbT[:, 0, P * j:P * j + P], vrow[:, 0, P * j:P * j + P], True, False)
            ins = mm(b[:, P * j:P * j + P], kbT[:, 1, P * j:P * j + P], un[:, P * j:P * j + P], False, True)
        ins.then_inc(made, 1)
        rw_y(0)
        pe.wait_ge(*plan.emptied("gs1"))
        gd("gp1", lambda h: KQ[:, h, 1, 0, :], lambda h: state_g[:, h, :])
        gd("go0", lambda h: GM[:, h, 1, :], lambda h: vnew[:, gcol(h)])
        rw_w(1)
        pe.wait_ge(r1_ready, 1)
        gd("gz1", lambda h: tinv[:, 20 + h, 1, :], lambda h: r1[:, gcol(h)])
        rw_u(1)
        pe.wait_ge(*plan.emptied("gz1"))
        gd("go1", lambda h: GM[:, 4 + h, 1, :], lambda h: vnew[:, gcol(h)])
        gd("gos", lambda h: KQ[:, h, 1, 1, :], lambda h: state_g[:, h, :])
        rw_y(1)
        pe.wait_ge(sgate_ready, 1)
        for t in range(NT):
            b = fill(f"lg{t}")
            mm(b, sgate[:, P * t:P * t + P], g2sb[:, :]).then_inc(made, 1)
        pe.wait_ge(ycat_ready, 1)
        for n in range(4):
            b = fill(f"yt{n}")
            for j in range(2):
                for t in range(NT):
                    c = 2 * n + j
                    ins = nc.tensor.transpose(b[:, 256 * j + P * t:256 * j + P * t + P],
                                              ycat[:, t, P * c:P * c + P], ident)
            ins.then_inc(made, 1)
        pe.wait_ge(*plan.emptied("yt3"))
        for half in range(2):
            pe.wait_ge(*strip_landed(8 + half))
        for t in range(NT):
            for half in range(2):
                rows_of(f"op{t}{half}", 8 + half, t, yT, KC, lambda c: strips[:, half, c, :])

        def router_logits(tag, layer):
            pe.wait_ge(*plan.emptied(f"{tag}nt3"))
            b_ = fill(f"{tag}rl")
            for t in range(NT):
                for c in range(KC):
                    ins_ = mm(b_[:, 20 * t:20 * t + 20], hT[:, c, P * t:P * t + P], router[:, layer, c, :],
                              c == 0, c == KC - 1)
            ins_.then_inc(made, 1)

        def moe(tag, layer, first):
            router_logits(tag, layer)
            pe.wait_ge(*plan.emptied(f"{tag}rl"))
            for n in range(4):
                t, half = n // 2, n % 2
                ins_ = mm(psum[:, n, :], ident, X[:, t, 512 * half:512 * half + 512], True, True)
                ins_.then_inc(h_made if n < 3 else y_made, 1)
            mm(psum[:, 4, 0:2], ident, ident[:, 0:2]).then_inc(y_made, 1)
            with pe.Fori(0, NE // 2) as i:
                for u in range(2):
                    n = first + u
                    pe.wait_ge(d_strip[n % 2], i * 32 + 32 * (n // 2 + 1))
                    for t in range(NT):
                        pe.wait_ge(g_made, i * 4 + ((2 * NE + 2) * layer + 2 * u + t + 1))
                        for c in range(KC):
                            ins_ = mm(psum[:, 4 + t, :], hT[:, c, P * t:P * t + P], strips[:, n % 2, c, :],
                                      c == 0, c == KC - 1)
                        ins_.then_inc(h_made, 1)
                    for t in range(NT):
                        pe.wait_ge(g_made, i * 4 + ((2 * NE + 2) * layer + 2 * u + t + 3))
                        pe.wait_ge(gT_copied, i * 4 + ((2 * NE + 2) * layer + 2 * u + t + 1))
                        for k in range(2):
                            ins_ = nc.tensor.transpose(psum[:, 6 + t, P * k:P * k + P],
                                                       moeg[:, t, P * k:P * k + P], ident)
                        ins_.then_inc(gT_made, 1)
                        if t == 0:
                            pe.wait_ge(d_down[u], i * 16 + (16 * (NE // 2) * layer + 16))
                        pe.wait_ge(gT_copied, i * 4 + ((2 * NE + 2) * layer + 2 * u + t + 3))
                        for k in range(2):
                            for half in range(2):
                                ins_ = nc.tensor.matmul(psum[:, 2 * t + half, :], moegT[:, t, k, :],
                                                        downs[:, u, k, 512 * half:512 * half + 512],
                                                        start=False, stop=False, skip_group_check=True)
                    ins_.then_inc(y_made, 1)

        norm_columns("b", 1)
        moe("b", 0, MOE0)
        norm_columns("c", 2)
        pe.wait_ge(*plan.emptied("cnt3"))

        def qk_transposes(s, t):
            pe.wait_ge(roped, NT * s + t + 1)
            four_transposes(f"qt{s}{t}", lambda j: qkv[:, t, 512 * s + P * j:512 * s + P * j + P])

        for s in range(9):
            pe.wait_ge(*strip_landed(ODB + s))
            for t in range(NT):
                rows_of(f"s{s}{t}", ODB + s, t, hT, KC, lambda c: strips[:, (ODB + s) % 2, c, :])
                if s < 6 and (s, t) != (0, 0):
                    qk_transposes(*((s, t - 1) if t else (s - 1, 1)))
                if (s, t) == (6, 0):
                    qk_transposes(5, 1)

        def scores(h, t):
            nk = P * (t + 1)
            j, lo = h // 2, AD * (h % 2)
            b_ = fill(f"sc{h}{t}a")
            for g in range(AG):
                if t and g == 2:
                    b_ = fill(f"sc{h}{t}b")
                at_ = nk * g if not (t and g == 2) else 0
                ins_ = mm(b_[:, at_:at_ + nk], qkT[lo:lo + AD, 4 * g + j, P * t:P * t + P],
                          qkT[lo:lo + AD, 12 + 4 * g + j, 0:nk])
                if g == 2 or (t and g == 1):
                    ins_.then_inc(made, 1)

        pe.wait_ge(*plan.emptied("qt51"))
        pe.wait_ge(*plan.emptied("s81"))
        scores(0, 0)
        for n, (h, t) in enumerate(HT_):
            if n + 1 < len(HT_):
                scores(*HT_[n + 1])
            pe.wait_ge(probs_ready, n + 1)
            b = fill(f"pt{h}{t}a")
            for j in range(AG * (t + 1)):
                if j == 4:
                    b = fill(f"pt{h}{t}b")
                ins = nc.tensor.transpose(b[:, P * (j % 4):P * (j % 4) + P], probs[:, n % 2, P * j:P * j + P], ident)
                if j in ((2,) if t == 0 else (3, 5)):
                    ins.then_inc(made, 1)
            pe.wait_ge(*plan.emptied(f"pt{h}{t}{'b' if t else 'a'}"))
            b = fill(f"pv{h}{t}")
            for j in range(AG * (t + 1)):
                g, kt = j // (t + 1), j % (t + 1)
                c0 = 3072 + 512 * g + AD * h
                ins = mm(b[:, 0:AD], pT[:, n % 2, P * j:P * j + P], qkv[:, kt, c0:c0 + AD], j == 0,
                         j == AG * (t + 1) - 1)
            ins.then_inc(made, 1)
        pe.wait_ge(*plan.emptied("pv71"))
        for n in range(2):
            b = fill(f"at{n}")
            for j in range(2):
                for t in range(NT):
                    c = 2 * n + j
                    ins = nc.tensor.transpose(b[:, 256 * j + P * t:256 * j + P * t + P],
                                              arow[:, t, P * c:P * c + P], ident)
            ins.then_inc(made, 1)
        pe.wait_ge(*plan.emptied("at1"))
        pe.wait_ge(*strip_landed(ODB + 9))
        odo = strips[:, (ODB + 9) % 2].rearrange("p (c a) n -> p c (a n)", a=2)
        for t in range(NT):
            for half in range(2):
                rows_of(f"ao{t}{half}", ODB + 9, t, aT, 4, lambda c: odo[:, c, 512 * half:512 * half + 512])
        norm_columns("d", 3)
        moe("d", 1, MOE1)

    @block.vector
    def _(dve):
        counts = {}

        def then(ins, s_=None):
            s_ = s_ or s_dve
            counts[id(s_)] = counts.get(id(s_), 0) + 1
            ins.then_inc(s_, 1)
            dve.wait_ge(s_, counts[id(s_)])

        V = nc.vector

        def take(name):
            dve.wait_ge(made, plan.made(name))
            return psum[:, plan.bank(name), :]

        def tt(o, a, b_, op, s_=None):
            then(V.tensor_tensor(o, a, b_, op), s_)

        def ts(o, a, s1, s2, op0, op1=None, s_=None):
            if op1 is None:
                then(V.tensor_scalar(o, a, s1, None, op0), s_)
            else:
                then(V.tensor_scalar(o, a, s1, s2, op0, op1), s_)

        def stt(o, a, s1, b_, op0, op1, s_=None):
            then(V.scalar_tensor_tensor(out=o, in0=a, scalar=s1, in1=b_, op0=op0, op1=op1), s_)

        def reduce(o, a, op, s_=None):
            then(V.tensor_reduce(o, a, AX.X, op), s_)

        roots = [0]

        def root(m):
            then(V.reciprocal(m, m), root_in)
            roots[0] += 1
            dve.wait_ge(root_out, roots[0])

        def rstd_of(k):
            dve.wait_ge(sq_done, NT * (k + 1))
            ts(sm["rstd"], sm["ssq"], 1.0 / D, RMS_EPS, MUL, ADD)
            root(sm["rstd"])

        def rms_rows(tag, k):
            rstd_of(k)
            for t in range(NT):
                ts(hn[:, t, :].rearrange("q (c p) -> q p c", c=KC), X[:, t, :].rearrange("q (p c) -> q p c", c=KC),
                   sm["rstd"][:, t:t + 1], None, MUL, s_=hn_ready if t == NT - 1 else None)
            dve.wait_ge(d_small, 16 * SMALL_DMAS)
            for n in range(4):
                b = take(f"{tag}nt{n}").rearrange("p (c n) -> p c n", c=2)
                tt(hT[:, 2 * n:2 * n + 2, :], b, gains[:, k, 2 * n:2 * n + 2].unsqueeze(2).broadcast_to([P, 2, S]), MUL,
                   s_=dve_read)

        b = take("params")
        then(V.tensor_copy(par[:, :], b[:, 0:P_ROWS]), dve_read)
        ts(npar[:, 0:8], par[:, P_W0:P_W0 + 8], -1.0, None, MUL, s_=npar_ready)
        ts(omka[:, :], par[:, P_KA:P_KA + RT], -1.0, 1.0, MUL, ADD)
        rms_rows("a", 0)

        dve.wait_ge(*plan.emptied("lora"))
        for j, w in ((0, 64), (1, 96)):
            tt(ft[0:w, j, :], rawL[0:w, j, 0:256], rawL[0:w, j, 1:257], SUB)
            stt(fe2[0:w, j, :], ft[0:w, j, :], par[0:w, P_MUL + j:P_MUL + j + 1], rawL[0:w, j, 1:257], MUL, ADD,
                s_=mixl_ready)
        for n, (name, dst, mu) in enumerate((("k1", fk, 4), ("r1", fr, 0), ("v1", fv, 8))):
            dve.wait_ge(*plan.emptied(name))
            raw = rawB[:, 4 * n:4 * n + 4, :]
            tt(ft, raw[:, :, 0:256], raw[:, :, 1:257], SUB)
            for j in range(4):
                stt(dst[:, j, :], ft[:, j, :], par[:, P_MU + mu + j:P_MU + mu + j + 1], raw[:, j, 1:257], MUL, ADD,
                    s_=fv_ready if name == "v1" else None)
        for j in range(RT):
            ts(fkk[:, j, :], fk[:, j, :], par[:, P_KK + j:P_KK + j + 1], None, MUL)
        tt(ft, fkk, fkk, MUL, s_=kksq_ready)
        dve.wait_ge(lorain_ready, 2)
        ts(sgate[:, :], sgate[:, :], 1.0, None, ADD)
        then(V.reciprocal(sgate[:, :], sgate[:, :]), sgate_ready)
        dve.wait_ge(*plan.emptied("wz1"))
        ts(fsg, fsg, 1.0, None, ADD)
        then(V.reciprocal(fsg, fsg))
        dve.wait_ge(*plan.emptied("az1"))
        ts(fal, fal, 1.0, None, ADD)
        then(V.reciprocal(fal, fal))
        for j in range(RT):
            for c in range(2):
                v = slice(CH * c, CH * c + CH)
                then(V.tensor_tensor_scan(fdx[:, j, v], ones[:, :], fsg[:, j, v], 0.0, MUL, ADD))
        mid = fdx.rearrange("p t (c n) -> p t c n", c=2)
        fsv = sm["fs"].rearrange("p (t o) -> p t o", o=1)
        tt(fsv, mid[:, :, 0, CH - 1:CH], mid[:, :, 0, CH // 2:CH // 2 + 1], SUB)
        tt(fsv, fsv, mid[:, :, 1, CH // 2:CH // 2 + 1], ADD)
        tt(fd.rearrange("p t (c n) -> p t c n", c=2), mid,
           mid[:, :, :, CH // 2:CH // 2 + 1].broadcast_to([P, RT, 2, CH]), SUB)
        tt(fdx, fd, fsg, SUB, s_=decay_in)
        then(V.memset(sm["mark"], 0.0), decay_in)
        for k in range(2):
            b = take(f"ss{k}")
            ts(ft[:, 2 * k:2 * k + 2, :], b.rearrange("p (t n) -> p t n", t=2), 1e-6, None, ADD, s_=dve_read)
        root(ft)
        tt(fkk, fkk, ft, MUL)
        tt(ft, fkk, fal, MUL)
        for j in range(RT):
            ts(fal[:, j, :], fal[:, j, :], par[:, P_KA + j:P_KA + j + 1], omka[:, j:j + 1], MUL, ADD)
        tt(fk, fk, fal, MUL)
        dve.wait_ge(decay_out, 3)
        tt(Bt, ft, fd, MUL)
        tt(Kt, fk, fd, MUL)

        def chunks(m):
            return m.rearrange("p t (c n) -> p t c n", c=2)

        tt(AR[:, :, :, 0, :], chunks(fkk), chunks(fdx), MUL)
        tt(AR[:, :, :, 1, :], chunks(fr), chunks(fe2), MUL, s_=cols_ready)
        tt(fr, fr, fk, MUL)
        for j in range(RT):
            ts(fr[:, j, :], fr[:, j, :], par[:, P_RK + j:P_RK + j + 1], None, MUL,
               s_=rkr_ready if j == RT - 1 else None)
        b = take("bon")
        then(V.tensor_copy(sm["bonus"], b[:, 0:16]), dve_read)

        def convolve(n, name, tile0):
            dve.wait_ge(*plan.emptied(name))
            for j in range(4):
                o = conv_out[n][:, j]
                for i in range(CONV):
                    tap = rawA[:, 4 * n + j, i:i + 256].rearrange("p (c n) -> p c n", c=2)
                    wt = par[:, P_CONV + 12 * i + tile0 + j:P_CONV + 12 * i + tile0 + j + 1]
                    last = i == CONV - 1 and j == 3
                    if i == 0:
                        ts(o, tap, wt, None, MUL)
                    else:
                        stt(o, tap, wt, o, MUL, ADD, s_=silu_in if last else None)

        def silu(n):
            dve.wait_ge(silu_exp, n + 1)
            ts(gtmp_h(n), gtmp_h(n), 1.0, None, ADD)
            then(V.reciprocal(gtmp_h(n), gtmp_h(n)))
            tt(conv_out[n], conv_out[n], gtmp_h(n), MUL, s_=silu_out)

        convolve(0, "gk1", 4)
        convolve(1, "gq1", 0)
        silu(0)
        convolve(2, "gv1", 8)
        silu(1)
        silu(2)
        kqf = w_(18432, 2048)
        tt(gtmp, kqf, kqf, MUL, s_=gsq_ready)
        abv = sm["ab"].rearrange("p (c s h) -> p c s h", c=2, s=2)

        def ch(m):
            return m.rearrange("p (c h) -> p c h", c=2)

        tt(ch(sm["gx"]), abv[:, :, 0, :], gab[:, 1, :].unsqueeze(1).broadcast_to([P, 2, GH]), ADD)
        stt(sm["gg"], sm["gx"], -1.0, sm["gx"], MUL, MAX, s_=gate_in)
        ts(sm["gx"], sm["gx"], 0.0, None, MAX)
        dve.wait_ge(gate_exp, 4)
        ts(sm["beta"], sm["beta"], 1.0, None, ADD)
        then(V.reciprocal(sm["beta"], sm["beta"]))
        tt(sm["gx"], sm["gx"], sm["ga"], ADD)
        stt(ch(sm["gx"]), ch(sm["gx"]), -1.0, sm["eal"].unsqueeze(1).broadcast_to([P, 2, GH]), MUL, MUL, s_=g_ready)
        for m in range(4):
            b = take(f"gss{m}")
            ts(gtmp[:, 512 * m:512 * m + 512], b, 1e-6, None, ADD, s_=dve_read)
        root(gtmp)
        inv = gtmp.rearrange("p (h c s n) -> p h c s n", h=GH, c=2, s=2)
        tt(KQ[:, :, :, 0, :], KQ[:, :, :, 0, :], inv[:, :, :, 0, :], MUL)
        stt(KQ[:, :, :, 1, :], KQ[:, :, :, 1, :], float(GD) ** -0.5, inv[:, :, :, 1, :], MUL, MUL, s_=kq_ready)
        then(V.memset(sm["mark"], 0.0), early_done)
        tt(UG, const("incl").unsqueeze(1).broadcast_to([P, 8, P]), sm["gx"].unsqueeze(2).broadcast_to([P, 8, P]), MUL,
           s_=ug_ready)
        b = take("gc")
        then(V.tensor_copy(sm["gc2"], b[:, 0:16]), dve_read)
        tt(sm["kd"], sm["glast"], sm["gc"], SUB)
        for m in range(2):
            b = take(f"gb{m}").rearrange("p (q n) -> p q n", q=4)
            o = GM[:, 4 * m:4 * m + 4, 1, :]
            tt(o, b, sm["gc"][:, 4 * m:4 * m + 4].unsqueeze(2).broadcast_to([P, 4, P]), SUB, s_=dve_read)
            tt(o, o, const("far").unsqueeze(1).broadcast_to([P, 4, P]), ADD, s_=dt_in if m else None)
        dve.wait_ge(dt_exp, 1)
        for q in range(8):
            stt(GM[:, q, 0, :], GM[:, q, 1, :], sm["beta"][:, q:q + 1], const("strict"), MUL, MUL)
        dve.wait_ge(gc_exp, 2)
        b = take("gkt")
        tt(kdec.rearrange("p (h n) -> p h n", h=GH), b.rearrange("p (h n) -> p h n", h=GH),
           sm["kd"][:, 0:4].unsqueeze(2).broadcast_to([P, GH, GD]), MUL, s_=dve_read)
        for n in range(4):
            b = take(f"ga{n}")
            gmv = GM[:, 2 * n:2 * n + 2, :, :].rearrange("p q s n -> p (q s n)")
            tt(gmv, gmv, b, MUL, s_=dve_read)
        dve.wait_ge(m4_zero, 1)
        for q in range(16):
            b = take(f"m{q}")
            then(V.copy_predicated(m4[:, q, :], const("causal4").bitcast(U32), b), dve_read)
        dve.wait_ge(tinv_set, 1)

        def masked_product(n):
            l, g = INV0[n]
            b_ = take(f"i1_{l}_{g}").rearrange("p (q n) -> p q n", q=4)
            tt(Gb[:, n % 3, :].rearrange("p (q n) -> p q n", q=4), b_,
               const(f"level{l}").unsqueeze(1).broadcast_to([P, 4, P]), MUL, s_=dve_read)

        masked_product(0)
        for n, (l, g) in enumerate(INV0):
            if n + 1 < len(INV0):
                masked_product(n + 1)
            for k, name in enumerate(("i2", "i3")):
                b = take(f"{name}_{l}_{g}")
                q = 4 * g + 2 * k
                o = tinv[:, q:q + 2, :, :].rearrange("p q s n -> p (q s n)")
                tt(o, o, b, SUB, s_=dve_read)

        def h4(m):
            return m.rearrange("p (h n) -> p h n", h=GH)

        def per_head(m, c):
            return m[:, 4 * c:4 * c + 4].unsqueeze(2).broadcast_to([P, GH, GD])

        b = take("gz0")
        tt(h4(vnew), h4(b), per_head(sm["beta"], 0), MUL, s_=dve_read)
        b = take("st")
        dve.wait_ge(decay_out, 4)
        for j in range(RT):
            stt(state_r[:, j, :], b[:, P * j:P * j + P], sm["fs"][:, j:j + 1], const("heads64"), MUL, MUL,
                s_=dve_read if j == RT - 1 else None)
        b = take("gp1")
        tt(h4(tmpd), h4(b), per_head(sm["egc"], 1), MUL, s_=dve_read)
        tt(r1, gvrow[:, 1, :], tmpd, SUB, s_=r1_ready)
        dve.wait_ge(z_exp, 1)
        zs = UG.rearrange("p (t q) n -> p t (q n)", t=NT)
        ts(zs, zs, 1.0, None, ADD)
        then(V.reciprocal(zs, zs))
        tt(zr, zr, zs, MUL)
        b = take("gz1")
        dve.wait_ge(made, plan.made("go0"))
        tt(h4(vnew), h4(b), per_head(sm["beta"], 1), MUL, s_=dve_read)
        b = take("gos")
        tt(h4(tmpd), h4(b), per_head(sm["egc"], 1), MUL, s_=dve_read)
        dve.wait_ge(*plan.emptied("go1"))
        tt(ycat[:, 1, 0:512], ycat[:, 1, 0:512], tmpd, ADD)
        for t in range(NT):
            o = ycat[:, t, 0:512]
            tt(tmpd, o, o, MUL)
            reduce(sm["stat"][:, GH * t:GH * t + GH], h4(tmpd), ADD)
        ts(sm["stat"][:, 0:8], sm["stat"][:, 0:8], 1.0 / GD, RMS_EPS, MUL, ADD)
        root(sm["stat"][:, 0:8])
        for t in range(NT):
            o = ycat[:, t, 0:512]
            st = sm["stat"][:, GH * t:GH * t + GH]
            tt(h4(o), h4(o), st.unsqueeze(2).broadcast_to([P, GH, GD]), MUL)
            tt(h4(o), h4(o), gnw[:, :].unsqueeze(1).broadcast_to([P, GH, GD]), MUL)
            tt(o, o, zr[:, t, :], MUL)
        dve.wait_ge(*plan.emptied("y1"))

        def h8(m):
            return m.rearrange("p (h n) -> p h n", h=RH)

        def b8(m):
            return m.unsqueeze(2).broadcast_to([P, RH, RD])

        for t in range(NT):
            o = ycat[:, t, 512:1024]
            st, st2 = sm["stat"][:, 0:RH], sm["stat2"][:, RH * t:RH * t + RH]
            reduce(st, h8(o), ADD)
            ts(st, st, 1.0 / RD, None, MUL)
            tt(h8(o), h8(o), b8(st), SUB)
            tt(tmpd, o, o, MUL)
            reduce(st2, h8(tmpd), ADD)
            ts(st2, st2, 1.0 / RD, LN_EPS, MUL, ADD)
        root(sm["stat2"])
        for t in range(NT):
            o = ycat[:, t, 512:1024]
            st2 = sm["stat2"][:, RH * t:RH * t + RH]
            tt(h8(o), h8(o), b8(st2), MUL)
            tt(o, o, lnw[:, :], MUL)
            tt(o, o, lnb[:, :], ADD)
            tt(h8(tmpd), h8(vrow[:, t, :]), b8(sm["bonus"][:, 8 * t:8 * t + 8]), MUL)
            tt(o, o, tmpd, ADD)
            b = take(f"lg{t}")
            tt(o, o, b, MUL, s_=dve_read)
        then(V.memset(sm["mark"], 0.0), ycat_ready)

        def add_residual(prefix):
            for t in range(NT):
                for half in range(2):
                    b_ = take(f"{prefix}{t}{half}")
                    o = X[:, t, 512 * half:512 * half + 512]
                    tt(o, o, b_, ADD, s_=dve_read)
                then(V.memset(sm["mark"], 0.0), x_ready)

        add_residual("op")

        def pairs(m, n=4):
            return m.rearrange("p (t n) -> p t n", t=NT)

        def top(dst, src, best):
            tt(pairs(dst), pairs(src), best.unsqueeze(2).broadcast_to([P, NT, 4]), EQ)
            tt(pairs(dst), pairs(dst), const("rank4").unsqueeze(1).broadcast_to([P, NT, 4]), MUL)
            reduce(sm["gt2"], pairs(dst), MAX)
            tt(pairs(dst), pairs(dst), sm["gt2"].unsqueeze(2).broadcast_to([P, NT, 4]), EQ)

        def route(tag, layer):
            b_ = take(f"{tag}rl")
            then(V.tensor_copy(sm["logits"], b_[:, 0:40]), dve_read)
            lg = sm["logits"].rearrange("p (t n) -> p t n", t=NT)
            reduce(sm["gm"], lg[:, :, 0:NG], MAX)
            tt(pairs(sm["ge"]), lg[:, :, 0:NG], sm["gm"].unsqueeze(2).broadcast_to([P, NT, NG]), SUB, s_=route_in)
            then(V.tensor_copy(pairs(sm["gt"]), lg[:, :, 0:NG]))
            top(sm["goh"], sm["gt"], sm["gm"])
            el = lg[:, :, NG:NG + NE].rearrange("p t (g e) -> p t e g", g=NG)
            prod = gates.rearrange("p t (e g) -> p t e g", g=NG)
            tt(prod, el, pairs(sm["goh"]).unsqueeze(2).broadcast_to([P, NT, 4, NG]), MUL)
            reduce(pairs(sm["sel"]), prod, ADD)
            reduce(sm["v1"], pairs(sm["sel"]), MAX)
            top(sm["oh1"], sm["sel"], sm["v1"])
            stt(sm["s2"], sm["oh1"], -3.0e38, sm["sel"], MUL, ADD)
            reduce(sm["v2"], pairs(sm["s2"]), MAX)
            tt(sm["dv"], sm["v2"], sm["v1"], SUB, s_=route_in)
            top(sm["oh2"], sm["s2"], sm["v2"])
            dve.wait_ge(route_exp, 2 * layer + 2)
            reduce(sm["pg"], pairs(sm["ge"]), ADD)
            then(V.reciprocal(sm["pg"], sm["pg"]))
            ts(sm["i1"], sm["dv"], 1.0, None, ADD)
            then(V.reciprocal(sm["i1"], sm["i1"]))
            tt(sm["i1"], sm["i1"], sm["pg"], MUL)
            tt(sm["i2"], sm["i1"], sm["dv"], MUL)
            tt(pairs(sm["oh1"]), pairs(sm["oh1"]), sm["i1"].unsqueeze(2).broadcast_to([P, NT, 4]), MUL)
            tt(pairs(sm["oh2"]), pairs(sm["oh2"]), sm["i2"].unsqueeze(2).broadcast_to([P, NT, 4]), MUL)
            tt(sm["inn"], sm["oh1"], sm["oh2"], ADD)
            for t in range(NT):
                ins = V.tensor_tensor(gates[:, t, :].rearrange("p (g e) -> p g e", g=NG),
                                      pairs(sm["goh"])[:, t, :].unsqueeze(2).broadcast_to([P, NG, 4]),
                                      pairs(sm["inn"])[:, t, :].unsqueeze(1).broadcast_to([P, NG, 4]), MUL)
                ins.then_inc(g_made, 1)
            dve.wait_ge(g_made, (2 * NE + 2) * layer + 2)

        def moe(tag, layer):
            route(tag, layer)
            with dve.Fori(0, NE) as e:
                for t in range(NT):
                    dve.wait_ge(silu_done, e * 2 + (2 * NE * layer + t + 1))
                    V.scalar_tensor_tensor(out=moeg[:, t, :], in0=moes[:, t, :], scalar=gates[:, t, bass.ds(e, 1)],
                                           in1=psum[:, 4 + t, FF:2 * FF], op0=MUL, op1=MUL).then_inc(g_made, 1)
            dve.wait_ge(y_made, (NE + 2) * (layer + 1))
            for t in range(NT):
                for half in range(2):
                    then(V.tensor_copy(X[:, t, 512 * half:512 * half + 512], psum[:, 2 * t + half, :]),
                         x_ready if half else None)

        rms_rows("b", 1)
        moe("b", 0)
        rms_rows("c", 2)
        half_d = AD // 2
        ang, turns, sin_, cos_ = (trig[:, 64 * n:64 * n + 64] for n in range(4))
        posf = sm["mx"]
        then(V.tensor_copy(posf, possb[:, :]))
        tt(pairs(ang), posf.unsqueeze(2).broadcast_to([P, NT, half_d]),
           const("invf").unsqueeze(1).broadcast_to([P, NT, half_d]), MUL)
        ROUND = 12582912.0
        ts(turns, ang, float(1.0 / (2.0 * np.pi)), None, MUL)
        ts(turns, turns, ROUND, None, ADD)
        ts(turns, turns, ROUND, None, SUB)
        two_pi = 2.0 * np.pi
        p1 = 6.28125
        p2 = float(np.float32(np.round((two_pi - p1) * 2 ** 21) / 2 ** 21))
        p3 = two_pi - p1 - p2
        for part in (p1, p2, p3):
            stt(ang, turns, -part, ang, MUL, ADD)
        ts(sin_, ang, -3.14159, 3.14159, MAX, ALU.min)
        stt(cos_, sin_, -1.0, sin_, MUL, MAX)
        ts(cos_, cos_, -1.0, float(np.pi / 2), MUL, ADD, s_=trig_in)
        dve.wait_ge(trig_done, 1)
        ccos = w_(24704, 128).rearrange("p (t n) -> p t n", t=NT)
        csin = w_(24832, 128).rearrange("p (t n) -> p t n", t=NT)
        for a in range(2):
            then(V.tensor_copy(ccos[:, :, 32 * a:32 * a + 32], pairs(cos_)))
            ts(csin[:, :, 32 * a:32 * a + 32], pairs(sin_), 1.0 if a else -1.0, None, MUL)
        for s in range(6):
            for t in range(NT):
                n = NT * s + t
                b = take(f"s{s}{t}").rearrange("p (h a n) -> p h a n", h=8, a=2)
                if n >= 2:
                    dve.wait_ge(roped, n - 1)
                o = rtmp[:, n % 2, :, 0:512].rearrange("p s (h a n) -> p s h a n", h=8, a=2)
                for a in range(2):
                    cb = ccos[:, t, 32 * a:32 * a + 32].unsqueeze(1).broadcast_to([P, 8, 32])
                    sb_ = csin[:, t, 32 * a:32 * a + 32].unsqueeze(1).broadcast_to([P, 8, 32])
                    then(V.tensor_tensor(o[:, 0, :, a, :], b[:, :, a, :], cb, MUL))
                    ins = V.tensor_tensor(o[:, 1, :, a, :], b[:, :, 1 - a, :], sb_, MUL)
                    if a == 0:
                        then(ins)
                then(ins, dve_read)
                then(V.memset(sm["mark"], 0.0), rope_ready)
        dve.wait_ge(d_mask, 16)

        def masked_scores(n):
            h, t = HT_[n]
            nk = P * (t + 1)
            m0 = 384 * t
            b_ = take(f"sc{h}{t}a")
            w = 384 if t == 0 else 512
            o = scs[:, n % 2, :]
            stt(o[:, 0:w], b_[:, 0:w], float(AD) ** -0.5, masks[:, m0:m0 + w], MUL, ADD, s_=dve_read)
            if t:
                b_ = take(f"sc{h}{t}b")
                stt(o[:, 512:768], b_[:, 0:256], float(AD) ** -0.5, masks[:, m0 + 512:m0 + 768], MUL, ADD, s_=dve_read)
            reduce(sm["mx"][:, n % 2:n % 2 + 1], o[:, 0:AG * nk], MAX)
            ts(sm["nmx"][:, n % 2:n % 2 + 1], sm["mx"][:, n % 2:n % 2 + 1], -1.0, None, MUL, s_=scores_ready)

        masked_scores(0)
        for n in range(len(HT_)):
            if n + 1 < len(HT_):
                masked_scores(n + 1)
            dve.wait_ge(probs_ready, n + 1)
            then(V.reciprocal(sm["rden"][:, n % 2:n % 2 + 1], sm["den"][:, n % 2:n % 2 + 1]), rden_ready)
        add_residual("ao")
        rms_rows("d", 3)
        moe("d", 1)
        rstd_of(4)
        dve.wait_ge(d_fin, 16)
        for t in range(NT):
            stt(hn[:, t, :], X[:, t, :], sm["rstd"][:, t:t + 1], w_(0, D), MUL, MUL, s_=out_ready)


_INS = ['x', 'positions', 'ev_norm', 'ev_w_in', 'ev_w_out', 'gdn_conv_w', 'gdn_A_log', 'gdn_dt_bias', 'gdn_norm',
        'rwkv_mu', 'rwkv_w0', 'rwkv_w2', 'rwkv_a0', 'rwkv_a2', 'rwkv_g2', 'rwkv_k_k', 'rwkv_k_a', 'rwkv_r_k',
        'rwkv_ln_w', 'rwkv_ln_b', 'od_norm', 'od_w_in', 'od_w_out', 'ffn_norm', 'moe_w_group', 'moe_w_expert',
        'moe_w1', 'moe_w3', 'moe_w2', 'final_norm']


def kernel(**inputs):
    import numpy as _np
    import concourse.bacc as _bacc
    from concourse import mybir as _mybir
    from concourse.bass_utils import run_bass_kernel_spmd as _run

    nc = _bacc.Bacc("TRN2", target_bir_lowering=False, num_devices=1)
    arrays, args = {}, []
    given = {name: _np.ascontiguousarray(inputs[name]) for name in _INS}
    given["const_mats"], _, given["attn_masks"] = constants()
    for name, a in given.items():
        arrays[f"in_{name}_dram"] = a
        args.append(nc.dram_tensor(f"in_{name}_dram", a.shape, _mybir.dt.from_np(a.dtype), kind="ExternalInput").ap())
    args.append(nc.dram_tensor("out_0_dram", (1, S, D), _mybir.dt.float32, kind="ExternalOutput").ap())
    trunk(nc, *args)
    r = _run(nc, [arrays], core_ids=[0])
    return r.results[0]["out_0_dram"]
```

```python
from contextlib import ExitStack

import numpy as np

import concourse.bass as bass
from concourse import mybir

P = 128
F32 = mybir.dt.float32
F32R = mybir.dt.float32r
I32 = mybir.dt.int32
U32 = mybir.dt.uint32
ALU = mybir.AluOpType
ACT = mybir.ActivationFunctionType
AX = mybir.AxisListType
ADD, SUB, MUL, MAX, EQ = ALU.add, ALU.subtract, ALU.mult, ALU.max, ALU.is_equal

SMALL_DMAS = 20
D = 1024
S = 256
NT = S // P
KC = D // P
RMS_EPS = 1e-6
GH, GD = 4, 128
CONV = 4
RH, RD = 8, 64
RT = RH * RD // P
LORA_W, LORA_A, LORA_G = 32, 32, 96
LN_EPS = 64e-5
NG, NEG_ = 4, 4
NE = NG * NEG_
FF = 256
AH, AD, AG = 8, 64, 3
DILATIONS = (1, 4, 16)
SPAN = 128
ROPE_THETA = 10000.0
CH = 128
LEVELS = 7
DECAY = float(np.exp(-0.5))
FAR = -1.0e30
BANKS = 8

C_Q, C_K, C_V, C_Z, C_AB, C_R, C_RK, C_RV, C_LORA = 0, 512, 1024, 1536, 2048, 2056, 2568, 3080, 3592


def constants():
    i = np.arange(P)[:, None]
    j = np.arange(P)[None, :]
    incl = (i <= j).astype(np.float32)
    strict = (i < j).astype(np.float32)
    parts = {"ident": np.eye(P, dtype=np.float32), "strict": strict, "incl": incl,
             "far": np.where(i <= j, 0.0, FAR).astype(np.float32),
             "heads64": (i // RD == j // RD).astype(np.float32)}
    for l in range(LEVELS):
        b = 1 << l
        parts[f"level{l}"] = ((i // (2 * b) == j // (2 * b)) & (i // b % 2 == 1) & (j // b % 2 == 0)).astype(np.float32)
    parts["invf"] = np.tile((ROPE_THETA ** (-np.arange(AD // 2, dtype=np.float32) * 2.0 / AD)).astype(np.float32), (P, 1))
    parts["rank4"] = np.tile(np.array([4, 3, 2, 1], np.float32), (P, 1))
    place, at = {}, 0
    for name, m in parts.items():
        place[name] = (at, m.shape[1])
        at += m.shape[1]
    masks = []
    for t in range(NT):
        keys = np.arange((t + 1) * P)[None, :]
        rel = (t * P + i) - keys
        masks.append(np.concatenate([np.where((rel >= 0) & (rel % d == 0) & (rel <= SPAN * d), 0.0, FAR)
                                     for d in DILATIONS], 1).astype(np.float32))
    return np.concatenate(list(parts.values()), 1), place, np.concatenate(masks, 1)


P_CONV, P_MU, P_MUL, P_W0, P_A0, P_KK, P_KA, P_RK = 0, 48, 60, 62, 66, 70, 74, 78
P_ROWS = 82


class PsumPlan:

    def __init__(self, sems):
        self.sems = sems
        self.jobs = []
        self.index = {}
        self.first = 0

    def segment(self):
        self.first = len(self.jobs)

    def add(self, name, reader):
        assert name not in self.index, name
        self.index[name] = len(self.jobs)
        self.jobs.append((name, reader, self.first))

    def bank(self, name):
        n = self.index[name]
        return (n - self.jobs[n][2]) % BANKS

    def made(self, name):
        return self.index[name] + 1

    def emptied(self, name):
        n = self.index[name]
        reader = self.jobs[n][1]
        return self.sems[reader], sum(1 for job in self.jobs[:n + 1] if job[1] == reader)

    def must_be_empty(self, name):
        n = self.index[name]
        upto = n - BANKS + 1 if n - self.jobs[n][2] >= BANKS else self.jobs[n][2]
        for reader in ("act", "dve"):
            count = sum(1 for job in self.jobs[:upto] if job[1] == reader)
            if count:
                yield self.sems[reader], count


class Stream:
    SLOTS = 3

    def __init__(self, plan):
        self.plan = plan
        self.units = []
        self.low_by = []
        self.sems = {}

    def add(self, loads, release, low_by):
        self.units.append((loads, release))
        self.low_by.append(low_by)

    def slot(self, g):
        return g % self.SLOTS

    def landed(self, g):
        count = sum(16 * len(self.units[k][0]) for k in range(g + 1) if k % self.SLOTS == g % self.SLOTS)
        return self.sems["landed"][g % self.SLOTS], count

    def high(self, g):
        return self.sems["high"], g + 1

    def low(self, g):
        return self.sems["low_" + self.low_by[g]], self.low_by[:g + 1].count(self.low_by[g])

    def released(self, g):
        release = self.units[g][1]
        if release in ("used", "h_made", "y_made"):
            return self.sems[release], sum(1 for u in self.units[:g + 1] if u[1] == release)
        return self.sems["made"], self.plan.made(release)


def trunk(nc, x, positions, ev_norm, ev_w_in, ev_w_out, gdn_conv_w, gdn_A_log, gdn_dt_bias, gdn_norm, rwkv_mu,
          rwkv_w0, rwkv_w2, rwkv_a0, rwkv_a2, rwkv_g2, rwkv_k_k, rwkv_k_a, rwkv_r_k, rwkv_ln_w, rwkv_ln_b,
          od_norm, od_w_in, od_w_out, ffn_norm, moe_w_group, moe_w_expert, moe_w1, moe_w3, moe_w2, final_norm,
          const_mats, attn_masks, out):
    _, CP, _ = constants()
    ctx = ExitStack()

    def sb(name, shape, dt=F32):
        return ctx.enter_context(nc.sbuf_tensor(name, shape, dt))

    def sem(name):
        return ctx.enter_context(nc.semaphore(name))

    consts = sb("consts", [P, const_mats.shape[1]])

    def const(name):
        a, w = CP[name]
        return consts[:, a:a + w]

    ident = const("ident")
    ones = sb("ones", [P, P])
    X = sb("X", [P, NT, D])
    hn = sb("hn", [P, NT, D])
    hTh = sb("hTh", [P, KC, S], F32R)
    hTl = sb("hTl", [P, KC, S], F32R)
    raw = sb("raw", [P, Stream.SLOTS, 1024])
    wh = sb("wh", [P, Stream.SLOTS, 1024], F32R)
    wl = sb("wl", [P, Stream.SLOTS, 1024], F32R)
    moegTh = sb("moegTh", [P, NT, 2, P], F32R)
    moegTl = sb("moegTl", [P, NT, 2, P], F32R)
    work = sb("work", [P, 27648])
    par = sb("par", [P, P_ROWS])
    omka = sb("omka", [P, RT])
    gains = sb("gains", [P, 4, KC])
    loraw = sb("loraw", [LORA_W + LORA_A, 512])
    gnw = sb("gnw", [P, GD])
    gab = sb("gab", [P, 2, GH])
    router = sb("router", [P, 2, KC, NG + NE])
    possb = sb("possb", [P, NT], I32)
    small = sb("small", [P, 512])
    sgate = sb("sgate", [LORA_G, S])
    psum = ctx.enter_context(nc.psum_tensor("psum", [P, BANKS, 512], F32))

    def w_(a, n):
        return work[:, a:a + n]

    m4 = w_(0, 8192).rearrange("p (q n) -> p q n", n=512)
    tinv = w_(8192, 6144).rearrange("p (q s n) -> p q s n", s=2, n=P)
    AR = w_(14336, 2048).rearrange("p (t c s n) -> p t c s n", t=RT, c=2, s=2)
    Bt = w_(16384, 1024).rearrange("p (t n) -> p t n", t=RT)
    Kt = w_(17408, 1024).rearrange("p (t n) -> p t n", t=RT)
    KQ = w_(18432, 2048).rearrange("p (h c s n) -> p h c s n", h=GH, c=2, s=2)
    GM = w_(20480, 2048).rearrange("p (q s n) -> p q s n", s=2, n=P)
    zr = w_(22528, 1024).rearrange("p (t n) -> p t n", t=NT)
    UG = w_(23552, 1024).rearrange("p (q n) -> p q n", n=P)
    kbT = w_(24576, 1024).rearrange("p (s n) -> p s n", s=2)
    kdec = w_(25600, 512)
    Gb = w_(26112, 1536).rearrange("p (b n) -> p b n", b=3)
    vrow = hn[:, 0, :].rearrange("p (t n) -> p t n", t=NT)
    gvrow = hn[:, 1, :].rearrange("p (t n) -> p t n", t=NT)
    rawB = w_(0, 12 * 257).rearrange("p (t n) -> p t n", n=257)
    rawA = w_(3084, 12 * 259).rearrange("p (t n) -> p t n", n=259)
    rawL = w_(6192, 514).rearrange("p (t n) -> p t n", n=257)
    prow = w_(7730, P)
    convv = w_(6706, 1024).rearrange("p (t n) -> p t n", t=4)
    fk, fr, fsg, fal, fd, fdx = [w_(8192 + 1024 * n, 1024).rearrange("p (t n) -> p t n", t=RT) for n in range(6)]
    fv, fe2, fkk, ft = [w_(23552 + 1024 * n, 1024).rearrange("p (t n) -> p t n", t=RT) for n in range(4)]
    gtmp = w_(20480, 2048)
    conv_out = [KQ[:, :, :, 0, :], KQ[:, :, :, 1, :], convv.rearrange("p h (c n) -> p h c n", c=2)]
    fshift = w_(16384, 1024).rearrange("p (t n) -> p t n", t=RT)
    wsb = w_(16384, 512)
    un = w_(16896, 512)
    state_r = w_(17408, 512).rearrange("p (t n) -> p t n", t=RT)
    vnew = w_(17920, 512)
    r1 = w_(26112, 512)
    state_g = w_(26624, 512).rearrange("p (h n) -> p h n", h=GH)
    tmpd = w_(27136, 512)
    ycat = w_(8192, 2048).rearrange("p (t n) -> p t n", t=NT)
    lnw, lnb = w_(18432, 512), w_(18944, 512)
    g2sb = w_(19456, 512)[0:LORA_G]
    qkv = w_(0, 2 * 4608).rearrange("p (t n) -> p t n", t=NT)
    qkT = w_(9216, 6144).rearrange("p (i n) -> p i n", n=S)
    masks = w_(15360, 1152)
    probs = w_(16512, 1536).rearrange("p (b n) -> p b n", b=2)
    pT = w_(18048, 1536).rearrange("p (b n) -> p b n", b=2)
    scs = w_(19584, 1536).rearrange("p (b n) -> p b n", b=2)
    rtmp = w_(21120, 2048).rearrange("p (b s n) -> p b s n", b=2, s=2)
    trig = w_(23168, 512)
    arow = w_(23680, 1024).rearrange("p (t n) -> p t n", t=NT)
    moes = w_(26112, 512).rearrange("p (t n) -> p t n", t=NT)
    moeg = w_(26624, 512).rearrange("p (t n) -> p t n", t=NT)
    sm = {}
    at = GC0 = 0
    for name, n in (("ssq", 2), ("rstd", 2), ("ab", 16), ("beta", 8), ("gx", 8), ("ga", 8), ("gg", 8), ("gc", 8),
                    ("glast", 8), ("egc", 8), ("kd", 8), ("fs", 4), ("bonus", 16), ("stat", 16), ("stat2", 16),
                    ("logits", 40), ("gm", 2), ("gt", 8), ("gt2", 2), ("goh", 8), ("ge", 8), ("gs", 2), ("pg", 2),
                    ("sel", 8), ("v1", 2), ("v2", 2), ("oh1", 8), ("oh2", 8), ("s2", 8), ("dv", 2), ("i1", 2),
                    ("i2", 2), ("inn", 8), ("gates", 32), ("mx", 2), ("nmx", 2), ("den", 2), ("rden", 2), ("eal", 4), ("mark", 2)):
        sm[name] = small[:, at:at + n]
        GC0 = at if name == "gc" else GC0
        at += n
    assert at <= 512
    sm["gc2"] = small[:, GC0:GC0 + 16]
    gates = sm["gates"].rearrange("p (t e) -> p t e", t=NT)

    eps6 = sb("eps6", [P, 1])

    made, act_read, dve_read = sem("made"), sem("act_read"), sem("dve_read")
    s_act, s_dve, s_pool = sem("act_steps"), sem("dve_steps"), sem("pool_steps")
    d_const, d_x, d_par, d_small, d_mask = sem("d_const"), sem("d_x"), sem("d_par"), sem("d_small"), sem("d_mask")
    d_fin, d_out = sem("d_fin"), sem("d_out")
    landed = [sem(f"landed{b}") for b in range(Stream.SLOTS)]
    high, low_pool, low_dve, used = sem("high"), sem("low_pool"), sem("low_dve"), sem("used")
    d_late, half_done = sem("d_late"), sem("half_done")
    ones_set, pads_set, m4_zero = sem("ones_set"), sem("pads_set"), sem("m4_zero")
    sq_done, hn_ready = sem("sq_done"), sem("hn_ready")
    mixl_ready, lorain_ready, sgate_ready = sem("mixl_ready"), sem("lorain_ready"), sem("sgate_ready")
    kksq_ready, rkr_ready, cols_ready, decay_in, decay_out = (sem("kksq_ready"), sem("rkr_ready"), sem("cols_ready"),
                                                               sem("decay_in"), sem("decay_out"))
    fv_ready, convv_ready, conv_done, silu_in, silu_exp = (sem("fv_ready"), sem("convv_ready"), sem("conv_done"),
                                                           sem("silu_in"), sem("silu_exp"))
    conv_silu, rden_ready, beta_done = sem("conv_silu"), sem("rden_ready"), sem("beta_done")
    gsq_ready, kq_ready = sem("gsq_ready"), sem("kq_ready")
    gate_in, gate_exp, g_ready, ug_ready, dt_in, dt_exp, gc_exp = (sem("gate_in"), sem("gate_exp"), sem("g_ready"),
                                                                   sem("ug_ready"), sem("dt_in"), sem("dt_exp"),
                                                                   sem("gc_exp"))
    early_done, tinv_set = sem("early_done"), sem("tinv_set")
    r1_ready, z_exp, ycat_ready = sem("r1_ready"), sem("z_exp"), sem("ycat_ready")
    x_ready = sem("x_ready")
    route_in, route_exp, gates_ready = sem("route_in"), sem("route_exp"), sem("gates_ready")
    root_in, root_out = sem("root_in"), sem("root_out")
    kknorm_done, kqnorm_done, gT_high, gT_low = sem("kknorm_done"), sem("kqnorm_done"), sem("gT_high"), sem("gT_low")
    columns_low = sem("columns_low")
    h_made, silu_done, g_made, gT_made, gT_copied, y_made = (sem("h_made"), sem("silu_done"), sem("g_made"),
                                                             sem("gT_made"), sem("gT_copied"), sem("y_made"))
    trig_in, trig_done, rope_ready, roped = sem("trig_in"), sem("trig_done"), sem("rope_ready"), sem("roped")
    scores_ready, probs_ready, out_ready = sem("scores_ready"), sem("probs_ready"), sem("out_ready")

    plan = PsumPlan({"act": act_read, "dve": dve_read})

    def plan_norm(tag):
        for n in range(4):
            plan.add(f"{tag}nt{n}", "dve")

    INV0 = [(l, g) for l in range(LEVELS) for g in range(6)]
    plan.add("params", "dve")
    plan_norm("a")
    for n, e in (("loraA", "act"), ("ab", "act"), ("loraB", "act"), ("k0", "act"), ("k1", "act"),
                 ("wz0", "act"), ("wz1", "act"), ("az0", "act"), ("az1", "act"),
                 ("r0", "act"), ("r1", "act"), ("ss0", "act"), ("ss1", "act"), ("v0", "act"), ("v1", "act"),
                 ("gk0", "act"), ("gk1", "act"), ("gq0", "act"), ("gq1", "act"), ("vt0", "act"), ("vt1", "act"),
                 ("gv0", "act"), ("gv1", "act"), ("bon", "dve"), ("z0", "act"), ("z1", "act"),
                 ("kt0", "act"), ("bt0", "act"),
                 ("gss0", "act"), ("gss1", "act"), ("gss2", "act"), ("gss3", "act"), ("gc", "dve"),
                 ("gb0", "dve"), ("gb1", "dve"), ("gvt0", "act"), ("gvt1", "act"), ("gkt", "dve")):
        plan.add(n, e)
    for n in range(4):
        plan.add(f"ga{n}", "dve")
    for q in range(16):
        plan.add(f"m{q}", "dve")
    for n, (l, g) in enumerate(INV0):
        if n == 0:
            plan.add(f"i1_{l}_{g}", "dve")
        if n + 1 < len(INV0):
            l1, g1 = INV0[n + 1]
            plan.add(f"i1_{l1}_{g1}", "dve")
        plan.add(f"i2_{l}_{g}", "dve")
        plan.add(f"i3_{l}_{g}", "dve")
    for n, e in (("w0", "act"), ("gz0", "dve"), ("u0", "act"), ("gs1", "act"), ("st", "dve"), ("y0", "act"),
                 ("gp1", "dve"), ("go0", "act"), ("w1", "act"), ("gz1", "dve"), ("u1", "act"), ("go1", "act"),
                 ("gos", "dve"), ("y1", "act"), ("lg0", "dve"), ("lg1", "dve")):
        plan.add(n, e)
    for n in range(4):
        plan.add(f"yt{n}", "dve")
    for t in range(NT):
        for half in range(2):
            plan.add(f"op{t}{half}", "dve")
    plan_norm("b")
    plan.add("brl", "dve")
    plan.segment()
    plan_norm("c")
    for s in range(9):
        for t in range(NT):
            plan.add(f"s{s}{t}", "dve" if s < 6 else "act")
        if 1 <= s <= 6:
            for t in range(NT):
                plan.add(f"qt{s - 1}{t}", "act")
    HT_ = [(h, t) for h in range(AH) for t in range(NT)]

    def plan_scores(h, t):
        plan.add(f"sc{h}{t}a", "dve")
        if t:
            plan.add(f"sc{h}{t}b", "dve")

    plan_scores(0, 0)
    for n, (h, t) in enumerate(HT_):
        if n + 1 < len(HT_):
            plan_scores(*HT_[n + 1])
        plan.add(f"pt{h}{t}a", "act")
        if t:
            plan.add(f"pt{h}{t}b", "act")
        plan.add(f"pv{h}{t}", "act")
    for n in range(2):
        plan.add(f"at{n}", "dve")
    for t in range(NT):
        for half in range(2):
            plan.add(f"ao{t}{half}", "dve")
    plan_norm("d")
    plan.add("drl", "dve")

    stream = Stream(plan)
    stream.sems = {"landed": landed, "high": high, "low_pool": low_pool, "low_dve": low_dve, "used": used,
                   "made": made, "h_made": h_made, "y_made": y_made}
    ev_k = ev_w_in[0].rearrange("(p c) n -> p c n", c=KC)
    od_k = od_w_in[0].rearrange("(p c) n -> p c n", c=KC)
    evo_k = ev_w_out[0].rearrange("(c p) n -> p c n", p=P)
    odo_k = od_w_out[0].rearrange("(c p) n -> p c n", p=P)

    def unit_cols(loads, release, low_by):
        stream.add([(("cols", a, n), src) for a, n, src in loads], release, low_by)

    def add_tiles(c0, names):
        for j in range(4):
            unit_cols([(0, P, ev_k[:, :, c0 + P * j:c0 + P * j + P])], names[j // 2] if j % 2 else "used", "pool")

    def add_strip(src, c0, last, low_by):
        for j in range(4):
            stream.add([(("chunks", 0, 512), src[:, 2 * j:2 * j + 2, c0:c0 + 512])], last if j == 3 else "used", low_by)

    def add_rows(src, n, last, low_by):
        for c in range(n):
            stream.add([(("row", 0, D), src[:, c, :])], last if c == n - 1 else "used", low_by)

    def hidden_loads(layer, e, u):
        return [(("chunks", FF * k, FF), expert(w, layer, e).rearrange("(p c) f -> p c f", c=KC)[:, 2 * u:2 * u + 2, :])
                for k, w in enumerate((moe_w1, moe_w3))]

    def down_load(layer, e, k):
        return [(("row", 0, D), expert(moe_w2, layer, e).rearrange("(k p) n -> p k n", p=P)[:, k, :])]

    def expert(w, layer, e):
        return w[layer, e] if isinstance(e, int) else w[layer, bass.ds(e, 1)].rearrange("o a b -> (o a) b")

    def add_moe(layer):
        first = len(stream.units)
        for e in range(NE + 1):
            if e < NE:
                for u in range(4):
                    stream.add(hidden_loads(layer, e, u), "h_made" if u == 3 else "used", "dve")
            if e:
                for k in range(2):
                    stream.add(down_load(layer, e - 1, k), "y_made" if k else "used", "dve")
        return first

    unit_cols([(0, 64, ev_k[:, :, C_LORA:C_LORA + 64]), (64, 8, ev_k[:, :, C_AB:C_AB + 8]), (72, 56, ev_k[:, :, 0:56])],
              "ab", "pool")
    unit_cols([(0, 96, ev_k[:, :, C_LORA + 64:C_LORA + 160]), (96, 32, ev_k[:, :, 0:32])], "loraB", "pool")
    U_K = len(stream.units)
    for c0, names in ((C_RK, "k"), (C_R, "r"), (C_RV, "v"), (C_K, "gk"), (C_Q, "gq"), (C_V, "gv")):
        add_tiles(c0, (f"{names}0", f"{names}1"))
    U_Z = len(stream.units)
    add_strip(ev_k, C_Z, "z1", "pool")
    U_EVO = len(stream.units)
    add_rows(evo_k, KC, "op11", "pool")
    MOE = [add_moe(0)]
    U_OD = len(stream.units)
    for n in range(9):
        add_strip(od_k, 512 * n, f"s{n}1", "dve")
    U_ODO = len(stream.units)
    add_rows(odo_k, 4, "ao11", "dve")
    MOE.append(add_moe(1))

    def view(buf, g, kind):
        flat = buf[:, stream.slot(g), :]
        if kind == "cols":
            return flat.rearrange("p (c n) -> p c n", c=KC)
        return flat.rearrange("p (c n) -> p c n", c=2) if kind == "chunks" else flat

    LANDED_PER_STEP = [16 * (len(stream.units[MOE[0] + 4 + u][0]) + len(stream.units[MOE[0] + 7 + u][0]))
                       for u in range(3)]
    RELEASED_PER_STEP = {"used": 4, "h_made": 1, "y_made": 1}

    def step_unit(layer, e, u):
        return MOE[layer] + 4 + 6 * (e - 1) + u

    block = ctx.enter_context(nc.Block())

    @block.sync
    def _(sp):
        xr = x[0].rearrange("(t p) n -> p t n", p=P)
        for t in range(NT):
            sp.dma_start(X[:, t, :], xr[:, t, :]).then_inc(d_x, 16)
        sp.dma_start(consts[:, :], const_mats).then_inc(d_const, 16)
        rows = [(P_CONV, gdn_conv_w[0].rearrange("k (t p) -> (k t) p", p=P), 48),
                (P_MU, rwkv_mu[:, 0:1536].rearrange("o (t p) -> (o t) p", p=P), 12),
                (P_W0, rwkv_w0.rearrange("o (t p) -> (o t) p", p=P), 4),
                (P_A0, rwkv_a0.rearrange("o (t p) -> (o t) p", p=P), 4),
                (P_KK, rwkv_k_k.rearrange("o (t p) -> (o t) p", p=P), 4),
                (P_KA, rwkv_k_a.rearrange("o (t p) -> (o t) p", p=P), 4),
                (P_RK, rwkv_r_k[0].rearrange("(t h) d -> t (h d)", h=2), 4)]
        sp.wait_ge(pads_set, 1)
        for r, src, n in rows:
            sp.dma_start(prow[r:r + n, :], src).then_inc(d_par, 16)
        sp.dma_start(prow[P_MUL:P_MUL + 1, 0:64], rwkv_mu[:, 1536:1600]).then_inc(d_par, 16)
        sp.dma_start(prow[P_MUL + 1:P_MUL + 2, 0:96], rwkv_mu[:, 1600:1696]).then_inc(d_par, 16)
        for n, src in enumerate((ev_norm[0], ffn_norm[0], od_norm[0], ffn_norm[1])):
            sp.dma_start(gains[:, n, :], src.rearrange("(p c) -> p c", c=KC)).then_inc(d_small, 16)

        def load(g, loads=None, i=None, per_round=None):
            loads = loads or stream.units[g][0]
            if g >= Stream.SLOTS:
                s_, v = stream.low(g - Stream.SLOTS)
                sp.wait_ge(s_, v if i is None else i * 6 + v)
            for (kind, a, n), src in loads:
                dst = view(raw, g, kind)
                dst = dst[:, a:a + n] if kind == "row" else dst[:, :, a:a + n]
                sp.dma_start(dst, src).then_inc(landed[stream.slot(g)], 16)

        for g in range(Stream.SLOTS):
            load(g)
        small_dmas = [(loraw[0:32, :], rwkv_w2[0]), (loraw[32:64, :], rwkv_a2[0]),
                      (gnw[:, :], gdn_norm[0].partition_broadcast(P)),
                      (gab[:, 0, :], gdn_A_log[0].partition_broadcast(P)),
                      (gab[:, 1, :], gdn_dt_bias[0].partition_broadcast(P)),
                      (possb[:, :], positions[0].rearrange("(t p) -> p t", p=P))]
        for l in range(2):
            small_dmas.append((router[:, l, :, 0:NG], moe_w_group[l].rearrange("(p c) g -> p c g", c=KC)))
            for g in range(NG):
                small_dmas.append((router[:, l, :, NG + 4 * g:NG + 4 * g + 4],
                                   moe_w_expert[l, g].rearrange("(p c) e -> p c e", c=KC)))
        assert 4 + len(small_dmas) == SMALL_DMAS
        for dst, src in small_dmas:
            sp.dma_start(dst, src, allow_slow_non_contiguous=True).then_inc(d_small, 16)
        for g in range(Stream.SLOTS, U_EVO + Stream.SLOTS):
            load(g)
        sp.wait_ge(made, plan.made("gos"))
        for dst, src in ((lnw, rwkv_ln_w[0].partition_broadcast(P)), (lnb, rwkv_ln_b[0].partition_broadcast(P)),
                         (g2sb, rwkv_g2[0])):
            sp.dma_start(dst, src).then_inc(d_late, 16)
        for g in range(U_EVO + Stream.SLOTS, MOE[0]):
            load(g)

        def experts(layer):
            for g in range(MOE[layer], step_unit(layer, 2, 0)):
                load(g)
            with sp.Fori(0, NE - 2) as i:
                for u in range(6):
                    loads = hidden_loads(layer, i + 2, u) if u < 4 else down_load(layer, i + 1, u - 4)
                    load(step_unit(layer, 2, u), loads, i)
            for g in range(step_unit(layer, NE, 0), step_unit(layer, NE, 2)):
                load(g)

        experts(0)
        sp.dma_start(masks, attn_masks).then_inc(d_mask, 16)
        for g in range(U_OD, MOE[1]):
            load(g)
        experts(1)
        sp.dma_start(w_(0, D), final_norm.partition_broadcast(P)).then_inc(d_fin, 16)
        outr = out[0].rearrange("(t p) n -> p t n", p=P)
        for t in range(NT):
            sp.wait_ge(out_ready, t + 1)
            sp.dma_start(outr[:, t, :], hn[:, t, :]).then_inc(d_out, 16)
        sp.wait_ge(d_out, 16 * NT)

    @block.gpsimd
    def _(pool):
        nc.gpsimd.memset(eps6[:, :], 1e-6)
        nc.gpsimd.memset(prow, 0.0).then_inc(pads_set, 1)
        nc.gpsimd.memset(ones[:, :], 1.0).then_inc(ones_set, 1)
        nc.gpsimd.memset(rawB[:, :, 0:1], 0.0)
        nc.gpsimd.memset(rawL[:, :, 0:1], 0.0)
        nc.gpsimd.memset(rawA[:, :, 0:3], 0.0).then_inc(pads_set, 1)

        def low_part(g):
            pool.wait_ge(*stream.high(g))
            if g >= Stream.SLOTS:
                pool.wait_ge(*stream.released(g - Stream.SLOTS))
            nc.gpsimd.tensor_tensor(wl[:, stream.slot(g), :], raw[:, stream.slot(g), :],
                                    wh[:, stream.slot(g), :].bitcast(F32), SUB).then_inc(low_pool, 1)

        for g in range(U_EVO + Stream.SLOTS):
            low_part(g)
        pool.wait_ge(early_done, 1)
        pool.wait_ge(*plan.emptied("gvt1"))
        nc.gpsimd.memset(w_(0, 8192), 0.0).then_inc(m4_zero, 1)
        pool.wait_ge(d_const, 16)
        nc.gpsimd.tensor_copy(w_(8192, 6144).rearrange("p (q n) -> p q n", n=P),
                              ident.unsqueeze(1).broadcast_to([P, 48, P])).then_inc(tinv_set, 1)
        for g in range(U_EVO + Stream.SLOTS, MOE[0]):
            low_part(g)
        for s in range(6):
            for t in range(NT):
                n = NT * s + t
                pool.wait_ge(rope_ready, n + 1)
                nc.gpsimd.tensor_tensor(qkv[:, t, 512 * s:512 * s + 512], rtmp[:, n % 2, 0, 0:512],
                                        rtmp[:, n % 2, 1, 0:512], ADD).then_inc(roped, 1)

    @block.scalar
    def _(act):
        steps = [0]

        def step(ins):
            steps[0] += 1
            ins.then_inc(s_act, 1)
            act.wait_ge(s_act, steps[0])

        def take(name):
            act.wait_ge(made, plan.made(name))
            return psum[:, plan.bank(name), :]

        roots = [0]

        def root(m):
            roots[0] += 1
            act.wait_ge(root_in, roots[0])
            nc.scalar.activation(m, m, ACT.Sqrt).then_inc(root_out, 1)

        def norm_squares(k):
            for t in range(NT):
                act.wait_ge(*((d_x, 16 * NT) if k == 0 else (x_ready, NT * (k - 1) + t + 1)))
                nc.scalar.activation(hn[:, t, :], X[:, t, :], ACT.Square,
                                     accum_out=sm["ssq"][:, t:t + 1]).then_inc(sq_done, 1)
            root(sm["rstd"])

        split = [0]

        def highs(upto):
            for g in range(split[0], upto):
                high_part(g)
            split[0] = max(split[0], upto)

        def high_part(g, i=None, rounds=(6, 6)):
            s_, v = stream.landed(g)
            act.wait_ge(s_, v if i is None else i * rounds[0] + v)
            if g >= Stream.SLOTS:
                s_, v = stream.released(g - Stream.SLOTS)
                act.wait_ge(s_, v if i is None else i * rounds[1] + v)
            nc.scalar.copy(wh[:, stream.slot(g), :], raw[:, stream.slot(g), :]).then_inc(high, 1)

        def columns_high(tag, k):
            if k == 0:
                act.wait_ge(d_small, 16 * SMALL_DMAS)
            for n in range(4):
                b_ = take(f"{tag}nt{n}")
                for j in range(2):
                    c = 2 * n + j
                    ins = nc.scalar.activation(hTh[:, c, :], b_[:, 256 * j:256 * j + 256], ACT.Copy,
                                               scale=gains[:, k, c:c + 1])
                ins.then_inc(half_done, 1)

        norm_squares(0)
        highs(Stream.SLOTS)
        columns_high("a", 0)
        act.wait_ge(pads_set, 2)
        b = take("loraA")
        nc.scalar.copy(rawL[0:64, 0, 1:257], b[0:64, 0:256]).then_inc(act_read, 1)
        highs(4)
        b = take("ab")
        nc.scalar.copy(sm["ab"], b[:, 0:16]).then_inc(act_read, 1)
        highs(5)
        b = take("loraB")
        nc.scalar.copy(rawL[0:96, 1, 1:257], b[0:96, 0:256]).then_inc(act_read, 1)

        def raw_tiles(buf, pad, tile, name, last):
            highs(last + 1 + Stream.SLOTS)
            b_ = take(name)
            nc.scalar.copy(buf[:, tile:tile + 2, pad:pad + 256], b_.rearrange("p (t n) -> p t n", t=2)
                           ).then_inc(act_read, 1)

        raw_tiles(rawB, 1, 0, "k0", U_K + 1)
        raw_tiles(rawB, 1, 2, "k1", U_K + 3)
        act.wait_ge(mixl_ready, 2)
        nc.scalar.activation(fe2[0:32, 0, :], fe2[0:32, 0, :], ACT.Tanh).then_inc(lorain_ready, 1)
        nc.scalar.activation(sgate[:, :], fe2[0:96, 1, :], ACT.Sigmoid).then_inc(sgate_ready, 1)
        for k, (name, dst) in enumerate((("wz0", fsg), ("wz1", fsg), ("az0", fal), ("az1", fal))):
            b = take(name)
            for j in range(2):
                t = 2 * (k % 2) + j
                ins = nc.scalar.activation(dst[:, t, :], b[:, 256 * j:256 * j + 256], ACT.Sigmoid,
                                           bias=par[:, P_W0 + 4 * (k // 2) + t:P_W0 + 4 * (k // 2) + t + 1])
            ins.then_inc(act_read, 1)
        act.wait_ge(*plan.emptied("ab"))
        abv = sm["ab"].rearrange("p (c s h) -> p c s h", c=2, s=2)
        nc.scalar.activation(sm["beta"].rearrange("p (c h) -> p c h", c=2), abv[:, :, 1, :],
                             ACT.Sigmoid).then_inc(beta_done, 1)
        raw_tiles(rawB, 1, 4, "r0", U_K + 5)
        raw_tiles(rawB, 1, 6, "r1", U_K + 7)
        highs(U_K + 12)
        for k in range(2):
            b = take(f"ss{k}")
            nc.scalar.activation(ft[:, 2 * k:2 * k + 2, :], b.rearrange("p (t n) -> p t n", t=2), ACT.Ln,
                                 bias=eps6[:, 0:1]).then_inc(act_read, 1)
        raw_tiles(rawB, 1, 8, "v0", U_K + 9)
        raw_tiles(rawB, 1, 10, "v1", U_K + 11)
        act.wait_ge(*plan.emptied("ss1"))
        nc.scalar.activation(ft, ft, ACT.Exp, scale=-0.5).then_inc(kknorm_done, 1)
        act.wait_ge(decay_in, 1)
        nc.scalar.activation(fe2, fd, ACT.Exp, scale=-DECAY).then_inc(decay_out, 1)
        act.wait_ge(decay_out, 1)
        nc.scalar.activation(fd, fd, ACT.Exp, scale=DECAY).then_inc(decay_out, 1)
        nc.scalar.activation(fdx, fdx, ACT.Exp, scale=-DECAY).then_inc(decay_out, 1)
        act.wait_ge(decay_in, 2)
        nc.scalar.activation(sm["fs"], sm["fs"], ACT.Exp, scale=-DECAY).then_inc(decay_out, 1)
        raw_tiles(rawA, 3, 0, "gk0", U_K + 13)
        raw_tiles(rawA, 3, 2, "gk1", U_K + 15)
        raw_tiles(rawA, 3, 4, "gq0", U_K + 17)
        raw_tiles(rawA, 3, 6, "gq1", U_K + 19)
        highs(U_K + 21)
        for t in range(NT):
            b = take(f"vt{t}")
            nc.scalar.copy(vrow[:, t, :], b).then_inc(act_read, 1)
        raw_tiles(rawA, 3, 8, "gv0", U_K + 21)
        raw_tiles(rawA, 3, 10, "gv1", U_K + 23)
        highs(U_EVO + Stream.SLOTS)
        for t in range(NT):
            b = take(f"z{t}")
            nc.scalar.activation(zr[:, t, :], b, ACT.Silu).then_inc(act_read, 1)
        for n in range(3):
            act.wait_ge(silu_in, n + 1)
            nc.scalar.activation(conv_out[n], conv_out[n], ACT.Silu).then_inc(conv_silu, 1)
        for s, name in enumerate(("kt0", "bt0")):
            b = take(name)
            nc.scalar.copy(kbT[:, s, :], b).then_inc(act_read, 1)
        nc.scalar.activation(sm["eal"], gab[:, 0, :], ACT.Exp).then_inc(gate_exp, 1)
        act.wait_ge(gate_in, 1)
        nc.scalar.activation(sm["ga"], sm["gg"], ACT.Exp, scale=-1.0).then_inc(gate_exp, 1)
        act.wait_ge(gate_exp, 2)
        nc.scalar.activation(sm["ga"], sm["ga"], ACT.Ln, bias=1.0).then_inc(gate_exp, 1)
        for m in range(4):
            b = take(f"gss{m}")
            nc.scalar.activation(gtmp[:, 512 * m:512 * m + 512], b, ACT.Ln, bias=eps6[:, 0:1]).then_inc(act_read, 1)
        act.wait_ge(*plan.emptied("gss3"))
        nc.scalar.activation(gtmp, gtmp, ACT.Exp, scale=-0.5).then_inc(kqnorm_done, 1)
        act.wait_ge(dt_in, 1)
        nc.scalar.activation(GM[:, :, 1, :], GM[:, :, 1, :], ACT.Exp).then_inc(dt_exp, 1)
        nc.scalar.activation(sm["egc"], sm["gc"], ACT.Exp).then_inc(gc_exp, 1)
        nc.scalar.activation(sm["kd"], sm["kd"], ACT.Exp).then_inc(gc_exp, 1)
        for t in range(NT):
            b = take(f"gvt{t}")
            nc.scalar.copy(gvrow[:, t, :], b).then_inc(act_read, 1)
        b = take("w0")
        nc.scalar.copy(wsb, b).then_inc(act_read, 1)
        b = take("u0")
        nc.scalar.mul(un, b, -1.0).then_inc(act_read, 1)
        b = take("gs1")
        nc.scalar.copy(state_g.rearrange("p h n -> p (h n)"), b).then_inc(act_read, 1)
        b = take("y0")
        nc.scalar.copy(ycat[:, 0, 512:1024], b).then_inc(act_read, 1)
        b = take("go0")
        nc.scalar.copy(ycat[:, 0, 0:512], b).then_inc(act_read, 1)
        b = take("w1")
        nc.scalar.copy(wsb, b).then_inc(act_read, 1)
        b = take("u1")
        nc.scalar.mul(un, b, -1.0).then_inc(act_read, 1)
        b = take("go1")
        nc.scalar.copy(ycat[:, 1, 0:512], b).then_inc(act_read, 1)
        b = take("y1")
        nc.scalar.copy(ycat[:, 1, 512:1024], b).then_inc(act_read, 1)
        root(sm["stat"][:, 0:8])
        root(sm["stat2"])
        for n in range(4):
            b = take(f"yt{n}")
            nc.scalar.copy(hTh[:, 2 * n:2 * n + 2, :], b.rearrange("p (c n) -> p c n", c=2)).then_inc(half_done, 1)
        highs(MOE[0] + Stream.SLOTS)

        def moe(layer):
            act.wait_ge(route_in, 2 * layer + 1)
            nc.scalar.activation(sm["ge"], sm["ge"], ACT.Exp).then_inc(route_exp, 1)
            act.wait_ge(route_in, 2 * layer + 2)
            nc.scalar.activation(sm["dv"], sm["dv"], ACT.Exp).then_inc(route_exp, 1)
            def hidden_highs(e, us, i=None):
                for u in us:
                    g = step_unit(layer, e, u)
                    high_part(g, i, (2 * LANDED_PER_STEP[u % 3], 2 * RELEASED_PER_STEP[stream.units[g - 3][1]]))

            def silu(e, i=None):
                v = NE * layer + e + 1
                act.wait_ge(h_made, v if i is None else i * 2 + v)
                nc.scalar.activation(moes, psum[:, 4 + 2 * (e % 2):6 + 2 * (e % 2), 0:FF],
                                     ACT.Silu).then_inc(silu_done, 1)

            def transposed_high(e, i=None):
                v = NE * layer + e + 1
                act.wait_ge(gT_made, v if i is None else i * 2 + v)
                if e or layer:
                    act.wait_ge(y_made, v - 1 if i is None else i * 2 + v - 1)
                nc.scalar.copy(moegTh[:, :, :, :].rearrange("p t k n -> p t (k n)"),
                               psum[:, 4 + 2 * (e % 2):6 + 2 * (e % 2), 0:FF]).then_inc(gT_high, 1)

            def act_step(e, i=None):
                hidden_highs(e, range(3), i)
                transposed_high(e - 1, i)
                hidden_highs(e, range(3, 6), i)
                silu(e, i)

            highs(MOE[layer] + 4)
            silu(0)
            act_step(1)
            with act.Fori(0, NE // 2 - 1) as i:
                act_step(2, i)
                act_step(3, i)
            split[0] = step_unit(layer, NE, 0)
            transposed_high(NE - 1)
            highs(step_unit(layer, NE, 0) + 2 + Stream.SLOTS if layer == 0 else step_unit(layer, NE, 0) + 2)

        norm_squares(1)
        columns_high("b", 1)
        moe(0)
        norm_squares(2)
        columns_high("c", 2)
        act.wait_ge(trig_in, 1)
        nc.scalar.activation(trig[:, 128:256], trig[:, 128:256], ACT.Sin).then_inc(trig_done, 1)

        def copy_qkT(s, t):
            b = take(f"qt{s}{t}")
            nc.scalar.copy(qkT[:, 4 * s:4 * s + 4, P * t:P * t + P],
                           b.rearrange("p (j n) -> p j n", j=4)).then_inc(act_read, 1)

        for s in range(9):
            for t in range(NT):
                if t == 0:
                    highs(min(U_OD + 4 * s + 4 + Stream.SLOTS, MOE[1]))
                if s >= 6:
                    b = take(f"s{s}{t}")
                    nc.scalar.copy(qkv[:, t, 512 * s:512 * s + 512], b).then_inc(act_read, 1)
            if 1 <= s <= 6:
                for t in range(NT):
                    copy_qkT(s - 1, t)
        for n, (h, t) in enumerate(HT_):
            keys = AG * P * (t + 1)
            act.wait_ge(scores_ready, n + 1)
            nc.scalar.activation(probs[:, n % 2, 0:keys], scs[:, n % 2, 0:keys], ACT.Exp,
                                 bias=sm["nmx"][:, n % 2:n % 2 + 1],
                                 accum_out=sm["den"][:, n % 2:n % 2 + 1]).then_inc(probs_ready, 1)
            b = take(f"pt{h}{t}a")
            w = 384 if t == 0 else 512
            nc.scalar.copy(pT[:, n % 2, 0:w], b[:, 0:w]).then_inc(act_read, 1)
            if t:
                b = take(f"pt{h}{t}b")
                nc.scalar.copy(pT[:, n % 2, 512:768], b[:, 0:256]).then_inc(act_read, 1)
            b = take(f"pv{h}{t}")
            act.wait_ge(rden_ready, n + 1)
            nc.scalar.activation(arow[:, t, AD * h:AD * h + AD], b[:, 0:AD], ACT.Copy,
                                 scale=sm["rden"][:, n % 2:n % 2 + 1]).then_inc(act_read, 1)
        for n in range(2):
            b = take(f"at{n}")
            nc.scalar.copy(hTh[:, 2 * n:2 * n + 2, :], b.rearrange("p (c n) -> p c n", c=2)).then_inc(half_done, 1)
        highs(MOE[1] + Stream.SLOTS)
        norm_squares(3)
        columns_high("d", 3)
        moe(1)
        norm_squares(4)

    @block.tensor
    def _(pe):
        seen = {}

        def fill(name):
            for s_, v in plan.must_be_empty(name):
                if v > seen.get(id(s_), 0):
                    seen[id(s_)] = v
                    pe.wait_ge(s_, v)
            return psum[:, plan.bank(name), :]

        def mm(out_, lhsT, rhs, start=True, stop=True, shared=False):
            return nc.tensor.matmul(out_, lhsT, rhs, start=start, stop=stop, skip_group_check=shared)

        def norm_columns(tag, k):
            pe.wait_ge(hn_ready, k + 1)
            for n in range(4):
                b = fill(f"{tag}nt{n}")
                for j in range(2):
                    for t in range(NT):
                        c = 2 * n + j
                        ins = nc.tensor.transpose(b[:, 256 * j + P * t:256 * j + P * t + P],
                                                  hn[:, t, P * c:P * c + P], ident)
                ins.then_inc(made, 1)

        def unit(g, i=None):
            s_, v = stream.low(g)
            pe.wait_ge(s_, v if i is None else i * 12 + v)

        def mm3(out_, lh, ll, rh, rl, start, stop, shared=False):
            mm(out_, lh, rh, start, False, shared)
            mm(out_, lh, rl, False, False, shared)
            return mm(out_, ll, rh, False, stop, shared)

        def column_tile(out_, g):
            unit(g)
            h_, l_ = view(wh, g, "cols"), view(wl, g, "cols")
            for c in range(KC):
                ins_ = mm3(out_, h_[:, c, :], l_[:, c, :], hTh[:, c, :], hTl[:, c, :], c == 0, c == KC - 1)
            return ins_

        def col_pair(name, g):
            b_ = fill(name)
            column_tile(b_[:, 0:256], g).then_inc(used, 1)
            column_tile(b_[:, 256:512], g + 1).then_inc(made, 1)

        def row_strip(names, g):
            banks = [fill(name) for name in names]
            for j in range(4):
                unit(g + j)
                h_, l_ = view(wh, g + j, "chunks"), view(wl, g + j, "chunks")
                for t in range(NT):
                    v_ = slice(P * t, P * t + P)
                    for c in range(2):
                        k = 2 * j + c
                        ins_ = mm3(banks[t], hTh[:, k, v_], hTl[:, k, v_], h_[:, c, :], l_[:, c, :], k == 0,
                                   k == KC - 1)
                    if j == 3:
                        ins_.then_inc(made, 1)
                if j < 3:
                    ins_.then_inc(used, 1)

        def row_block(names, g, n):
            banks = [fill(name) for name in names]
            for c in range(n):
                unit(g + c)
                h_, l_ = view(wh, g + c, "row"), view(wl, g + c, "row")
                for t in range(NT):
                    v_ = slice(P * t, P * t + P)
                    for half in range(2):
                        w = slice(512 * half, 512 * half + 512)
                        ins_ = mm3(banks[2 * t + half], hTh[:, c, v_], hTl[:, c, v_], h_[:, w], l_[:, w], c == 0,
                                   c == n - 1)
                        if c == n - 1:
                            ins_.then_inc(made, 1)
                if c < n - 1:
                    ins_.then_inc(used, 1)

        pe.wait_ge(d_const, 16)
        pe.wait_ge(d_par, 16 * 9)
        b = fill("params")
        nc.tensor.transpose(b[:, 0:P], prow[:, :], ident).then_inc(made, 1)
        norm_columns("a", 0)
        pe.wait_ge(*plan.emptied("ant3"))
        b = fill("loraA")
        column_tile(b[:, 0:256], 0).then_inc(made, 1)
        b = fill("ab")
        h_, l_ = view(wh, 0, "cols"), view(wl, 0, "cols")
        for t in range(NT):
            for c in range(KC):
                v_ = slice(P * t, P * t + P)
                ins = mm3(b[:, 8 * t:8 * t + 8], hTh[:, c, v_], hTl[:, c, v_], h_[:, c, 64:72], l_[:, c, 64:72],
                          c == 0, c == KC - 1)
        ins.then_inc(made, 1)
        b = fill("loraB")
        column_tile(b[:, 0:256], 1).then_inc(made, 1)
        col_pair("k0", U_K)
        col_pair("k1", U_K + 2)
        pe.wait_ge(lorain_ready, 1)
        for name, lo, hi in (("wz", 0, 32), ("az", 32, 64)):
            for k in range(2):
                b = fill(f"{name}{k}")
                for j in range(2):
                    c0 = P * (2 * k + j)
                    ins = mm(b[:, 256 * j:256 * j + 256], loraw[lo:hi, c0:c0 + P], fe2[lo:hi, 0, :])
                ins.then_inc(made, 1)
        col_pair("r0", U_K + 4)
        col_pair("r1", U_K + 6)
        pe.wait_ge(kksq_ready, 1)
        for k in range(2):
            b = fill(f"ss{k}")
            for j in range(2):
                ins = mm(b[:, 256 * j:256 * j + 256], const("heads64"), ft[:, 2 * k + j, :])
            ins.then_inc(made, 1)
        col_pair("v0", U_K + 8)
        col_pair("v1", U_K + 10)
        col_pair("gk0", U_K + 12)
        col_pair("gk1", U_K + 14)
        col_pair("gq0", U_K + 16)
        col_pair("gq1", U_K + 18)

        def four_transposes(name, of):
            b_ = fill(name)
            for j in range(4):
                ins_ = nc.tensor.transpose(b_[:, P * j:P * j + P], of(j), ident)
            ins_.then_inc(made, 1)

        pe.wait_ge(fv_ready, 1)
        for t in range(NT):
            four_transposes(f"vt{t}", lambda j: fv[:, j, P * t:P * t + P])
        col_pair("gv0", U_K + 20)
        col_pair("gv1", U_K + 22)
        pe.wait_ge(rkr_ready, 1)
        b = fill("bon")
        for t in range(NT):
            for j in range(RT):
                ins = mm(b[:, 8 * t + 2 * j:8 * t + 2 * j + 2], fr[:, j, P * t:P * t + P],
                         const("heads64")[:, 0:P:RD])
        ins.then_inc(made, 1)

        row_strip(("z0", "z1"), U_Z)
        pe.wait_ge(cols_ready, 1)
        four_transposes("kt0", lambda j: Kt[:, j, 0:P])
        four_transposes("bt0", lambda j: Bt[:, j, 0:P])
        pe.wait_ge(ones_set, 1)
        pe.wait_ge(gsq_ready, 1)
        for m in range(4):
            b = fill(f"gss{m}")
            mm(b, ones[:, :], gtmp[:, 512 * m:512 * m + 512]).then_inc(made, 1)
        pe.wait_ge(g_ready, 1)
        b = fill("gc")
        mm(b[:, 0:8], const("incl"), sm["gx"])
        mm(b[:, 8:16], ones[:, :], sm["gx"]).then_inc(made, 1)
        pe.wait_ge(ug_ready, 1)
        for m in range(2):
            b = fill(f"gb{m}")
            mm(b, ones[:, :], UG[:, 4 * m:4 * m + 4, :]).then_inc(made, 1)
        pe.wait_ge(conv_silu, 3)
        for t in range(NT):
            four_transposes(f"gvt{t}", lambda j: convv[:, j, P * t:P * t + P])
        pe.wait_ge(kq_ready, 1)
        four_transposes("gkt", lambda j: KQ[:, j, 0, 0, :])
        for n in range(4):
            b = fill(f"ga{n}")
            for j in range(2):
                q = 2 * n + j
                c, h = q // GH, q % GH
                ins = mm(b[:, 256 * j:256 * j + 256], KQ[:, h, c, 0, :], KQ[:, h, c, :, :])
            ins.then_inc(made, 1)
        for q in range(16):
            c, h = q // RH, q % RH
            j, lo = h // 2, RD * (h % 2)
            b = fill(f"m{q}")
            mm(b[:, 0:256], Bt[lo:lo + RD, j, P * c:P * c + P], AR[lo:lo + RD, j, c, :, :])
            mm(b[:, 256:512], Kt[lo:lo + RD, j, P * c:P * c + P], AR[lo:lo + RD, j, c, :, :]).then_inc(made, 1)

        def lt(q):
            return m4[:, q, 0:P] if q < 16 else GM[:, q - 16, 0, :]

        def inv1(n):
            l, g = INV0[n]
            if l:
                pe.wait_ge(*plan.emptied(f"i3_{l - 1}_{g}"))
            b_ = fill(f"i1_{l}_{g}")
            for j in range(4):
                q = 4 * g + j
                ins_ = mm(b_[:, P * j:P * j + P], lt(q), tinv[:, q, 0, :])
            ins_.then_inc(made, 1)

        pe.wait_ge(tinv_set, 1)
        pe.wait_ge(*plan.emptied("m15"))
        inv1(0)
        for n, (l, g) in enumerate(INV0):
            if n + 1 < len(INV0):
                inv1(n + 1)
            pe.wait_ge(*plan.emptied(f"i1_{l}_{g}"))
            for k, name in enumerate(("i2", "i3")):
                b = fill(f"{name}_{l}_{g}")
                for j in range(2):
                    q = 4 * g + 2 * k + j
                    gm = Gb[:, n % 3, P * (2 * k + j):P * (2 * k + j) + P]
                    mm(b[:, 256 * j:256 * j + P], tinv[:, q, 1, :], gm)
                    ins = mm(b[:, 256 * j + P:256 * j + 256], gm, tinv[:, q, 1, :])
                ins.then_inc(made, 1)

        pe.wait_ge(*plan.emptied(f"i3_{LEVELS - 1}_5"))

        def hcol(h):
            return slice(RD * h, RD * h + RD)

        def rw_w(c):
            b_ = fill(f"w{c}")
            if c:
                pe.wait_ge(*plan.emptied("st"))
            for h in range(RH):
                if c and h % 2 == 0:
                    mm(b_[:, P * (h // 2):P * (h // 2) + P], AR[:, h // 2, 1, 0, :], state_r[:, h // 2, :], True, False,
                       True)
                ins_ = mm(b_[:, hcol(h)], m4[:, 8 * c + h, 256:384], vrow[:, c, hcol(h)], c == 0, True, c == 1)
            ins_.then_inc(made, 1)

        def rw_u(c):
            pe.wait_ge(*plan.emptied(f"w{c}"))
            b_ = fill(f"u{c}")
            for h in range(RH):
                ins_ = mm(b_[:, hcol(h)], tinv[:, 8 * c + h, 1, :], wsb[:, hcol(h)])
            ins_.then_inc(made, 1)

        def rw_y(c):
            b_ = fill(f"y{c}")
            pe.wait_ge(*plan.emptied(f"u{c}"))
            for h in range(RH):
                if c and h % 2 == 0:
                    mm(b_[:, P * (h // 2):P * (h // 2) + P], AR[:, h // 2, 1, 1, :], state_r[:, h // 2, :], True, False,
                       True)
                mm(b_[:, hcol(h)], m4[:, 8 * c + h, 384:512], vrow[:, c, hcol(h)], c == 0, False, c == 1)
                ins_ = mm(b_[:, hcol(h)], m4[:, 8 * c + h, 128:256], un[:, hcol(h)], False, True, c == 1)
            ins_.then_inc(made, 1)

        def gcol(h):
            return slice(GD * h, GD * h + GD)

        def gd(name, lhs, rhs):
            b_ = fill(name)
            for h in range(GH):
                ins_ = mm(b_[:, gcol(h)], lhs(h), rhs(h))
            ins_.then_inc(made, 1)

        rw_w(0)
        gd("gz0", lambda h: tinv[:, 16 + h, 1, :], lambda h: gvrow[:, 0, gcol(h)])
        rw_u(0)
        pe.wait_ge(*plan.emptied("gz0"))
        gd("gs1", lambda h: kdec[:, gcol(h)], lambda h: vnew[:, gcol(h)])
        b = fill("st")
        pe.wait_ge(*plan.emptied("u0"))
        for j in range(RT):
            mm(b[:, P * j:P * j + P], kbT[:, 0, P * j:P * j + P], vrow[:, 0, P * j:P * j + P], True, False)
            ins = mm(b[:, P * j:P * j + P], kbT[:, 1, P * j:P * j + P], un[:, P * j:P * j + P], False, True)
        ins.then_inc(made, 1)
        rw_y(0)
        pe.wait_ge(*plan.emptied("gs1"))
        gd("gp1", lambda h: KQ[:, h, 1, 0, :], lambda h: state_g[:, h, :])
        gd("go0", lambda h: GM[:, h, 1, :], lambda h: vnew[:, gcol(h)])
        rw_w(1)
        pe.wait_ge(r1_ready, 1)
        gd("gz1", lambda h: tinv[:, 20 + h, 1, :], lambda h: r1[:, gcol(h)])
        rw_u(1)
        pe.wait_ge(*plan.emptied("gz1"))
        gd("go1", lambda h: GM[:, 4 + h, 1, :], lambda h: vnew[:, gcol(h)])
        gd("gos", lambda h: KQ[:, h, 1, 1, :], lambda h: state_g[:, h, :])
        rw_y(1)
        pe.wait_ge(sgate_ready, 1)
        pe.wait_ge(d_late, 48)
        for t in range(NT):
            b = fill(f"lg{t}")
            mm(b, sgate[:, P * t:P * t + P], g2sb[:, :]).then_inc(made, 1)
        pe.wait_ge(ycat_ready, 1)
        for n in range(4):
            b = fill(f"yt{n}")
            for j in range(2):
                for t in range(NT):
                    c = 2 * n + j
                    ins = nc.tensor.transpose(b[:, 256 * j + P * t:256 * j + P * t + P],
                                              ycat[:, t, P * c:P * c + P], ident)
            ins.then_inc(made, 1)
        pe.wait_ge(*plan.emptied("yt3"))
        row_block([f"op{t}{half}" for t in range(NT) for half in range(2)], U_EVO, KC)

        def router_logits(tag, layer):
            pe.wait_ge(*plan.emptied(f"{tag}nt3"))
            b_ = fill(f"{tag}rl")
            for t in range(NT):
                v_ = slice(P * t, P * t + P)
                for c in range(KC):
                    mm(b_[:, 20 * t:20 * t + 20], hTh[:, c, v_].bitcast(F32), router[:, layer, c, :], c == 0, False)
                    ins_ = mm(b_[:, 20 * t:20 * t + 20], hTl[:, c, v_].bitcast(F32), router[:, layer, c, :], False,
                              c == KC - 1)
            ins_.then_inc(made, 1)

        def moe(tag, layer):

            def hidden(e, us, i=None):
                for u in us:
                    g = step_unit(layer, e, u) if e else MOE[layer] + u
                    unit(g, i)
                    if u == 0 and e >= 2:
                        v = NE * layer + e - 1
                        pe.wait_ge(gT_low, v if i is None else i * 2 + v)
                    h_, l_ = view(wh, g, "chunks"), view(wl, g, "chunks")
                    for t in range(NT):
                        v_ = slice(P * t, P * t + P)
                        for c in range(2):
                            k = 2 * u + c
                            ins_ = mm3(psum[:, 4 + 2 * (e % 2) + t, :], hTh[:, k, v_], hTl[:, k, v_], h_[:, c, :],
                                       l_[:, c, :], k == 0, k == KC - 1)
                    ins_.then_inc(h_made if u == 3 else used, 1)

            def gated_transposes(e, i=None):
                v = NE * layer + e + 1
                pe.wait_ge(g_made, v if i is None else i * 2 + v)
                for t in range(NT):
                    for k in range(2):
                        ins_ = nc.tensor.transpose(psum[:, 4 + 2 * (e % 2) + t, P * k:P * k + P],
                                                   moeg[:, t, P * k:P * k + P], ident)
                ins_.then_inc(gT_made, 1)

            def down(e, i=None):
                v = NE * layer + e + 1
                pe.wait_ge(gT_low, v if i is None else i * 2 + v)
                for k in range(2):
                    g = step_unit(layer, e + 1, 4 + k) if e + 1 < NE else step_unit(layer, NE, k)
                    unit(g, i)
                    h_, l_ = view(wh, g, "row"), view(wl, g, "row")
                    for t in range(NT):
                        for half in range(2):
                            w = slice(512 * half, 512 * half + 512)
                            ins_ = mm3(psum[:, 2 * t + half, :], moegTh[:, t, k, :], moegTl[:, t, k, :], h_[:, w],
                                       l_[:, w], False, False, True)
                    ins_.then_inc(y_made if k else used, 1)

            def pe_step(e, i=None):
                hidden(e, range(2), i)
                gated_transposes(e - 1, i)
                hidden(e, range(2, 4), i)
                down(e - 1, i)

            router_logits(tag, layer)
            pe.wait_ge(*plan.emptied(f"{tag}rl"))
            for n in range(4):
                t, half = n // 2, n % 2
                mm(psum[:, n, :], ident, X[:, t, 512 * half:512 * half + 512], True, True)
            hidden(0, range(4))
            pe_step(1)
            with pe.Fori(0, NE // 2 - 1) as i:
                pe_step(2, i)
                pe_step(3, i)
            gated_transposes(NE - 1)
            down(NE - 1)

        norm_columns("b", 1)
        moe("b", 0)
        norm_columns("c", 2)
        pe.wait_ge(*plan.emptied("cnt3"))

        def qk_transposes(s, t):
            pe.wait_ge(roped, NT * s + t + 1)
            four_transposes(f"qt{s}{t}", lambda j: qkv[:, t, 512 * s + P * j:512 * s + P * j + P])

        for s in range(9):
            row_strip((f"s{s}0", f"s{s}1"), U_OD + 4 * s)
            if 1 <= s <= 6:
                for t in range(NT):
                    qk_transposes(s - 1, t)

        def scores(h, t):
            nk = P * (t + 1)
            j, lo = h // 2, AD * (h % 2)
            b_ = fill(f"sc{h}{t}a")
            for g in range(AG):
                if t and g == 2:
                    b_ = fill(f"sc{h}{t}b")
                at_ = nk * g if not (t and g == 2) else 0
                ins_ = mm(b_[:, at_:at_ + nk], qkT[lo:lo + AD, 4 * g + j, P * t:P * t + P],
                          qkT[lo:lo + AD, 12 + 4 * g + j, 0:nk])
                if g == 2 or (t and g == 1):
                    ins_.then_inc(made, 1)

        pe.wait_ge(*plan.emptied("qt51"))
        pe.wait_ge(*plan.emptied("s81"))
        scores(0, 0)
        for n, (h, t) in enumerate(HT_):
            if n + 1 < len(HT_):
                scores(*HT_[n + 1])
            pe.wait_ge(probs_ready, n + 1)
            b = fill(f"pt{h}{t}a")
            for j in range(AG * (t + 1)):
                if j == 4:
                    b = fill(f"pt{h}{t}b")
                ins = nc.tensor.transpose(b[:, P * (j % 4):P * (j % 4) + P], probs[:, n % 2, P * j:P * j + P], ident)
                if j in ((2,) if t == 0 else (3, 5)):
                    ins.then_inc(made, 1)
            pe.wait_ge(*plan.emptied(f"pt{h}{t}{'b' if t else 'a'}"))
            b = fill(f"pv{h}{t}")
            for j in range(AG * (t + 1)):
                g, kt = j // (t + 1), j % (t + 1)
                c0 = 3072 + 512 * g + AD * h
                ins = mm(b[:, 0:AD], pT[:, n % 2, P * j:P * j + P], qkv[:, kt, c0:c0 + AD], j == 0,
                         j == AG * (t + 1) - 1)
            ins.then_inc(made, 1)
        pe.wait_ge(*plan.emptied("pv71"))
        for n in range(2):
            b = fill(f"at{n}")
            for j in range(2):
                for t in range(NT):
                    c = 2 * n + j
                    ins = nc.tensor.transpose(b[:, 256 * j + P * t:256 * j + P * t + P],
                                              arow[:, t, P * c:P * c + P], ident)
            ins.then_inc(made, 1)
        pe.wait_ge(*plan.emptied("at1"))
        row_block([f"ao{t}{half}" for t in range(NT) for half in range(2)], U_ODO, 4)
        norm_columns("d", 3)
        moe("d", 1)

    @block.vector
    def _(dve):
        counts = {}

        def then(ins, s_=None):
            s_ = s_ or s_dve
            counts[id(s_)] = counts.get(id(s_), 0) + 1
            ins.then_inc(s_, 1)
            dve.wait_ge(s_, counts[id(s_)])

        V = nc.vector

        def take(name):
            dve.wait_ge(made, plan.made(name))
            return psum[:, plan.bank(name), :]

        def tt(o, a, b_, op, s_=None):
            then(V.tensor_tensor(o, a, b_, op), s_)

        def ts(o, a, s1, s2, op0, op1=None, s_=None):
            if op1 is None:
                then(V.tensor_scalar(o, a, s1, None, op0), s_)
            else:
                then(V.tensor_scalar(o, a, s1, s2, op0, op1), s_)

        def stt(o, a, s1, b_, op0, op1, s_=None):
            then(V.scalar_tensor_tensor(out=o, in0=a, scalar=s1, in1=b_, op0=op0, op1=op1), s_)

        def reduce(o, a, op, s_=None):
            then(V.tensor_reduce(o, a, AX.X, op), s_)

        roots = [0]
        halves = [0]

        def root(m):
            then(V.reciprocal(m, m), root_in)
            roots[0] += 1
            dve.wait_ge(root_out, roots[0])

        def rstd_of(k):
            dve.wait_ge(sq_done, NT * (k + 1))
            ts(sm["rstd"], sm["ssq"], 1.0 / D, RMS_EPS, MUL, ADD)
            root(sm["rstd"])

        def rms_rows(tag, k):
            rstd_of(k)
            for t in range(NT):
                ts(hn[:, t, :].rearrange("q (c p) -> q p c", c=KC), X[:, t, :].rearrange("q (p c) -> q p c", c=KC),
                   sm["rstd"][:, t:t + 1], None, MUL, s_=hn_ready if t == NT - 1 else None)
            for n in range(4):
                b_ = take(f"{tag}nt{n}")
                halves[0] += 1
                dve.wait_ge(half_done, halves[0])
                for j in range(2):
                    c = 2 * n + j
                    ins = V.scalar_tensor_tensor(out=hTl[:, c, :], in0=b_[:, 256 * j:256 * j + 256],
                                                 scalar=gains[:, k, c:c + 1], in1=hTh[:, c, :].bitcast(F32),
                                                 op0=MUL, op1=SUB)
                then(ins, dve_read)

        def columns_low_of(names):
            for n, name in enumerate(names):
                b_ = take(name)
                halves[0] += 1
                dve.wait_ge(half_done, halves[0])
                v_ = hTh[:, 2 * n:2 * n + 2, :].bitcast(F32)
                then(V.tensor_tensor(hTl[:, 2 * n:2 * n + 2, :], b_.rearrange("p (c n) -> p c n", c=2), v_, SUB),
                     dve_read)

        split = [MOE[0]]

        def low_part(g, i=None):
            s_, v = stream.high(g)
            dve.wait_ge(s_, v if i is None else i * 12 + v)
            V.tensor_tensor(wl[:, stream.slot(g), :], raw[:, stream.slot(g), :],
                            wh[:, stream.slot(g), :].bitcast(F32), SUB).then_inc(low_dve, 1)

        def lows(upto):
            for g in range(split[0], upto):
                low_part(g)
            split[0] = max(split[0], upto)

        b = take("params")
        then(V.tensor_copy(par[:, :], b[:, 0:P_ROWS]), dve_read)
        ts(omka[:, :], par[:, P_KA:P_KA + RT], -1.0, 1.0, MUL, ADD)
        rms_rows("a", 0)

        dve.wait_ge(*plan.emptied("loraB"))
        for j, w in ((0, 64), (1, 96)):
            tt(ft[0:w, j, :], rawL[0:w, j, 0:256], rawL[0:w, j, 1:257], SUB)
            stt(fe2[0:w, j, :], ft[0:w, j, :], par[0:w, P_MUL + j:P_MUL + j + 1], rawL[0:w, j, 1:257], MUL, ADD,
                s_=mixl_ready)

        def shift(n, name, dst, mu):
            dve.wait_ge(*plan.emptied(name))
            r_ = rawB[:, 4 * n:4 * n + 4, :]
            tt(ft if n == 0 else fshift, r_[:, :, 0:256], r_[:, :, 1:257], SUB)
            for j in range(4):
                stt(dst[:, j, :], (ft if n == 0 else fshift)[:, j, :], par[:, P_MU + mu + j:P_MU + mu + j + 1],
                    r_[:, j, 1:257], MUL, ADD, s_=fv_ready if name == "v1" and j == 3 else None)

        shift(0, "k1", fk, 4)
        for j in range(RT):
            ts(fkk[:, j, :], fk[:, j, :], par[:, P_KK + j:P_KK + j + 1], None, MUL)
        tt(ft, fkk, fkk, MUL, s_=kksq_ready)
        dve.wait_ge(*plan.emptied("az1"))
        for j in range(RT):
            for c in range(2):
                v = slice(CH * c, CH * c + CH)
                then(V.tensor_tensor_scan(fdx[:, j, v], ones[:, :], fsg[:, j, v], 0.0, MUL, ADD))
        mid = fdx.rearrange("p t (c n) -> p t c n", c=2)
        fsv = sm["fs"].rearrange("p (t o) -> p t o", o=1)
        tt(fsv, mid[:, :, 0, CH - 1:CH], mid[:, :, 0, CH // 2:CH // 2 + 1], SUB)
        tt(fsv, fsv, mid[:, :, 1, CH // 2:CH // 2 + 1], ADD)
        tt(fd.rearrange("p t (c n) -> p t c n", c=2), mid,
           mid[:, :, :, CH // 2:CH // 2 + 1].broadcast_to([P, RT, 2, CH]), SUB)
        tt(fdx, fd, fsg, SUB, s_=decay_in)
        then(V.memset(sm["mark"], 0.0), decay_in)
        shift(1, "r1", fr, 0)
        shift(2, "v1", fv, 8)
        dve.wait_ge(kknorm_done, 1)
        tt(fkk, fkk, ft, MUL)
        tt(ft, fkk, fal, MUL)
        for j in range(RT):
            ts(fal[:, j, :], fal[:, j, :], par[:, P_KA + j:P_KA + j + 1], omka[:, j:j + 1], MUL, ADD)
        tt(fk, fk, fal, MUL)
        dve.wait_ge(decay_out, 3)
        tt(Bt, ft, fd, MUL)
        tt(Kt, fk, fd, MUL)

        def chunks(m):
            return m.rearrange("p t (c n) -> p t c n", c=2)

        tt(AR[:, :, :, 0, :], chunks(fkk), chunks(fdx), MUL)
        tt(AR[:, :, :, 1, :], chunks(fr), chunks(fe2), MUL, s_=cols_ready)
        tt(fr, fr, fk, MUL)
        for j in range(RT):
            ts(fr[:, j, :], fr[:, j, :], par[:, P_RK + j:P_RK + j + 1], None, MUL,
               s_=rkr_ready if j == RT - 1 else None)
        b = take("bon")
        then(V.tensor_copy(sm["bonus"], b[:, 0:16]), dve_read)

        def convolve(n, name, tile0):
            dve.wait_ge(*plan.emptied(name))
            for j in range(4):
                o = conv_out[n][:, j]
                for i in range(CONV):
                    tap = rawA[:, 4 * n + j, i:i + 256].rearrange("p (c n) -> p c n", c=2)
                    wt = par[:, P_CONV + 12 * i + tile0 + j:P_CONV + 12 * i + tile0 + j + 1]
                    last = i == CONV - 1 and j == 3
                    if i == 0:
                        ts(o, tap, wt, None, MUL)
                    else:
                        stt(o, tap, wt, o, MUL, ADD, s_=silu_in if last else None)

        convolve(0, "gk1", 4)
        convolve(1, "gq1", 0)
        convolve(2, "gv1", 8)
        kqf = w_(18432, 2048)
        dve.wait_ge(conv_silu, 2)
        tt(gtmp, kqf, kqf, MUL, s_=gsq_ready)
        abv = sm["ab"].rearrange("p (c s h) -> p c s h", c=2, s=2)

        def ch(m):
            return m.rearrange("p (c h) -> p c h", c=2)

        tt(ch(sm["gx"]), abv[:, :, 0, :], gab[:, 1, :].unsqueeze(1).broadcast_to([P, 2, GH]), ADD)
        stt(sm["gg"], sm["gx"], -1.0, sm["gx"], MUL, MAX, s_=gate_in)
        ts(sm["gx"], sm["gx"], 0.0, None, MAX)
        dve.wait_ge(gate_exp, 3)
        tt(sm["gx"], sm["gx"], sm["ga"], ADD)
        stt(ch(sm["gx"]), ch(sm["gx"]), -1.0, sm["eal"].unsqueeze(1).broadcast_to([P, 2, GH]), MUL, MUL, s_=g_ready)
        dve.wait_ge(made, plan.made("vt1"))
        tt(UG, const("incl").unsqueeze(1).broadcast_to([P, 8, P]), sm["gx"].unsqueeze(2).broadcast_to([P, 8, P]), MUL,
           s_=ug_ready)
        dve.wait_ge(kqnorm_done, 1)
        inv = gtmp.rearrange("p (h c s n) -> p h c s n", h=GH, c=2, s=2)
        tt(KQ[:, :, :, 0, :], KQ[:, :, :, 0, :], inv[:, :, :, 0, :], MUL)
        stt(KQ[:, :, :, 1, :], KQ[:, :, :, 1, :], float(GD) ** -0.5, inv[:, :, :, 1, :], MUL, MUL, s_=kq_ready)
        then(V.memset(sm["mark"], 0.0), early_done)
        b = take("gc")
        then(V.tensor_copy(sm["gc2"], b[:, 0:16]), dve_read)
        tt(sm["kd"], sm["glast"], sm["gc"], SUB)
        for m in range(2):
            b = take(f"gb{m}").rearrange("p (q n) -> p q n", q=4)
            o = GM[:, 4 * m:4 * m + 4, 1, :]
            tt(o, b, sm["gc"][:, 4 * m:4 * m + 4].unsqueeze(2).broadcast_to([P, 4, P]), SUB, s_=dve_read)
            tt(o, o, const("far").unsqueeze(1).broadcast_to([P, 4, P]), ADD, s_=dt_in if m else None)
        dve.wait_ge(dt_exp, 1)
        for q in range(8):
            stt(GM[:, q, 0, :], GM[:, q, 1, :], sm["beta"][:, q:q + 1], const("strict"), MUL, MUL)
        dve.wait_ge(gc_exp, 2)
        b = take("gkt")
        tt(kdec.rearrange("p (h n) -> p h n", h=GH), b.rearrange("p (h n) -> p h n", h=GH),
           sm["kd"][:, 0:4].unsqueeze(2).broadcast_to([P, GH, GD]), MUL, s_=dve_read)
        for n in range(4):
            b = take(f"ga{n}")
            gmv = GM[:, 2 * n:2 * n + 2, :, :].rearrange("p q s n -> p (q s n)")
            tt(gmv, gmv, b, MUL, s_=dve_read)
        dve.wait_ge(m4_zero, 1)
        a0 = CP["strict"][0]
        assert CP["incl"][0] == a0 + P
        causal2 = consts[:, a0:a0 + 2 * P].bitcast(U32).unsqueeze(1).broadcast_to([P, 2, 2 * P])
        for q in range(16):
            b = take(f"m{q}")
            then(V.copy_predicated(m4[:, q, :].rearrange("p (s n) -> p s n", s=2), causal2,
                                   b.rearrange("p (s n) -> p s n", s=2)), dve_read)
        dve.wait_ge(tinv_set, 1)

        def masked_product(n):
            l, g = INV0[n]
            b_ = take(f"i1_{l}_{g}").rearrange("p (q n) -> p q n", q=4)
            tt(Gb[:, n % 3, :].rearrange("p (q n) -> p q n", q=4), b_,
               const(f"level{l}").unsqueeze(1).broadcast_to([P, 4, P]), MUL, s_=dve_read)

        masked_product(0)
        for n, (l, g) in enumerate(INV0):
            if n + 1 < len(INV0):
                masked_product(n + 1)
            for k, name in enumerate(("i2", "i3")):
                b = take(f"{name}_{l}_{g}")
                q = 4 * g + 2 * k
                o = tinv[:, q:q + 2, :, :].rearrange("p q s n -> p (q s n)")
                tt(o, o, b, SUB, s_=dve_read)

        def h4(m):
            return m.rearrange("p (h n) -> p h n", h=GH)

        def per_head(m, c):
            return m[:, 4 * c:4 * c + 4].unsqueeze(2).broadcast_to([P, GH, GD])

        b = take("gz0")
        tt(h4(vnew), h4(b), per_head(sm["beta"], 0), MUL, s_=dve_read)
        b = take("st")
        dve.wait_ge(decay_out, 4)
        for j in range(RT):
            stt(state_r[:, j, :], b[:, P * j:P * j + P], sm["fs"][:, j:j + 1], const("heads64"), MUL, MUL,
                s_=dve_read if j == RT - 1 else None)
        b = take("gp1")
        tt(h4(tmpd), h4(b), per_head(sm["egc"], 1), MUL, s_=dve_read)
        tt(r1, gvrow[:, 1, :], tmpd, SUB, s_=r1_ready)
        b = take("gz1")
        dve.wait_ge(made, plan.made("go0"))
        tt(h4(vnew), h4(b), per_head(sm["beta"], 1), MUL, s_=dve_read)
        b = take("gos")
        tt(h4(tmpd), h4(b), per_head(sm["egc"], 1), MUL, s_=dve_read)
        dve.wait_ge(*plan.emptied("go1"))
        tt(ycat[:, 1, 0:512], ycat[:, 1, 0:512], tmpd, ADD)
        for t in range(NT):
            o = ycat[:, t, 0:512]
            tt(tmpd, o, o, MUL)
            reduce(sm["stat"][:, GH * t:GH * t + GH], h4(tmpd), ADD)
        ts(sm["stat"][:, 0:8], sm["stat"][:, 0:8], 1.0 / GD, RMS_EPS, MUL, ADD)
        root(sm["stat"][:, 0:8])
        for t in range(NT):
            o = ycat[:, t, 0:512]
            st = sm["stat"][:, GH * t:GH * t + GH]
            tt(h4(o), h4(o), st.unsqueeze(2).broadcast_to([P, GH, GD]), MUL)
            tt(h4(o), h4(o), gnw[:, :].unsqueeze(1).broadcast_to([P, GH, GD]), MUL)
            tt(o, o, zr[:, t, :], MUL)
        dve.wait_ge(d_late, 48)
        dve.wait_ge(*plan.emptied("y1"))

        def h8(m):
            return m.rearrange("p (h n) -> p h n", h=RH)

        def b8(m):
            return m.unsqueeze(2).broadcast_to([P, RH, RD])

        for t in range(NT):
            o = ycat[:, t, 512:1024]
            st, st2 = sm["stat"][:, 0:RH], sm["stat2"][:, RH * t:RH * t + RH]
            reduce(st, h8(o), ADD)
            ts(st, st, 1.0 / RD, None, MUL)
            tt(h8(o), h8(o), b8(st), SUB)
            tt(tmpd, o, o, MUL)
            reduce(st2, h8(tmpd), ADD)
            ts(st2, st2, 1.0 / RD, LN_EPS, MUL, ADD)
        root(sm["stat2"])
        for t in range(NT):
            o = ycat[:, t, 512:1024]
            st2 = sm["stat2"][:, RH * t:RH * t + RH]
            tt(h8(o), h8(o), b8(st2), MUL)
            tt(o, o, lnw, MUL)
            tt(o, o, lnb, ADD)
            tt(h8(tmpd), h8(vrow[:, t, :]), b8(sm["bonus"][:, 8 * t:8 * t + 8]), MUL)
            tt(o, o, tmpd, ADD)
            b = take(f"lg{t}")
            tt(o, o, b, MUL, s_=dve_read)
        then(V.memset(sm["mark"], 0.0), ycat_ready)

        def add_residual(prefix):
            for t in range(NT):
                for half in range(2):
                    b_ = take(f"{prefix}{t}{half}")
                    o = X[:, t, 512 * half:512 * half + 512]
                    tt(o, o, b_, ADD, s_=dve_read)
                then(V.memset(sm["mark"], 0.0), x_ready)

        columns_low_of([f"yt{n}" for n in range(4)])
        add_residual("op")
        lows(MOE[0] + Stream.SLOTS)

        def pairs(m, n=4):
            return m.rearrange("p (t n) -> p t n", t=NT)

        def top(dst, src, best):
            tt(pairs(dst), pairs(src), best.unsqueeze(2).broadcast_to([P, NT, 4]), EQ)
            tt(pairs(dst), pairs(dst), const("rank4").unsqueeze(1).broadcast_to([P, NT, 4]), MUL)
            reduce(sm["gt2"], pairs(dst), MAX)
            tt(pairs(dst), pairs(dst), sm["gt2"].unsqueeze(2).broadcast_to([P, NT, 4]), EQ)

        def route(tag, layer):
            b_ = take(f"{tag}rl")
            then(V.tensor_copy(sm["logits"], b_[:, 0:40]), dve_read)
            lg = sm["logits"].rearrange("p (t n) -> p t n", t=NT)
            reduce(sm["gm"], lg[:, :, 0:NG], MAX)
            tt(pairs(sm["ge"]), lg[:, :, 0:NG], sm["gm"].unsqueeze(2).broadcast_to([P, NT, NG]), SUB, s_=route_in)
            then(V.tensor_copy(pairs(sm["gt"]), lg[:, :, 0:NG]))
            top(sm["goh"], sm["gt"], sm["gm"])
            el = lg[:, :, NG:NG + NE].rearrange("p t (g e) -> p t e g", g=NG)
            prod = gates.rearrange("p t (e g) -> p t e g", g=NG)
            tt(prod, el, pairs(sm["goh"]).unsqueeze(2).broadcast_to([P, NT, 4, NG]), MUL)
            reduce(pairs(sm["sel"]), prod, ADD)
            reduce(sm["v1"], pairs(sm["sel"]), MAX)
            top(sm["oh1"], sm["sel"], sm["v1"])
            stt(sm["s2"], sm["oh1"], -3.0e38, sm["sel"], MUL, ADD)
            reduce(sm["v2"], pairs(sm["s2"]), MAX)
            tt(sm["dv"], sm["v2"], sm["v1"], SUB, s_=route_in)
            top(sm["oh2"], sm["s2"], sm["v2"])
            dve.wait_ge(route_exp, 2 * layer + 2)
            reduce(sm["pg"], pairs(sm["ge"]), ADD)
            then(V.reciprocal(sm["pg"], sm["pg"]))
            ts(sm["i1"], sm["dv"], 1.0, None, ADD)
            then(V.reciprocal(sm["i1"], sm["i1"]))
            tt(sm["i1"], sm["i1"], sm["pg"], MUL)
            tt(sm["i2"], sm["i1"], sm["dv"], MUL)
            tt(pairs(sm["oh1"]), pairs(sm["oh1"]), sm["i1"].unsqueeze(2).broadcast_to([P, NT, 4]), MUL)
            tt(pairs(sm["oh2"]), pairs(sm["oh2"]), sm["i2"].unsqueeze(2).broadcast_to([P, NT, 4]), MUL)
            tt(sm["inn"], sm["oh1"], sm["oh2"], ADD)
            for t in range(NT):
                ins = V.tensor_tensor(gates[:, t, :].rearrange("p (g e) -> p g e", g=NG),
                                      pairs(sm["goh"])[:, t, :].unsqueeze(2).broadcast_to([P, NG, 4]),
                                      pairs(sm["inn"])[:, t, :].unsqueeze(1).broadcast_to([P, NG, 4]), MUL)
                then(ins)

        def moe(tag, layer):
            route(tag, layer)

            def gate(e, i=None):
                v = NE * layer + e + 1
                dve.wait_ge(silu_done, v if i is None else i * 2 + v)
                for t in range(NT):
                    ge = gates[:, t, e:e + 1] if i is None else gates[:, t, bass.ds(i * 2 + e, 1)]
                    ins_ = V.scalar_tensor_tensor(out=moeg[:, t, :], in0=moes[:, t, :], scalar=ge,
                                                  in1=psum[:, 4 + 2 * (e % 2) + t, FF:2 * FF], op0=MUL, op1=MUL)
                ins_.then_inc(g_made, 1)

            def transposed_low(e, i=None):
                v = NE * layer + e + 1
                dve.wait_ge(gT_high, v if i is None else i * 2 + v)
                V.tensor_tensor(moegTl[:, :, :, :].rearrange("p t k n -> p t (k n)"),
                                psum[:, 4 + 2 * (e % 2):6 + 2 * (e % 2), 0:FF],
                                moegTh[:, :, :, :].rearrange("p t k n -> p t (k n)").bitcast(F32),
                                SUB).then_inc(gT_low, 1)

            def dve_step(e, i=None):
                for u in range(3):
                    low_part(step_unit(layer, e, u), i)
                transposed_low(e - 1, i)
                for u in range(3, 6):
                    low_part(step_unit(layer, e, u), i)
                gate(e, i)

            lows(MOE[layer] + 4)
            gate(0)
            dve_step(1)
            with dve.Fori(0, NE // 2 - 1) as i:
                dve_step(2, i)
                dve_step(3, i)
            split[0] = step_unit(layer, NE, 0)
            transposed_low(NE - 1)
            lows(split[0] + 2)
            if layer == 0:
                lows(split[0] + Stream.SLOTS)
            dve.wait_ge(y_made, NE * (layer + 1))
            for t in range(NT):
                for half in range(2):
                    then(V.tensor_copy(X[:, t, 512 * half:512 * half + 512], psum[:, 2 * t + half, :]),
                         x_ready if half else None)

        rms_rows("b", 1)
        moe("b", 0)
        rms_rows("c", 2)
        half_d = AD // 2
        ang, turns, sin_, cos_ = (trig[:, 64 * n:64 * n + 64] for n in range(4))
        posf = sm["mx"]
        then(V.tensor_copy(posf, possb[:, :]))
        tt(pairs(ang), posf.unsqueeze(2).broadcast_to([P, NT, half_d]),
           const("invf").unsqueeze(1).broadcast_to([P, NT, half_d]), MUL)
        ROUND = 12582912.0
        ts(turns, ang, float(1.0 / (2.0 * np.pi)), None, MUL)
        ts(turns, turns, ROUND, None, ADD)
        ts(turns, turns, ROUND, None, SUB)
        two_pi = 2.0 * np.pi
        p1 = 6.28125
        p2 = float(np.float32(np.round((two_pi - p1) * 2 ** 21) / 2 ** 21))
        p3 = two_pi - p1 - p2
        for part in (p1, p2, p3):
            stt(ang, turns, -part, ang, MUL, ADD)
        ts(sin_, ang, -3.14159, 3.14159, MAX, ALU.min)
        stt(cos_, sin_, -1.0, sin_, MUL, MAX)
        ts(cos_, cos_, -1.0, float(np.pi / 2), MUL, ADD, s_=trig_in)
        dve.wait_ge(trig_done, 1)
        ccos = w_(24704, 128).rearrange("p (t n) -> p t n", t=NT)
        csin = w_(24832, 128).rearrange("p (t n) -> p t n", t=NT)
        for a in range(2):
            then(V.tensor_copy(ccos[:, :, 32 * a:32 * a + 32], pairs(cos_)))
            ts(csin[:, :, 32 * a:32 * a + 32], pairs(sin_), 1.0 if a else -1.0, None, MUL)
        for s in range(6):
            for t in range(NT):
                n = NT * s + t
                lows(U_OD + 4 * s + 4 + Stream.SLOTS)
                b = take(f"s{s}{t}").rearrange("p (h a n) -> p h a n", h=8, a=2)
                if n >= 2:
                    dve.wait_ge(roped, n - 1)
                o = rtmp[:, n % 2, :, 0:512].rearrange("p s (h a n) -> p s h a n", h=8, a=2)
                for a in range(2):
                    cb = ccos[:, t, 32 * a:32 * a + 32].unsqueeze(1).broadcast_to([P, 8, 32])
                    sb_ = csin[:, t, 32 * a:32 * a + 32].unsqueeze(1).broadcast_to([P, 8, 32])
                    then(V.tensor_tensor(o[:, 0, :, a, :], b[:, :, a, :], cb, MUL))
                    ins = V.tensor_tensor(o[:, 1, :, a, :], b[:, :, 1 - a, :], sb_, MUL)
                    if a == 0:
                        then(ins)
                then(ins, dve_read)
                then(V.memset(sm["mark"], 0.0), rope_ready)
        lows(U_ODO + Stream.SLOTS)
        dve.wait_ge(d_mask, 16)

        def masked_scores(n):
            h, t = HT_[n]
            nk = P * (t + 1)
            m0 = 384 * t
            b_ = take(f"sc{h}{t}a")
            w = 384 if t == 0 else 512
            o = scs[:, n % 2, :]
            stt(o[:, 0:w], b_[:, 0:w], float(AD) ** -0.5, masks[:, m0:m0 + w], MUL, ADD, s_=dve_read)
            if t:
                b_ = take(f"sc{h}{t}b")
                stt(o[:, 512:768], b_[:, 0:256], float(AD) ** -0.5, masks[:, m0 + 512:m0 + 768], MUL, ADD, s_=dve_read)
            reduce(sm["mx"][:, n % 2:n % 2 + 1], o[:, 0:AG * nk], MAX)
            ts(sm["nmx"][:, n % 2:n % 2 + 1], sm["mx"][:, n % 2:n % 2 + 1], -1.0, None, MUL, s_=scores_ready)

        masked_scores(0)
        for n in range(len(HT_)):
            if n + 1 < len(HT_):
                masked_scores(n + 1)
            dve.wait_ge(probs_ready, n + 1)
            then(V.reciprocal(sm["rden"][:, n % 2:n % 2 + 1], sm["den"][:, n % 2:n % 2 + 1]), rden_ready)
        columns_low_of([f"at{n}" for n in range(2)])
        lows(MOE[1])
        add_residual("ao")
        lows(MOE[1] + Stream.SLOTS)
        rms_rows("d", 3)
        moe("d", 1)
        rstd_of(4)
        dve.wait_ge(d_fin, 16)
        for t in range(NT):
            stt(hn[:, t, :], X[:, t, :], sm["rstd"][:, t:t + 1], w_(0, D), MUL, MUL, s_=out_ready)


_INS = ['x', 'positions', 'ev_norm', 'ev_w_in', 'ev_w_out', 'gdn_conv_w', 'gdn_A_log', 'gdn_dt_bias', 'gdn_norm',
        'rwkv_mu', 'rwkv_w0', 'rwkv_w2', 'rwkv_a0', 'rwkv_a2', 'rwkv_g2', 'rwkv_k_k', 'rwkv_k_a', 'rwkv_r_k',
        'rwkv_ln_w', 'rwkv_ln_b', 'od_norm', 'od_w_in', 'od_w_out', 'ffn_norm', 'moe_w_group', 'moe_w_expert',
        'moe_w1', 'moe_w3', 'moe_w2', 'final_norm']


def kernel(**inputs):
    import numpy as _np
    import concourse.bacc as _bacc
    from concourse import mybir as _mybir
    from concourse.bass_utils import run_bass_kernel_spmd as _run

    nc = _bacc.Bacc("TRN2", target_bir_lowering=False, num_devices=1)
    arrays, args = {}, []
    given = {name: _np.ascontiguousarray(inputs[name]) for name in _INS}
    given["const_mats"], _, given["attn_masks"] = constants()
    for name, a in given.items():
        arrays[f"in_{name}_dram"] = a
        args.append(nc.dram_tensor(f"in_{name}_dram", a.shape, _mybir.dt.from_np(a.dtype), kind="ExternalInput").ap())
    args.append(nc.dram_tensor("out_0_dram", (1, S, D), _mybir.dt.float32, kind="ExternalOutput").ap())
    trunk(nc, *args)
    r = _run(nc, [arrays], core_ids=[0])
    return r.results[0]["out_0_dram"]
```

```python
from contextlib import ExitStack

import numpy as np

import concourse.bass as bass
from concourse import mybir

P = 128
F32 = mybir.dt.float32
F32R = mybir.dt.float32r
I32 = mybir.dt.int32
U32 = mybir.dt.uint32
ALU = mybir.AluOpType
ACT = mybir.ActivationFunctionType
AX = mybir.AxisListType
ADD, SUB, MUL, MAX, EQ = ALU.add, ALU.subtract, ALU.mult, ALU.max, ALU.is_equal

SMALL_DMAS = 14
D = 1024
S = 256
NT = S // P
KC = D // P
RMS_EPS = 1e-6
GH, GD = 4, 128
CONV = 4
RH, RD = 8, 64
RT = RH * RD // P
LORA_W, LORA_A, LORA_G = 32, 32, 96
LN_EPS = 64e-5
NG, NEG_ = 4, 4
NE = NG * NEG_
FF = 256
AH, AD, AG = 8, 64, 3
DILATIONS = (1, 4, 16)
SPAN = 128
AB = 3
ROPE_THETA = 10000.0
CH = 128
LEVELS = 7
DECAY = float(np.exp(-0.5))
FAR = -1.0e30
BANKS = 8

C_Q, C_K, C_V, C_Z, C_AB, C_R, C_RK, C_RV, C_LORA = 0, 512, 1024, 1536, 2048, 2056, 2568, 3080, 3592


def constants():
    i = np.arange(P)[:, None]
    j = np.arange(P)[None, :]
    incl = (i <= j).astype(np.float32)
    strict = (i < j).astype(np.float32)
    parts = {"ident": np.eye(P, dtype=np.float32), "strict": strict, "incl": incl,
             "far": np.where(i <= j, 0.0, FAR).astype(np.float32),
             "heads64": (i // RD == j // RD).astype(np.float32)}
    parts["neg"] = -np.eye(P, dtype=np.float32)
    for l in range(LEVELS):
        b = 1 << l
        parts[f"level{l}"] = ((i // (2 * b) == j // (2 * b)) & (i // b % 2 == 1) & (j // b % 2 == 0)).astype(np.float32)
        if l == 0:
            parts["level0t"] = parts["level0"].T
    parts["invf"] = np.tile((ROPE_THETA ** (-np.arange(AD // 2, dtype=np.float32) * 2.0 / AD)).astype(np.float32), (P, 1))
    parts["rank4"] = np.tile(np.array([4, 3, 2, 1], np.float32), (P, 1))
    place, at = {}, 0
    for name, m in parts.items():
        place[name] = (at, m.shape[1])
        at += m.shape[1]
    masks = []
    for t in range(NT):
        keys = np.arange((t + 1) * P)[None, :]
        rel = (t * P + i) - keys
        masks.append(np.concatenate([np.where((rel >= 0) & (rel % d == 0) & (rel <= SPAN * d), 0.0, FAR)
                                     for d in DILATIONS], 1).astype(np.float32))
    return np.concatenate(list(parts.values()), 1), place, np.concatenate(masks, 1)


P_CONV, P_MU, P_MUL, P_W0, P_A0, P_KK, P_KA, P_RK = 0, 48, 60, 62, 66, 70, 74, 78
P_ROWS = 82


class PsumPlan:

    def __init__(self, sems):
        self.sems = sems
        self.jobs = []
        self.index = {}
        self.first = 0
        self.first_bank = 0
        self.norm = 0

    def segment(self, bank=0, norm=0):
        self.first = len(self.jobs)
        self.first_bank = bank
        self.norm = norm

    def add(self, name, reader):
        assert name not in self.index, name
        self.index[name] = len(self.jobs)
        self.jobs.append((name, reader, self.first, self.first_bank, self.norm))

    def bank(self, name):
        n = self.index[name]
        return (n - self.jobs[n][2] + self.jobs[n][3]) % BANKS

    def made(self, name):
        return self.index[name] + 1

    def emptied(self, name):
        n = self.index[name]
        reader = self.jobs[n][1]
        return self.sems[reader], sum(1 for job in self.jobs[:n + 1] if job[1] == reader)

    def must_be_empty(self, name):
        n = self.index[name]
        upto = n - BANKS + 1 if n - self.jobs[n][2] >= BANKS else self.jobs[n][2] - self.jobs[n][4]
        for reader in ("act", "dve"):
            count = sum(1 for job in self.jobs[:upto] if job[1] == reader)
            if count:
                yield self.sems[reader], count


class Stream:
    SLOTS = 3

    def __init__(self, plan):
        self.plan = plan
        self.units = []
        self.low_by = []
        self.sems = {}

    def add(self, loads, release, low_by):
        self.units.append((loads, release))
        self.low_by.append(low_by)

    def slot(self, g):
        return g % self.SLOTS

    def landed(self, g):
        count = sum(16 * len(self.units[k][0]) for k in range(g + 1) if k % self.SLOTS == g % self.SLOTS)
        return self.sems["landed"][g % self.SLOTS], count

    def high(self, g):
        return self.sems["high"], g + 1

    def low(self, g):
        return self.sems["low_" + self.low_by[g]], self.low_by[:g + 1].count(self.low_by[g])

    def released(self, g):
        release = self.units[g][1]
        if release in ("used", "h_made", "y_made"):
            return self.sems[release], sum(1 for u in self.units[:g + 1] if u[1] == release)
        return self.sems["made"], self.plan.made(release)


def trunk(nc, x, positions, ev_norm, ev_w_in, ev_w_out, gdn_conv_w, gdn_A_log, gdn_dt_bias, gdn_norm, rwkv_mu,
          rwkv_w0, rwkv_w2, rwkv_a0, rwkv_a2, rwkv_g2, rwkv_k_k, rwkv_k_a, rwkv_r_k, rwkv_ln_w, rwkv_ln_b,
          od_norm, od_w_in, od_w_out, ffn_norm, moe_w_group, moe_w_expert, moe_w1, moe_w3, moe_w2, final_norm,
          const_mats, attn_masks, out):
    _, CP, _ = constants()
    ctx = ExitStack()

    def sb(name, shape, dt=F32):
        return ctx.enter_context(nc.sbuf_tensor(name, shape, dt))

    def sem(name):
        return ctx.enter_context(nc.semaphore(name))

    consts = sb("consts", [P, const_mats.shape[1]])

    def const(name):
        a, w = CP[name]
        return consts[:, a:a + w]

    ident = const("ident")
    ones = sb("ones", [P, P])
    X = sb("X", [P, NT, D])
    hn = sb("hn", [P, NT, D])
    hTh = sb("hTh", [P, KC, S], F32R)
    hTl = sb("hTl", [P, KC, S], F32R)
    raw = sb("raw", [P, Stream.SLOTS, 1024])
    wh = sb("wh", [P, Stream.SLOTS, 1024], F32R)
    wl = sb("wl", [P, Stream.SLOTS, 1024], F32R)
    moegTh = sb("moegTh", [P, NT, 2, P], F32R)
    moegTl = sb("moegTl", [P, NT, 2, P], F32R)
    work = sb("work", [P, 27648])
    par = sb("par", [P, P_ROWS])
    omka = sb("omka", [P, RT])
    gains = sb("gains", [P, 4, KC])
    loraw = sb("loraw", [LORA_W + LORA_A, 512])
    gnw = sb("gnw", [P, GD])
    gab = sb("gab", [P, 2, GH])
    RW = 2 * KC * (NG + NE) + P - (NG + NE)
    router_flat = sb("router", [P, RW])
    router = router_flat[:, 0:2 * KC * (NG + NE)].rearrange("p (l c n) -> p l c n", l=2, c=KC)
    routerh = sb("routerh", [P, RW], F32R)
    routerl = sb("routerl", [P, RW], F32R)
    possb = sb("possb", [P, NT], I32)
    small = sb("small", [P, 512])
    logitsT = sb("logitsT", [NG + NE, S])
    sgate = sb("sgate", [LORA_G, S])
    psum = ctx.enter_context(nc.psum_tensor("psum", [P, BANKS, 512], F32))

    def w_(a, n):
        return work[:, a:a + n]

    m4 = w_(0, 8192).rearrange("p (q n) -> p q n", n=512)
    tinv = w_(8192, 6144).rearrange("p (q s n) -> p q s n", s=2, n=P)
    tinv4 = w_(8192, 6144).rearrange("p (q n) -> p q n", n=P)
    AR = w_(14336, 2048).rearrange("p (t c s n) -> p t c s n", t=RT, c=2, s=2)
    Bt = w_(16384, 1024).rearrange("p (t n) -> p t n", t=RT)
    Kt = w_(17408, 1024).rearrange("p (t n) -> p t n", t=RT)
    Bt_odd = w_(23552, 1024).rearrange("p (t n) -> p t n", t=RT)
    Kt_odd = w_(26112, 1024).rearrange("p (t n) -> p t n", t=RT)
    KQ = w_(18432, 2048).rearrange("p (h c s n) -> p h c s n", h=GH, c=2, s=2)
    GM = w_(20480, 2048).rearrange("p (q s n) -> p q s n", s=2, n=P)
    zr = w_(22528, 1024).rearrange("p (t n) -> p t n", t=NT)
    UG = w_(23552, 1024).rearrange("p (q n) -> p q n", n=P)
    kbT = w_(24576, 1024).rearrange("p (s n) -> p s n", s=2)
    kdec = w_(25600, 512)
    Gb = w_(26112, 1536).rearrange("p (b n) -> p b n", b=3)
    vrow = hn[:, 0, :].rearrange("p (t n) -> p t n", t=NT)
    gvrow = hn[:, 1, :].rearrange("p (t n) -> p t n", t=NT)
    rawB = w_(0, 12 * 257).rearrange("p (t n) -> p t n", n=257)
    rawA = w_(3084, 12 * 259).rearrange("p (t n) -> p t n", n=259)
    rawL = w_(6192, 514).rearrange("p (t n) -> p t n", n=257)
    prow = w_(7730, P)
    convv = w_(6706, 1024).rearrange("p (t n) -> p t n", t=4)
    fk, fr, fsg, fal, fd, fdx = [w_(8192 + 1024 * n, 1024).rearrange("p (t n) -> p t n", t=RT) for n in range(6)]
    fv, fe2, fkk, ft = [w_(23552 + 1024 * n, 1024).rearrange("p (t n) -> p t n", t=RT) for n in range(4)]
    gtmp = w_(25600, 2048)
    conv_out = [KQ[:, :, :, 0, :], KQ[:, :, :, 1, :], convv.rearrange("p h (c n) -> p h c n", c=2)]
    fshift = w_(16384, 1024).rearrange("p (t n) -> p t n", t=RT)
    wsb = w_(16384, 512)
    un = w_(16896, 512)
    state_r = w_(17408, 512).rearrange("p (t n) -> p t n", t=RT)
    vnew = w_(17920, 512)
    r1 = w_(26112, 512)
    state_g = w_(26624, 512).rearrange("p (h n) -> p h n", h=GH)
    tmpd = w_(27136, 512)
    ycat = w_(8192, 2048).rearrange("p (t n) -> p t n", t=NT)
    lnw, lnb = KQ[:, :, 0, 0, :], KQ[:, :, 0, 1, :]
    g2sb = AR[0:LORA_G, :, 0, 0, :]
    vb = w_(23552, 1024).rearrange("p (t n) -> p t n", t=NT)
    qkv = w_(0, 2 * 4608).rearrange("p (t n) -> p t n", t=NT)
    qkT = w_(9216, 6144).rearrange("p (i n) -> p i n", n=S)
    masks = w_(15360, 1152)
    probs = w_(16512, 768 * AB).rearrange("p (b n) -> p b n", b=AB)
    pT, scs = [w_(a, 768 * 2).rearrange("p (b n) -> p b n", b=2) for a in (18816, 24960)]
    q_odd = [hn[:, n // 4, S * (n % 4):S * (n % 4) + S] for n in range(8)] + [w_(26496 + S * n, S) for n in range(4)]
    rtmp = w_(21120, 2048).rearrange("p (b s n) -> p b s n", b=2, s=2)
    trig = w_(23168, 512)
    arow = w_(23680, 1024).rearrange("p (t n) -> p t n", t=NT)
    moes = w_(26112, 512).rearrange("p (t n) -> p t n", t=NT)
    moeg = w_(26624, 512).rearrange("p (t n) -> p t n", t=NT)
    sm = {}
    at = GC0 = 0
    for name, n in (("ssq", 2), ("rstd", 2), ("ab", 16), ("beta", 8), ("gx", 8), ("ga", 8), ("gg", 8), ("gc", 8),
                    ("glast", 8), ("egc", 8), ("kd", 8), ("fs", 4), ("bonus", 16), ("stat", 8), ("var", 24),
                    ("logits", 40), ("gm", 2), ("unused", 1), ("gt", 8), ("gt2", 2), ("goh", 8), ("ge", 8), ("pg", 2),
                    ("sel", 8), ("v1", 2), ("v2", 2), ("oh1", 8), ("oh2", 8), ("s2", 8), ("dv", 2), ("i1", 2),
                    ("i2", 2), ("inn", 8), ("gates", 32), ("posf", 2), ("mx", AB), ("nmx", AB), ("den", AB), ("rden", AB), ("eal", 4), ("mark", 2)):
        sm[name] = small[:, at:at + n]
        GC0 = at if name == "gc" else GC0
        at += n
    assert at <= 512
    sm["gc2"] = small[:, GC0:GC0 + 16]
    gates = sm["gates"].rearrange("p (t e) -> p t e", t=NT)

    eps6 = sb("eps6", [P, 1])

    made, act_read, dve_read = sem("made"), sem("act_read"), sem("dve_read")
    s_act, s_dve, s_pool = sem("act_steps"), sem("dve_steps"), sem("pool_steps")
    d_x = [sem(f"d_x{t}") for t in range(NT)]
    d_const, d_par, d_small, d_mask = sem("d_const"), sem("d_par"), sem("d_small"), sem("d_mask")
    d_lora = sem("d_lora")
    d_gains, d_ident = sem("d_gains"), sem("d_ident")
    d_fin, d_out = sem("d_fin"), sem("d_out")
    landed = [sem(f"landed{b}") for b in range(Stream.SLOTS)]
    high, low_pool, low_dve, used = sem("high"), sem("low_pool"), sem("low_dve"), sem("used")
    first_sums = sem("first_sums")
    d_late, half_done = sem("d_late"), sem("half_done")
    ones_set, pads_set, m4_zero = sem("ones_set"), sem("pads_set"), sem("m4_zero")
    router_split_h, router_split = sem("router_split_h"), sem("router_split")
    rms_ready, hn_ready = sem("rms_ready"), sem("hn_ready")
    mixl_ready, lorain_ready, sgate_ready = sem("mixl_ready"), sem("lorain_ready"), sem("sgate_ready")
    kksq_ready, rkr_ready, cols_ready, decay_in, decay_out = (sem("kksq_ready"), sem("rkr_ready"), sem("cols_ready"),
                                                               sem("decay_in"), sem("decay_out"))
    fv_ready, silu_in = sem("fv_ready"), sem("silu_in")
    conv_silu, rden_ready, beta_done = sem("conv_silu"), sem("rden_ready"), sem("beta_done")
    gsq_ready, kq_ready = sem("gsq_ready"), sem("kq_ready")
    gate_in, gate_exp, g_ready, ug_ready, dt_in, dt_exp, gc_exp = (sem("gate_in"), sem("gate_exp"), sem("g_ready"),
                                                                   sem("ug_ready"), sem("dt_in"), sem("dt_exp"),
                                                                   sem("gc_exp"))
    odd_heads = sem("odd_heads")
    one_head, terms_ready = sem("one_head"), sem("terms_ready")
    inverse_ready, gated_ready = sem("inverse_ready"), sem("gated_ready")
    var_ready, deviation_ready = sem("var_ready"), sem("deviation_ready")
    r1_ready, ycat_ready = sem("r1_ready"), sem("ycat_ready")
    x_ready = sem("x_ready")
    route_in, route_exp = sem("route_in"), sem("route_exp")
    kknorm_done, kqnorm_done, gT_high, gT_low = sem("kknorm_done"), sem("kqnorm_done"), sem("gT_high"), sem("gT_low")
    h_made, silu_done, g_made, gT_made, y_made = (sem("h_made"), sem("silu_done"), sem("g_made"), sem("gT_made"),
                                                  sem("y_made"))
    q_zeros = sem("q_zeros")
    trig_in, trig_done, rope_ready, roped = sem("trig_in"), sem("trig_done"), sem("rope_ready"), sem("roped")
    scores_ready, probs_ready, out_ready = sem("scores_ready"), sem("probs_ready"), sem("out_ready")

    plan = PsumPlan({"act": act_read, "dve": dve_read})

    def plan_norm(tag):
        for n in range(4):
            plan.add(f"{tag}nt{n}", "dve")

    def plan_router(tag):
        plan.segment(6, norm=4)
        plan.add(f"{tag}rt", "dve")
        plan.add(f"{tag}rl", "dve")
        plan.segment()

    FORM = []
    for k in range(9):
        FORM += [("m", q) for q in (2 * k, 2 * k + 1) if k < 8]
        FORM += [("i0", k - 1)] if k else []
    FORM += [("i0", k) for k in range(8, 12)]
    INV0 = [(l, g) for l in range(1, LEVELS) for g in range(6)]
    plan_norm("a")
    for n, e in (("loraA", "act"), ("loraB", "act"), ("params", "dve"), ("ab", "act"), ("k0", "act"), ("k1", "act"),
                 ("wz0", "act"), ("wz1", "act"), ("az0", "act"), ("az1", "act"),
                 ("r0", "act"), ("r1", "act"), ("ss0", "act"), ("ss1", "act"), ("v0", "act"), ("v1", "act"),
                 ("gk0", "act"), ("gk1", "act"), ("gq0", "act"), ("gq1", "act"), ("vt0", "act"), ("vt1", "act"),
                 ("gv0", "act"), ("gv1", "act"), ("bon", "dve"), 
                 ("gss0", "act"), ("gss1", "act"), ("gss2", "act"), ("gss3", "act"), ("z0", "act"), ("z1", "act"),
                 ("kt0", "act"), ("bt0", "act"), ("gc", "dve"), ("gb0", "dve"), ("gb1", "dve"), ("gvt0", "act"), ("gvt1", "act"),
                 ("gkt", "dve"), ("ga0", "dve"), ("ga1", "dve"), ("ga2", "dve"), ("ga3", "dve")):
        plan.add(n, e)
    for kind, q in FORM:
        plan.add(f"{kind}{q}" if kind == "m" else f"i0_{q}", "dve")
    for n, (l, g) in enumerate(INV0):
        if n == 0:
            plan.add(f"i1_{l}_{g}", "dve")
        if n + 1 < len(INV0):
            l1, g1 = INV0[n + 1]
            plan.add(f"i1_{l1}_{g1}", "dve")
        plan.add(f"i2_{l}_{g}", "dve")
        if n and INV0[n - 1][0] < LEVELS - 1:
            plan.add("tr_%d_%d" % INV0[n - 1], "act")
    for n, e in (("w0", "act"), ("gz0", "dve"), ("u0", "act"), ("gs1", "act"), ("st", "dve"), ("y0", "act"),
                 ("gp1", "dve"), ("go0", "act"), ("w1", "act"), ("gz1", "dve"), ("u1", "act"), ("go1", "act"),
                 ("gos", "dve"), ("y1", "act"), ("lg0", "dve"), ("lg1", "dve")):
        plan.add(n, e)
    for n in range(4):
        plan.add(f"yt{n}", "dve")
    for t in range(NT):
        for half in range(2):
            plan.add(f"op{t}{half}", "dve")
    plan_norm("b")
    plan_router("b")
    plan_norm("c")
    for s in range(9):
        for t in range(NT):
            plan.add(f"s{s}{t}", "dve" if s < 6 else "act")
        if 1 <= s <= 6:
            for t in range(NT):
                plan.add(f"qt{s - 1}{t}", "act")
    HT_ = [(h, t) for h in range(AH) for t in range(NT)]

    def plan_scores(h, t):
        plan.add(f"sc{h}{t}a", "dve")
        if t:
            plan.add(f"sc{h}{t}b", "dve")

    for n in range(-AB, len(HT_)):
        if n + AB < len(HT_):
            plan_scores(*HT_[n + AB])
        if 0 <= n + 1 < len(HT_):
            h, t = HT_[n + 1]
            plan.add(f"pt{h}{t}a", "act")
            if t:
                plan.add(f"pt{h}{t}b", "act")
        if n >= 0:
            plan.add("pv%d%d" % HT_[n], "act")
    for n in range(2):
        plan.add(f"at{n}", "dve")
    for t in range(NT):
        for half in range(2):
            plan.add(f"ao{t}{half}", "dve")
    plan_norm("d")
    plan_router("d")

    stream = Stream(plan)
    stream.sems = {"landed": landed, "high": high, "low_pool": low_pool, "low_dve": low_dve, "used": used,
                   "made": made, "h_made": h_made, "y_made": y_made}
    ev_k = ev_w_in[0].rearrange("(p c) n -> p c n", c=KC)
    od_k = od_w_in[0].rearrange("(p c) n -> p c n", c=KC)
    evo_k = ev_w_out[0].rearrange("(c p) n -> p c n", p=P)
    odo_k = od_w_out[0].rearrange("(c p) n -> p c n", p=P)

    def unit_cols(loads, release, low_by):
        stream.add([(("cols", a, n), src) for a, n, src in loads], release, low_by)

    def add_tiles(c0, names):
        for j in range(4):
            unit_cols([(0, P, ev_k[:, :, c0 + P * j:c0 + P * j + P])], names[j // 2] if j % 2 else "used", "pool")

    def add_strip(src, c0, last, low_by, pool_first=0):
        for j in range(4):
            stream.add([(("chunks", 0, 512), src[:, 2 * j:2 * j + 2, c0:c0 + 512])], last if j == 3 else "used",
                       "pool" if j < pool_first else low_by)

    def add_rows(src, n, last, low_by):
        for c in range(n):
            stream.add([(("row", 0, D), src[:, c, :])], last if c == n - 1 else "used", low_by)

    def hidden_loads(layer, e, u):
        return [(("chunks", FF * k, FF), expert(w, layer, e).rearrange("(p c) f -> p c f", c=KC)[:, 2 * u:2 * u + 2, :])
                for k, w in enumerate((moe_w1, moe_w3))]

    def down_load(layer, e, k):
        return [(("row", 0, D), expert(moe_w2, layer, e).rearrange("(k p) n -> p k n", p=P)[:, k, :])]

    def expert(w, layer, e):
        return w[layer, e] if isinstance(e, int) else w[layer, bass.ds(e, 1)].rearrange("o a b -> (o a) b")

    def add_moe(layer):
        first = len(stream.units)
        for e in range(NE + 1):
            if e < NE:
                for u in range(4):
                    stream.add(hidden_loads(layer, e, u), "h_made" if u == 3 else "used",
                               "pool" if e == 0 and u < Stream.SLOTS else "dve")
            if e:
                for k in range(2):
                    stream.add(down_load(layer, e - 1, k), "y_made" if k else "used", "dve")
        return first

    unit_cols([(0, 64, ev_k[:, :, C_LORA:C_LORA + 64]), (64, 8, ev_k[:, :, C_AB:C_AB + 8]), (72, 56, ev_k[:, :, 0:56])],
              "loraA", "dve")
    unit_cols([(0, 96, ev_k[:, :, C_LORA + 64:C_LORA + 160]), (96, 32, ev_k[:, :, 0:32])], "loraB", "dve")
    U_K = len(stream.units)
    for c0, names in ((C_RK, "k"), (C_R, "r"), (C_RV, "v"), (C_K, "gk"), (C_Q, "gq"), (C_V, "gv")):
        add_tiles(c0, (f"{names}0", f"{names}1"))
    U_Z = len(stream.units)
    add_strip(ev_k, C_Z, "z1", "pool")
    U_EVO = len(stream.units)
    add_rows(evo_k, KC, "op11", "pool")
    MOE = [add_moe(0)]
    U_OD = len(stream.units)
    for n in range(9):
        add_strip(od_k, 512 * n, f"s{n}1", "dve", Stream.SLOTS if n == 0 else 0)
    U_ODO = len(stream.units)
    add_rows(odo_k, 4, "ao11", "dve")
    MOE.append(add_moe(1))

    def view(buf, g, kind):
        flat = buf[:, stream.slot(g), :]
        if kind == "cols":
            return flat.rearrange("p (c n) -> p c n", c=KC)
        return flat.rearrange("p (c n) -> p c n", c=2) if kind == "chunks" else flat

    LANDED_PER_STEP = [16 * (len(stream.units[MOE[0] + 4 + u][0]) + len(stream.units[MOE[0] + 7 + u][0]))
                       for u in range(3)]
    RELEASED_PER_STEP = {"used": 4, "h_made": 1, "y_made": 1}

    def step_unit(layer, e, u):
        return MOE[layer] + 4 + 6 * (e - 1) + u

    block = ctx.enter_context(nc.Block())

    @block.sync
    def _(sp):
        xr = x[0].rearrange("(t p) n -> p t n", p=P)
        for t in range(NT):
            sp.dma_start(X[:, t, :], xr[:, t, :]).then_inc(d_x[t], 16)
        for n, src in enumerate((ev_norm[0], ffn_norm[0], od_norm[0], ffn_norm[1])):
            sp.dma_start(gains[:, n, :], src.rearrange("(p c) -> p c", c=KC)).then_inc(d_gains, 16)
        sp.dma_start(consts[:, 0:P], const_mats[:, 0:P]).then_inc(d_ident, 16)
        def load(g, loads=None, i=None, per_round=None):
            loads = loads or stream.units[g][0]
            if g >= Stream.SLOTS:
                s_, v = stream.low(g - Stream.SLOTS)
                sp.wait_ge(s_, v if i is None else i * 6 + v)
            for (kind, a, n), src in loads:
                dst = view(raw, g, kind)
                dst = dst[:, a:a + n] if kind == "row" else dst[:, :, a:a + n]
                sp.dma_start(dst, src).then_inc(landed[stream.slot(g)], 16)

        load(0)
        sp.dma_start(consts[:, P:], const_mats[:, P:]).then_inc(d_const, 16)
        rows = [(P_CONV, gdn_conv_w[0].rearrange("k (t p) -> (k t) p", p=P), 48),
                (P_MU, rwkv_mu[:, 0:1536].rearrange("o (t p) -> (o t) p", p=P), 12),
                (P_W0, rwkv_w0.rearrange("o (t p) -> (o t) p", p=P), 4),
                (P_A0, rwkv_a0.rearrange("o (t p) -> (o t) p", p=P), 4),
                (P_KK, rwkv_k_k.rearrange("o (t p) -> (o t) p", p=P), 4),
                (P_KA, rwkv_k_a.rearrange("o (t p) -> (o t) p", p=P), 4),
                (P_RK, rwkv_r_k[0].rearrange("(t h) d -> t (h d)", h=2), 4)]
        sp.wait_ge(pads_set, 1)
        for r, src, n in rows:
            sp.dma_start(prow[r:r + n, :], src).then_inc(d_par, 16)
        sp.dma_start(prow[P_MUL:P_MUL + 1, 0:64], rwkv_mu[:, 1536:1600]).then_inc(d_par, 16)
        sp.dma_start(prow[P_MUL + 1:P_MUL + 2, 0:96], rwkv_mu[:, 1600:1696]).then_inc(d_par, 16)

        for g in range(1, Stream.SLOTS):
            load(g)
        for dst, src in ((loraw[0:32, :], rwkv_w2[0]), (loraw[32:64, :], rwkv_a2[0])):
            sp.dma_start(dst, src).then_inc(d_lora, 16)
        small_dmas = [(gnw[:, :], gdn_norm[0].partition_broadcast(P)),
                      (gab[:, 0, :], gdn_A_log[0].partition_broadcast(P)),
                      (gab[:, 1, :], gdn_dt_bias[0].partition_broadcast(P)),
                      (possb[:, :], positions[0].rearrange("(t p) -> p t", p=P))]
        for l in range(2):
            small_dmas.append((router[:, l, :, 0:NG], moe_w_group[l].rearrange("(p c) g -> p c g", c=KC)))
            for g in range(NG):
                small_dmas.append((router[:, l, :, NG + 4 * g:NG + 4 * g + 4],
                                   moe_w_expert[l, g].rearrange("(p c) e -> p c e", c=KC)))
        assert len(small_dmas) == SMALL_DMAS
        for g in range(Stream.SLOTS, U_EVO + Stream.SLOTS):
            load(g)
            if small_dmas:
                dst, src = small_dmas.pop(0)
                sp.dma_start(dst, src, allow_slow_non_contiguous=True).then_inc(d_small, 16)
        sp.wait_ge(made, plan.made("m15"))
        for dst, src in ((lnw, rwkv_ln_w[0].partition_broadcast(P).rearrange("p (h n) -> p h n", h=4)),
                         (lnb, rwkv_ln_b[0].partition_broadcast(P).rearrange("p (h n) -> p h n", h=4)),
                         (g2sb, rwkv_g2[0].rearrange("p (h n) -> p h n", h=4))):
            sp.dma_start(dst, src).then_inc(d_late, 16)
        for g in range(U_EVO + Stream.SLOTS, MOE[0]):
            load(g)

        def experts(layer):
            for g in range(MOE[layer], step_unit(layer, 2, 0)):
                load(g)
            with sp.Fori(0, NE - 2) as i:
                for u in range(6):
                    loads = hidden_loads(layer, i + 2, u) if u < 4 else down_load(layer, i + 1, u - 4)
                    load(step_unit(layer, 2, u), loads, i)
            for g in range(step_unit(layer, NE, 0), step_unit(layer, NE, 2)):
                load(g)

        experts(0)
        sp.dma_start(masks, attn_masks).then_inc(d_mask, 16)
        for g in range(U_OD, MOE[1]):
            load(g)
        experts(1)
        sp.dma_start(w_(0, D), final_norm.partition_broadcast(P)).then_inc(d_fin, 16)
        outr = out[0].rearrange("(t p) n -> p t n", p=P)
        for t in range(NT):
            sp.wait_ge(out_ready, t + 1)
            sp.dma_start(outr[:, t, :], hn[:, t, :]).then_inc(d_out, 16)
        sp.wait_ge(d_out, 16 * NT)

    @block.gpsimd
    def _(pool):
        nc.gpsimd.memset(eps6[:, :], 1e-6)
        nc.gpsimd.memset(prow, 0.0).then_inc(pads_set, 1)
        nc.gpsimd.memset(ones[:, :], 1.0).then_inc(ones_set, 1)
        nc.gpsimd.memset(router_flat[:, 2 * KC * (NG + NE):RW], 0.0).then_inc(pads_set, 1)
        nc.gpsimd.memset(rawB[:, :, 0:1], 0.0)
        nc.gpsimd.memset(rawL[:, :, 0:1], 0.0)
        nc.gpsimd.memset(rawA[:, :, 0:3], 0.0).then_inc(pads_set, 1)

        def low_part(g):
            pool.wait_ge(*stream.high(g))
            if g >= Stream.SLOTS:
                pool.wait_ge(*stream.released(g - Stream.SLOTS))
            nc.gpsimd.tensor_tensor(wl[:, stream.slot(g), :], raw[:, stream.slot(g), :],
                                    wh[:, stream.slot(g), :].bitcast(F32), SUB).then_inc(low_pool, 1)

        for g in range(U_EVO + Stream.SLOTS):
            if stream.low_by[g] == "pool":
                low_part(g)
        pool.wait_ge(silu_in, 3)
        nc.gpsimd.memset(w_(0, 6656), 0.0).then_inc(m4_zero, 1)
        pool.wait_ge(made, plan.made("gvt1"))
        nc.gpsimd.memset(w_(6656, 1536), 0.0).then_inc(m4_zero, 1)
        pool.wait_ge(router_split_h, 1)
        nc.gpsimd.tensor_tensor(routerl[:, :], router_flat[:, :], routerh[:, :].bitcast(F32), SUB
                                ).then_inc(router_split, 1)
        steps = [0]

        def step(ins):
            steps[0] += 1
            ins.then_inc(s_pool, 1)
            pool.wait_ge(s_pool, steps[0])

        pool.wait_ge(*plan.emptied("z1"))
        pool.wait_ge(d_small, 16 * SMALL_DMAS)
        pool.wait_ge(*plan.emptied("bon"))
        pool.wait_ge(*plan.emptied("vt1"))
        pool.wait_ge(made, plan.made("m15"))
        pool.wait_ge(d_late, 48)
        for t in range(NT):
            zh = zr[:, t, :].rearrange("p (h n) -> p h n", h=GH)
            step(nc.gpsimd.tensor_tensor(zh, zh, gnw[:, :].unsqueeze(1).broadcast_to([P, GH, GD]), MUL))
            step(nc.gpsimd.tensor_tensor(vb[:, t, :].rearrange("p (h n) -> p h n", h=RH),
                                         vrow[:, t, :].rearrange("p (h n) -> p h n", h=RH),
                                         sm["bonus"][:, 8 * t:8 * t + 8].unsqueeze(2).broadcast_to([P, RH, RD]), MUL))
            vh = vb[:, t, :].rearrange("p (h n) -> p h n", h=4)
            nc.gpsimd.tensor_tensor(vh, vh, lnb, ADD).then_inc(terms_ready, 1)
        for t in range(NT):
            pool.wait_ge(inverse_ready, t + 1)
            o = ycat[:, t, 0:512].rearrange("p (h n) -> p h n", h=GH)
            step(nc.gpsimd.tensor_tensor(o, o, sm["var"][:, 12 * t:12 * t + GH].unsqueeze(2).broadcast_to([P, GH, GD]),
                                         MUL))
            nc.gpsimd.tensor_tensor(ycat[:, t, 0:512], ycat[:, t, 0:512], zr[:, t, :], MUL).then_inc(gated_ready, 1)
        for g in range(U_EVO + Stream.SLOTS, MOE[0] + Stream.SLOTS):
            low_part(g)
        for g in range(U_OD, U_OD + Stream.SLOTS):
            low_part(g)
        pool.wait_ge(made, plan.made("cnt3"))
        nc.gpsimd.memset(qkT[:, 0:12, :], 0.0).then_inc(q_zeros, 1)
        nc.gpsimd.memset(w_(26496, 4 * S), 0.0).then_inc(q_zeros, 1)
        nc.gpsimd.memset(hn[:, :, :], 0.0).then_inc(q_zeros, 1)
        for s in range(6):
            for t in range(NT):
                n = NT * s + t
                pool.wait_ge(rope_ready, n + 1)
                nc.gpsimd.tensor_tensor(qkv[:, t, 512 * s:512 * s + 512], rtmp[:, n % 2, 0, 0:512],
                                        rtmp[:, n % 2, 1, 0:512], ADD).then_inc(roped, 1)
        for g in range(MOE[1], MOE[1] + Stream.SLOTS):
            low_part(g)

    @block.scalar
    def _(act):
        steps = [0]

        def step(ins):
            steps[0] += 1
            ins.then_inc(s_act, 1)
            act.wait_ge(s_act, steps[0])

        def take(name):
            act.wait_ge(made, plan.made(name))
            return psum[:, plan.bank(name), :]

        def load_sqrt():
            step(nc.scalar.activation(sm["unused"], eps6[:, 0:1], ACT.Sqrt))

        def norm_squares(k):
            load_sqrt()
            for t in range(NT):
                act.wait_ge(*((d_x[t], 16) if k == 0 else (x_ready, NT * (k - 1) + t + 1)))
                ssq, rstd = sm["ssq"][:, t:t + 1], sm["rstd"][:, t:t + 1]
                step(nc.scalar.activation(hn[:, t, :], X[:, t, :], ACT.Square, accum_out=ssq))
                nc.scalar.activation(rstd, ssq, ACT.Sqrt, scale=1.0 / D, bias=eps6[:, 0:1]).then_inc(rms_ready, 1)

        split = [0]

        def highs(upto):
            for g in range(split[0], upto):
                high_part(g)
            split[0] = max(split[0], upto)

        def high_part(g, i=None, rounds=(6, 6)):
            s_, v = stream.landed(g)
            act.wait_ge(s_, v if i is None else i * rounds[0] + v)
            if g >= Stream.SLOTS:
                s_, v = stream.released(g - Stream.SLOTS)
                act.wait_ge(s_, v if i is None else i * rounds[1] + v)
            nc.scalar.copy(wh[:, stream.slot(g), :], raw[:, stream.slot(g), :]).then_inc(high, 1)

        def columns_high(tag, k):
            if k == 0:
                act.wait_ge(d_gains, 16 * 4)
            for n in range(4):
                b_ = take(f"{tag}nt{n}")
                for j in range(2):
                    c = 2 * n + j
                    ins = nc.scalar.activation(hTh[:, c, :], b_[:, 256 * j:256 * j + 256], ACT.Copy,
                                               scale=gains[:, k, c:c + 1])
                ins.then_inc(half_done, 1)

        act.wait_ge(ones_set, 1)
        norm_squares(0)
        highs(1)
        columns_high("a", 0)
        highs(Stream.SLOTS)
        act.wait_ge(pads_set, 3)
        b = take("loraA")
        nc.scalar.copy(rawL[0:72, 0, 1:257], b[0:72, 0:256]).then_inc(act_read, 1)
        highs(4)
        b = take("loraB")
        nc.scalar.copy(rawL[0:96, 1, 1:257], b[0:96, 0:256]).then_inc(act_read, 1)
        highs(5)
        b = take("ab")
        nc.scalar.copy(sm["ab"], b[:, 0:16]).then_inc(act_read, 1)

        def raw_tiles(buf, pad, tile, name, last):
            highs(last + 1 + Stream.SLOTS)
            b_ = take(name)
            nc.scalar.copy(buf[:, tile:tile + 2, pad:pad + 256], b_.rearrange("p (t n) -> p t n", t=2)
                           ).then_inc(act_read, 1)

        raw_tiles(rawB, 1, 0, "k0", U_K + 1)
        raw_tiles(rawB, 1, 2, "k1", U_K + 3)
        act.wait_ge(mixl_ready, 2)
        nc.scalar.activation(fe2[0:32, 0, :], fe2[0:32, 0, :], ACT.Tanh).then_inc(lorain_ready, 1)
        nc.scalar.activation(sgate[:, :], fe2[0:96, 1, :], ACT.Sigmoid).then_inc(sgate_ready, 1)
        for k, (name, dst) in enumerate((("wz0", fsg), ("wz1", fsg), ("az0", fal), ("az1", fal))):
            b = take(name)
            for j in range(2):
                t = 2 * (k % 2) + j
                ins = nc.scalar.activation(dst[:, t, :], b[:, 256 * j:256 * j + 256], ACT.Sigmoid,
                                           bias=par[:, P_W0 + 4 * (k // 2) + t:P_W0 + 4 * (k // 2) + t + 1])
            ins.then_inc(act_read, 1)
        act.wait_ge(*plan.emptied("ab"))
        abv = sm["ab"].rearrange("p (c s h) -> p c s h", c=2, s=2)
        nc.scalar.activation(sm["beta"].rearrange("p (c h) -> p c h", c=2), abv[:, :, 1, :],
                             ACT.Sigmoid).then_inc(beta_done, 1)
        raw_tiles(rawB, 1, 4, "r0", U_K + 5)
        raw_tiles(rawB, 1, 6, "r1", U_K + 7)
        highs(U_K + 12)
        for k in range(2):
            b = take(f"ss{k}")
            nc.scalar.activation(ft[:, 2 * k:2 * k + 2, :], b.rearrange("p (t n) -> p t n", t=2), ACT.Ln,
                                 bias=eps6[:, 0:1]).then_inc(act_read, 1)
        raw_tiles(rawB, 1, 8, "v0", U_K + 9)
        raw_tiles(rawB, 1, 10, "v1", U_K + 11)
        act.wait_ge(*plan.emptied("ss1"))
        nc.scalar.activation(ft, ft, ACT.Exp, scale=-0.5).then_inc(kknorm_done, 1)
        act.wait_ge(decay_in, 1)
        nc.scalar.activation(fe2, fd, ACT.Exp, scale=-DECAY).then_inc(decay_out, 1)
        act.wait_ge(decay_out, 1)
        nc.scalar.activation(fd, fd, ACT.Exp, scale=DECAY).then_inc(decay_out, 1)
        nc.scalar.activation(fdx, fdx, ACT.Exp, scale=-DECAY).then_inc(decay_out, 1)
        act.wait_ge(decay_in, 2)
        nc.scalar.activation(sm["fs"], sm["fs"], ACT.Exp, scale=-DECAY).then_inc(decay_out, 1)
        raw_tiles(rawA, 3, 0, "gk0", U_K + 13)
        raw_tiles(rawA, 3, 2, "gk1", U_K + 15)
        raw_tiles(rawA, 3, 4, "gq0", U_K + 17)
        raw_tiles(rawA, 3, 6, "gq1", U_K + 19)
        highs(U_K + 21)
        for t in range(NT):
            b = take(f"vt{t}")
            nc.scalar.copy(vrow[:, t, :], b).then_inc(act_read, 1)
        act.wait_ge(d_small, 16 * SMALL_DMAS)
        nc.scalar.activation(sm["eal"], gab[:, 0, :], ACT.Exp).then_inc(gate_exp, 1)
        act.wait_ge(gate_in, 1)
        nc.scalar.activation(sm["ga"], sm["gg"], ACT.Exp, scale=-1.0).then_inc(gate_exp, 1)
        act.wait_ge(gate_exp, 2)
        nc.scalar.activation(sm["ga"], sm["ga"], ACT.Ln, bias=1.0).then_inc(gate_exp, 1)

        def silu_conv(n):
            act.wait_ge(silu_in, n + 1)
            nc.scalar.activation(conv_out[n], conv_out[n], ACT.Silu).then_inc(conv_silu, 1)

        raw_tiles(rawA, 3, 8, "gv0", U_K + 21)
        silu_conv(0)
        raw_tiles(rawA, 3, 10, "gv1", U_K + 23)
        silu_conv(1)
        highs(U_EVO)
        for m in range(4):
            b = take(f"gss{m}")
            nc.scalar.activation(gtmp[:, 512 * m:512 * m + 512], b, ACT.Ln, bias=eps6[:, 0:1]).then_inc(act_read, 1)
        act.wait_ge(*plan.emptied("gss3"))
        nc.scalar.activation(gtmp, gtmp, ACT.Exp, scale=-0.5).then_inc(kqnorm_done, 1)
        highs(U_EVO + Stream.SLOTS)
        for t in range(NT):
            b = take(f"z{t}")
            nc.scalar.activation(zr[:, t, :], b, ACT.Silu).then_inc(act_read, 1)
        silu_conv(2)
        for s, name in enumerate(("kt0", "bt0")):
            b = take(name)
            nc.scalar.copy(kbT[:, s, :], b).then_inc(act_read, 1)
        act.wait_ge(dt_in, 1)
        nc.scalar.activation(GM[:, :, 1, :], GM[:, :, 1, :], ACT.Exp).then_inc(dt_exp, 1)
        nc.scalar.activation(sm["egc"], sm["gc"], ACT.Exp).then_inc(gc_exp, 1)
        nc.scalar.activation(sm["kd"], sm["kd"], ACT.Exp).then_inc(gc_exp, 1)

        def one_head_of(dst, src, h):
            nc.scalar.activation(dst, src, ACT.Copy, scale=const("heads64")[:, RD * h:RD * h + 1]).then_inc(one_head, 1)
        act.wait_ge(odd_heads, 2)
        one_head_of(Bt, Bt, 0)
        one_head_of(Kt, Kt, 0)
        for t in range(NT):
            b = take(f"gvt{t}")
            nc.scalar.copy(gvrow[:, t, :], b).then_inc(act_read, 1)
        nc.scalar.copy(routerh[:, :], router_flat[:, :]).then_inc(router_split_h, 1)
        for l, g in INV0:
            if l < LEVELS - 1:
                b = take(f"tr_{l}_{g}").rearrange("p (q n) -> p q n", q=4)
                nc.scalar.copy(tinv[:, 4 * g:4 * g + 4, 1, :], b).then_inc(act_read, 1)
        b = take("w0")
        nc.scalar.copy(wsb, b).then_inc(act_read, 1)
        b = take("u0")
        nc.scalar.mul(un, b, -1.0).then_inc(act_read, 1)
        b = take("gs1")
        nc.scalar.copy(state_g.rearrange("p h n -> p (h n)"), b).then_inc(act_read, 1)
        b = take("y0")
        nc.scalar.copy(ycat[:, 0, 512:1024], b).then_inc(act_read, 1)
        b = take("go0")
        nc.scalar.copy(ycat[:, 0, 0:512], b).then_inc(act_read, 1)
        b = take("w1")
        nc.scalar.copy(wsb, b).then_inc(act_read, 1)
        b = take("u1")
        nc.scalar.mul(un, b, -1.0).then_inc(act_read, 1)
        b = take("go1")
        nc.scalar.copy(ycat[:, 1, 0:512], b).then_inc(act_read, 1)

        def deviations(t):
            act.wait_ge(var_ready, t + 1)
            v = sm["var"][:, 12 * t:12 * t + 12]
            nc.scalar.activation(v, v, ACT.Sqrt).then_inc(deviation_ready, 1)

        load_sqrt()
        deviations(0)
        b = take("y1")
        nc.scalar.copy(ycat[:, 1, 512:1024], b).then_inc(act_read, 1)
        deviations(1)
        for n in range(4):
            b = take(f"yt{n}")
            nc.scalar.copy(hTh[:, 2 * n:2 * n + 2, :], b.rearrange("p (c n) -> p c n", c=2)).then_inc(half_done, 1)
        highs(MOE[0])

        def moe(layer):
            act.wait_ge(route_in, 2 * layer + 1)
            nc.scalar.activation(sm["ge"], sm["ge"], ACT.Exp).then_inc(route_exp, 1)
            highs(MOE[layer] + 6)
            act.wait_ge(route_in, 2 * layer + 2)
            nc.scalar.activation(sm["dv"], sm["dv"], ACT.Exp).then_inc(route_exp, 1)

            def hidden_highs(e, us, i=None):
                for u in us:
                    g = step_unit(layer, e, u)
                    high_part(g, i, (2 * LANDED_PER_STEP[u % 3], 2 * RELEASED_PER_STEP[stream.units[g - 3][1]]))

            def silu(e, i=None):
                v = NE * layer + e + 1
                act.wait_ge(h_made, v if i is None else i * 2 + v)
                nc.scalar.activation(moes, psum[:, 4 + 2 * (e % 2):6 + 2 * (e % 2), 0:FF],
                                     ACT.Silu).then_inc(silu_done, 1)

            def transposed_high(e, i=None):
                v = NE * layer + e + 1
                act.wait_ge(gT_made, v if i is None else i * 2 + v)
                if e or layer:
                    act.wait_ge(y_made, v - 1 if i is None else i * 2 + v - 1)
                nc.scalar.copy(moegTh[:, :, :, :].rearrange("p t k n -> p t (k n)"),
                               psum[:, 4 + 2 * (e % 2):6 + 2 * (e % 2), 0:FF]).then_inc(gT_high, 1)

            def act_step(e, i=None):
                hidden_highs(e, range(3) if e > 1 else (2,), i)
                transposed_high(e - 1, i)
                hidden_highs(e, range(3, 6), i)
                silu(e, i)

            silu(0)
            act_step(1)
            with act.Fori(0, NE // 2 - 1) as i:
                act_step(2, i)
                act_step(3, i)
            split[0] = step_unit(layer, NE, 0)
            transposed_high(NE - 1)
            highs(step_unit(layer, NE, 0) + 2)

        norm_squares(1)
        highs(MOE[0] + Stream.SLOTS)
        columns_high("b", 1)
        moe(0)
        norm_squares(2)
        highs(U_OD + Stream.SLOTS)
        columns_high("c", 2)
        act.wait_ge(trig_in, 1)
        nc.scalar.activation(trig[:, 128:256], trig[:, 128:256], ACT.Sin).then_inc(trig_done, 1)

        act.wait_ge(q_zeros, 3)

        def copy_qkT(s, t):
            b = take(f"qt{s}{t}").rearrange("p (j n) -> p j n", j=4)
            tokens = slice(P * t, P * t + P)
            if s >= AG:
                nc.scalar.copy(qkT[:, 4 * s:4 * s + 4, tokens], b).then_inc(act_read, 1)
            else:
                nc.scalar.copy(qkT[0:AD, 4 * s:4 * s + 4, tokens], b[0:AD])
                o = hn[AD:P, s, :] if s < 2 else w_(26496, 4 * S)[AD:P]
                nc.scalar.copy(o.rearrange("p (j n) -> p j n", j=4)[:, :, tokens], b[AD:P]).then_inc(act_read, 1)

        for s in range(9):
            for t in range(NT):
                if t == 0:
                    highs(min(U_OD + 4 * s + 4 + Stream.SLOTS, MOE[1]))
                if s >= 6:
                    b = take(f"s{s}{t}")
                    nc.scalar.copy(qkv[:, t, 512 * s:512 * s + 512], b).then_inc(act_read, 1)
            if 1 <= s <= 6:
                for t in range(NT):
                    copy_qkT(s - 1, t)

        def exponentials(n):
            h, t = HT_[n]
            keys = AG * P * (t + 1)
            act.wait_ge(scores_ready, n + 1)
            if n >= AB:
                act.wait_ge(made, plan.made("pt%d%d%s" % (*HT_[n - AB], "b" if HT_[n - AB][1] else "a")))
                act.wait_ge(rden_ready, n - AB + 1)
            nc.scalar.activation(probs[:, n % AB, 0:keys], scs[:, n % 2, 0:keys], ACT.Exp,
                                 bias=sm["nmx"][:, n % AB:n % AB + 1],
                                 accum_out=sm["den"][:, n % AB:n % AB + 1]).then_inc(probs_ready, 1)

        def transposed_probs(n):
            h, t = HT_[n]
            b_ = take(f"pt{h}{t}a")
            if n >= 2:
                act.wait_ge(made, plan.made("pv%d%d" % HT_[n - 2]))
            w = 384 if t == 0 else 512
            nc.scalar.copy(pT[:, n % 2, 0:w], b_[:, 0:w]).then_inc(act_read, 1)
            if t:
                b_ = take(f"pt{h}{t}b")
                nc.scalar.copy(pT[:, n % 2, 512:768], b_[:, 0:256]).then_inc(act_read, 1)

        for n in range(-2, len(HT_)):
            if n + 2 < len(HT_):
                exponentials(n + 2)
            if 0 <= n + 1 < len(HT_):
                transposed_probs(n + 1)
            if n >= 0:
                h, t = HT_[n]
                b = take(f"pv{h}{t}")
                act.wait_ge(rden_ready, n + 1)
                v = slice(AD * (h % 2), AD * (h % 2) + AD)
                nc.scalar.activation(arow[:, t, AD * h:AD * h + AD], b[:, v], ACT.Copy,
                                     scale=sm["rden"][:, n % AB:n % AB + 1]).then_inc(act_read, 1)
        for n in range(2):
            b = take(f"at{n}")
            nc.scalar.copy(hTh[:, 2 * n:2 * n + 2, :], b.rearrange("p (c n) -> p c n", c=2)).then_inc(half_done, 1)
        highs(MOE[1])
        norm_squares(3)
        highs(MOE[1] + Stream.SLOTS)
        columns_high("d", 3)
        moe(1)
        norm_squares(4)

    @block.tensor
    def _(pe):
        seen = {}

        def fill(name):
            for s_, v in plan.must_be_empty(name):
                if v > seen.get(id(s_), 0):
                    seen[id(s_)] = v
                    pe.wait_ge(s_, v)
            return psum[:, plan.bank(name), :]

        def mm(out_, lhsT, rhs, start=True, stop=True, shared=False):
            return nc.tensor.matmul(out_, lhsT, rhs, start=start, stop=stop, skip_group_check=shared)

        def norm_columns(tag, k):
            banks = [fill(f"{tag}nt{n}") for n in range(4)]
            for t in range(NT):
                pe.wait_ge(hn_ready, NT * k + t + 1)
                for c in range(KC):
                    at_ = 256 * (c % 2) + P * t
                    ins = nc.tensor.transpose(banks[c // 2][:, at_:at_ + P], hn[:, t, P * c:P * c + P], ident)
                    if t == NT - 1 and c % 2:
                        ins.then_inc(made, 1)

        def unit(g, i=None):
            s_, v = stream.low(g)
            pe.wait_ge(s_, v if i is None else i * 12 + v)

        def mm3(out_, lh, ll, rh, rl, start, stop, shared=False):
            mm(out_, lh, rh, start, False, shared)
            mm(out_, lh, rl, False, False, shared)
            return mm(out_, ll, rh, False, stop, shared)

        def columns_there(tag, c):
            if tag and c % 2 == 0:
                pe.wait_ge(*plan.emptied(f"{tag}nt{c // 2}"))

        def column_tile(out_, g, tag=None):
            unit(g)
            h_, l_ = view(wh, g, "cols"), view(wl, g, "cols")
            for c in range(KC):
                columns_there(tag, c)
                ins_ = mm3(out_, h_[:, c, :], l_[:, c, :], hTh[:, c, :], hTl[:, c, :], c == 0, c == KC - 1)
            return ins_

        def col_pair(name, g):
            b_ = fill(name)
            column_tile(b_[:, 0:256], g).then_inc(used, 1)
            column_tile(b_[:, 256:512], g + 1).then_inc(made, 1)

        def row_strip(names, g, tag=None, between=None):
            banks = [fill(name) for name in names]
            for j in range(4):
                if j == 2 and between:
                    between()
                unit(g + j)
                columns_there(tag, 2 * j)
                h_, l_ = view(wh, g + j, "chunks"), view(wl, g + j, "chunks")
                for t in range(NT):
                    v_ = slice(P * t, P * t + P)
                    for c in range(2):
                        k = 2 * j + c
                        ins_ = mm3(banks[t], hTh[:, k, v_], hTl[:, k, v_], h_[:, c, :], l_[:, c, :], k == 0,
                                   k == KC - 1)
                    if j == 3:
                        ins_.then_inc(made, 1)
                if j < 3:
                    ins_.then_inc(used, 1)

        def row_block(names, g, n, columns):
            banks = [fill(name) for name in names]
            for c in range(n):
                unit(g + c)
                if c % 2 == 0:
                    pe.wait_ge(*plan.emptied(f"{columns}{c // 2}"))
                h_, l_ = view(wh, g + c, "row"), view(wl, g + c, "row")
                for t in range(NT):
                    v_ = slice(P * t, P * t + P)
                    for half in range(2):
                        w = slice(512 * half, 512 * half + 512)
                        ins_ = mm3(banks[2 * t + half], hTh[:, c, v_], hTl[:, c, v_], h_[:, w], l_[:, w], c == 0,
                                   c == n - 1)
                        if c == n - 1:
                            ins_.then_inc(made, 1)
                if c < n - 1:
                    ins_.then_inc(used, 1)

        pe.wait_ge(d_ident, 16)
        norm_columns("a", 0)
        b = fill("loraA")
        column_tile(b[:, 0:256], 0, "a").then_inc(made, 1)
        b = fill("loraB")
        column_tile(b[:, 0:256], 1).then_inc(made, 1)
        pe.wait_ge(d_par, 16 * 9)
        b = fill("params")
        nc.tensor.transpose(b[:, 0:P], prow[:, :], ident).then_inc(made, 1)
        pe.wait_ge(*plan.emptied("loraA"))
        b = fill("ab")
        for t in range(NT):
            ins = nc.tensor.transpose(b[:, 8 * t:8 * t + 8], rawL[64:72, 0, 1 + P * t:1 + P * t + P],
                                      ident[64:72, 64:72])
        ins.then_inc(made, 1)
        pe.wait_ge(d_const, 16)
        col_pair("k0", U_K)
        col_pair("k1", U_K + 2)
        pe.wait_ge(d_lora, 32)
        pe.wait_ge(lorain_ready, 1)
        for name, lo, hi in (("wz", 0, 32), ("az", 32, 64)):
            for k in range(2):
                b = fill(f"{name}{k}")
                for j in range(2):
                    c0 = P * (2 * k + j)
                    ins = mm(b[:, 256 * j:256 * j + 256], loraw[lo:hi, c0:c0 + P], fe2[lo:hi, 0, :])
                ins.then_inc(made, 1)
        col_pair("r0", U_K + 4)
        col_pair("r1", U_K + 6)
        pe.wait_ge(kksq_ready, 1)
        for k in range(2):
            b = fill(f"ss{k}")
            for j in range(2):
                ins = mm(b[:, 256 * j:256 * j + 256], const("heads64"), ft[:, 2 * k + j, :])
            ins.then_inc(made, 1)
        col_pair("v0", U_K + 8)
        col_pair("v1", U_K + 10)
        col_pair("gk0", U_K + 12)
        col_pair("gk1", U_K + 14)
        col_pair("gq0", U_K + 16)
        col_pair("gq1", U_K + 18)

        def four_transposes(name, of):
            b_ = fill(name)
            for j in range(4):
                ins_ = nc.tensor.transpose(b_[:, P * j:P * j + P], of(j), ident)
            ins_.then_inc(made, 1)

        pe.wait_ge(fv_ready, 1)
        for t in range(NT):
            four_transposes(f"vt{t}", lambda j: fv[:, j, P * t:P * t + P])
        col_pair("gv0", U_K + 20)
        col_pair("gv1", U_K + 22)
        pe.wait_ge(rkr_ready, 1)
        b = fill("bon")
        for t in range(NT):
            for j in range(RT):
                ins = mm(b[:, 8 * t + 2 * j:8 * t + 2 * j + 2], fr[:, j, P * t:P * t + P],
                         const("heads64")[:, 0:P:RD])
        ins.then_inc(made, 1)


        def feature_sums():
            pe.wait_ge(gsq_ready, 1)
            for m in range(4):
                b = fill(f"gss{m}")
                mm(b, ones[:, :], gtmp[:, 512 * m:512 * m + 512]).then_inc(made, 1)

        pe.wait_ge(ones_set, 1)
        row_strip(("z0", "z1"), U_Z, between=feature_sums)
        pe.wait_ge(cols_ready, 1)
        four_transposes("kt0", lambda j: Kt[:, j, 0:P])
        four_transposes("bt0", lambda j: Bt[:, j, 0:P])
        pe.wait_ge(ones_set, 1)
        pe.wait_ge(g_ready, 1)
        b = fill("gc")
        mm(b[:, 0:8], const("incl"), sm["gx"])
        mm(b[:, 8:16], ones[:, :], sm["gx"]).then_inc(made, 1)
        pe.wait_ge(ug_ready, 1)
        for m in range(2):
            b = fill(f"gb{m}")
            mm(b, ones[:, :], UG[:, 4 * m:4 * m + 4, :]).then_inc(made, 1)
        pe.wait_ge(conv_silu, 3)
        for t in range(NT):
            four_transposes(f"gvt{t}", lambda j: convv[:, j, P * t:P * t + P])
        pe.wait_ge(kq_ready, 1)
        four_transposes("gkt", lambda j: KQ[:, j, 0, 0, :])
        for n in range(4):
            b = fill(f"ga{n}")
            for j in range(2):
                q = 2 * n + j
                c, h = q // GH, q % GH
                ins = mm(b[:, 256 * j:256 * j + 256], KQ[:, h, c, 0, :], KQ[:, h, c, :, :])
            ins.then_inc(made, 1)
        def lt(q):
            return m4[:, q, 0:P] if q < 16 else GM[:, q - 16, 0, :]

        def rwkv_products(q):
            c, h = q // RH, q % RH
            j, v_ = h // 2, slice(P * c, P * c + P)
            b_ = fill(f"m{q}")
            mm(b_[:, 0:256], (Bt, Bt_odd)[h % 2][:, j, v_], AR[:, j, c, :, :])
            mm(b_[:, 256:512], (Kt, Kt_odd)[h % 2][:, j, v_], AR[:, j, c, :, :]).then_inc(made, 1)

        def first_level(k):
            pe.wait_ge(*plan.emptied(f"m{2 * k + 1}" if k < 8 else "ga3"))
            b_ = fill(f"i0_{k}")
            for j in range(2):
                q = 2 * k + j
                mm(b_[:, 256 * j:256 * j + P], lt(q), const("neg"))
                ins_ = mm(b_[:, 256 * j + P:256 * j + 256], const("neg"), lt(q))
            ins_.then_inc(made, 1)

        for kind, q in FORM:
            if kind == "m":
                if q == 0:
                    pe.wait_ge(one_head, 2)
                rwkv_products(q)
            else:
                first_level(q)

        def inv1(n):
            l, g = INV0[n]
            pe.wait_ge(*plan.emptied(f"i2_{l - 1}_{g}" if l > 1 else f"i0_{2 * g + 1}"))
            b_ = fill(f"i1_{l}_{g}")
            for j in range(4):
                q = 4 * g + j
                ins_ = mm(b_[:, P * j:P * j + P], lt(q), tinv[:, q, 0, :])
            ins_.then_inc(made, 1)

        inv1(0)
        for n, (l, g) in enumerate(INV0):
            if n + 1 < len(INV0):
                inv1(n + 1)
            pe.wait_ge(*plan.emptied(f"i1_{l}_{g}"))
            if l > 1:
                pe.wait_ge(*plan.emptied(f"tr_{l - 1}_{g}"))
            b = fill(f"i2_{l}_{g}")
            for j in range(4):
                gm, ttr = Gb[:, n % 3, P * j:P * j + P], tinv[:, 4 * g + j, 1, :]
                ins = mm(b[:, P * j:P * j + P], *((ttr, gm) if l < LEVELS - 1 else (gm, ttr)))
            ins.then_inc(made, 1)
            if n and INV0[n - 1][0] < LEVELS - 1:
                l1, g1 = INV0[n - 1]
                pe.wait_ge(*plan.emptied(f"i2_{l1}_{g1}"))
                four_transposes(f"tr_{l1}_{g1}", lambda j: tinv[:, 4 * g1 + j, 0, :])

        pe.wait_ge(*plan.emptied(f"i2_{LEVELS - 1}_5"))

        def hcol(h):
            return slice(RD * h, RD * h + RD)

        def rw_w(c):
            b_ = fill(f"w{c}")
            if c:
                pe.wait_ge(*plan.emptied("st"))
            for h in range(RH):
                if c and h % 2 == 0:
                    mm(b_[:, P * (h // 2):P * (h // 2) + P], AR[:, h // 2, 1, 0, :], state_r[:, h // 2, :], True, False,
                       True)
                ins_ = mm(b_[:, hcol(h)], m4[:, 8 * c + h, 256:384], vrow[:, c, hcol(h)], c == 0, True, c == 1)
            ins_.then_inc(made, 1)

        def rw_u(c):
            pe.wait_ge(*plan.emptied(f"w{c}"))
            b_ = fill(f"u{c}")
            for h in range(RH):
                ins_ = mm(b_[:, hcol(h)], tinv[:, 8 * c + h, 1, :], wsb[:, hcol(h)])
            ins_.then_inc(made, 1)

        def rw_y(c):
            b_ = fill(f"y{c}")
            pe.wait_ge(*plan.emptied(f"u{c}"))
            for h in range(RH):
                if c and h % 2 == 0:
                    mm(b_[:, P * (h // 2):P * (h // 2) + P], AR[:, h // 2, 1, 1, :], state_r[:, h // 2, :], True, False,
                       True)
                mm(b_[:, hcol(h)], m4[:, 8 * c + h, 384:512], vrow[:, c, hcol(h)], c == 0, False, c == 1)
                ins_ = mm(b_[:, hcol(h)], m4[:, 8 * c + h, 128:256], un[:, hcol(h)], False, True, c == 1)
            ins_.then_inc(made, 1)

        def gcol(h):
            return slice(GD * h, GD * h + GD)

        def gd(name, lhs, rhs):
            b_ = fill(name)
            for h in range(GH):
                ins_ = mm(b_[:, gcol(h)], lhs(h), rhs(h))
            ins_.then_inc(made, 1)

        rw_w(0)
        gd("gz0", lambda h: tinv[:, 16 + h, 1, :], lambda h: gvrow[:, 0, gcol(h)])
        rw_u(0)
        pe.wait_ge(*plan.emptied("gz0"))
        gd("gs1", lambda h: kdec[:, gcol(h)], lambda h: vnew[:, gcol(h)])
        b = fill("st")
        pe.wait_ge(*plan.emptied("u0"))
        for j in range(RT):
            mm(b[:, P * j:P * j + P], kbT[:, 0, P * j:P * j + P], vrow[:, 0, P * j:P * j + P], True, False)
            ins = mm(b[:, P * j:P * j + P], kbT[:, 1, P * j:P * j + P], un[:, P * j:P * j + P], False, True)
        ins.then_inc(made, 1)
        rw_y(0)
        pe.wait_ge(*plan.emptied("gs1"))
        gd("gp1", lambda h: KQ[:, h, 1, 0, :], lambda h: state_g[:, h, :])
        gd("go0", lambda h: GM[:, h, 1, :], lambda h: vnew[:, gcol(h)])
        rw_w(1)
        pe.wait_ge(r1_ready, 1)
        gd("gz1", lambda h: tinv[:, 20 + h, 1, :], lambda h: r1[:, gcol(h)])
        rw_u(1)
        pe.wait_ge(*plan.emptied("gz1"))
        gd("go1", lambda h: GM[:, 4 + h, 1, :], lambda h: vnew[:, gcol(h)])
        gd("gos", lambda h: KQ[:, h, 1, 1, :], lambda h: state_g[:, h, :])
        rw_y(1)
        pe.wait_ge(sgate_ready, 1)
        pe.wait_ge(d_late, 48)
        for t in range(NT):
            b = fill(f"lg{t}")
            mm(b, sgate[:, P * t:P * t + P], g2sb).then_inc(made, 1)
        banks = [fill(f"yt{n}") for n in range(4)]
        for t in range(NT):
            pe.wait_ge(ycat_ready, t + 1)
            pe.wait_ge(gated_ready, t + 1)
            for c in range(KC):
                at_ = 256 * (c % 2) + P * t
                ins = nc.tensor.transpose(banks[c // 2][:, at_:at_ + P], ycat[:, t, P * c:P * c + P], ident)
                if t == NT - 1 and c % 2:
                    ins.then_inc(made, 1)
        row_block([f"op{t}{half}" for t in range(NT) for half in range(2)], U_EVO, KC, "yt")

        def router_logits(tag, layer):
            pe.wait_ge(router_split, 1)
            b_ = fill(f"{tag}rt")[:, 0:S]
            for c in range(KC):
                columns_there(tag, c)
                v_ = slice((NG + NE) * (KC * layer + c), (NG + NE) * (KC * layer + c) + P)
                ins_ = mm3(b_, routerh[:, v_], routerl[:, v_], hTh[:, c, :], hTl[:, c, :], c == 0, c == KC - 1)
            ins_.then_inc(made, 1)

        def router_rows(tag):
            pe.wait_ge(*plan.emptied(f"{tag}rt"))
            b_ = fill(f"{tag}rl")
            for t in range(NT):
                ins_ = nc.tensor.transpose(b_[:, 20 * t:20 * t + 20], logitsT[:, P * t:P * t + P],
                                           ident[0:NG + NE, 0:NG + NE])
            ins_.then_inc(made, 1)

        def moe(tag, layer):

            def hidden(e, us, i=None):
                for u in us:
                    g = step_unit(layer, e, u) if e else MOE[layer] + u
                    unit(g, i)
                    if u == 0 and e >= 2:
                        v = NE * layer + e - 1
                        pe.wait_ge(gT_low, v if i is None else i * 2 + v)
                    h_, l_ = view(wh, g, "chunks"), view(wl, g, "chunks")
                    for t in range(NT):
                        v_ = slice(P * t, P * t + P)
                        for c in range(2):
                            k = 2 * u + c
                            ins_ = mm3(psum[:, 4 + 2 * (e % 2) + t, :], hTh[:, k, v_], hTl[:, k, v_], h_[:, c, :],
                                       l_[:, c, :], k == 0, k == KC - 1)
                    ins_.then_inc(h_made if u == 3 else used, 1)

            def gated_transposes(e, i=None):
                v = NE * layer + e + 1
                pe.wait_ge(g_made, v if i is None else i * 2 + v)
                for t in range(NT):
                    for k in range(2):
                        ins_ = nc.tensor.transpose(psum[:, 4 + 2 * (e % 2) + t, P * k:P * k + P],
                                                   moeg[:, t, P * k:P * k + P], ident)
                ins_.then_inc(gT_made, 1)

            def down(e, i=None):
                v = NE * layer + e + 1
                pe.wait_ge(gT_low, v if i is None else i * 2 + v)
                for k in range(2):
                    g = step_unit(layer, e + 1, 4 + k)
                    unit(g, i)
                    h_, l_ = view(wh, g, "row"), view(wl, g, "row")
                    for t in range(NT):
                        ins_ = down_tile(t, k, h_, l_, i is None and e == 0 and k == 0)
                    ins_.then_inc(y_made if k else used, 1)

            def down_tile(t, k, h_, l_, start):
                for half in range(2):
                    w = slice(512 * half, 512 * half + 512)
                    ins_ = mm3(psum[:, 2 * t + half, :], moegTh[:, t, k, :], moegTl[:, t, k, :], h_[:, w], l_[:, w],
                               start, False, True)
                return ins_

            def last_down():
                pe.wait_ge(gT_low, NE * (layer + 1))
                for k in range(2):
                    unit(step_unit(layer, NE, k))
                for t in range(NT):
                    for k in range(2):
                        g = step_unit(layer, NE, k)
                        ins_ = down_tile(t, k, view(wh, g, "row"), view(wl, g, "row"), False)
                        if t == 0 and k == 1:
                            ins_.then_inc(first_sums, 1)
                        elif t:
                            ins_.then_inc(y_made if k else used, 1)

            def pe_step(e, i=None):
                hidden(e, range(2), i)
                gated_transposes(e - 1, i)
                hidden(e, range(2, 4), i)
                down(e - 1, i)

            router_logits(tag, layer)
            hidden(0, range(2))
            router_rows(tag)
            hidden(0, range(2, 4))
            pe.wait_ge(*plan.emptied(f"{tag}rl"))
            pe_step(1)
            with pe.Fori(0, NE // 2 - 1) as i:
                pe_step(2, i)
                pe_step(3, i)
            gated_transposes(NE - 1)
            last_down()

        norm_columns("b", 1)
        moe("b", 0)
        norm_columns("c", 2)

        def qk_transposes(s, t):
            pe.wait_ge(roped, NT * s + t + 1)
            four_transposes(f"qt{s}{t}", lambda j: qkv[:, t, 512 * s + P * j:512 * s + P * j + P])

        for s in range(9):
            row_strip((f"s{s}0", f"s{s}1"), U_OD + 4 * s, None if s else "c")
            if 1 <= s <= 6:
                for t in range(NT):
                    qk_transposes(s - 1, t)

        def scores(h, t):
            nk = P * (t + 1)
            j = h // 2
            b_ = fill(f"sc{h}{t}a")
            for g in range(AG):
                if t and g == 2:
                    b_ = fill(f"sc{h}{t}b")
                at_ = nk * g if not (t and g == 2) else 0
                q_ = q_odd[4 * g + j] if h % 2 else qkT[:, 4 * g + j, :]
                ins_ = mm(b_[:, at_:at_ + nk], q_[:, P * t:P * t + P], qkT[:, 12 + 4 * g + j, 0:nk])
                if g == 2 or (t and g == 1):
                    ins_.then_inc(made, 1)

        pe.wait_ge(*plan.emptied("qt51"))
        pe.wait_ge(*plan.emptied("s81"))

        def prob_transposes(n):
            h, t = HT_[n]
            pe.wait_ge(probs_ready, n + 1)
            b_ = fill(f"pt{h}{t}a")
            for j in range(AG * (t + 1)):
                if j == 4:
                    b_ = fill(f"pt{h}{t}b")
                ins_ = nc.tensor.transpose(b_[:, P * (j % 4):P * (j % 4) + P], probs[:, n % AB, P * j:P * j + P], ident)
                if j in ((2,) if t == 0 else (3, 5)):
                    ins_.then_inc(made, 1)

        for n in range(-AB, len(HT_)):
            if n + AB < len(HT_):
                scores(*HT_[n + AB])
            if 0 <= n + 1 < len(HT_):
                prob_transposes(n + 1)
            if n >= 0:
                h, t = HT_[n]
                pe.wait_ge(*plan.emptied(f"pt{h}{t}{'b' if t else 'a'}"))
                b = fill(f"pv{h}{t}")
                for j in range(AG * (t + 1)):
                    g, kt = j // (t + 1), j % (t + 1)
                    c0 = 3072 + 512 * g + P * (h // 2)
                    ins = mm(b[:, 0:P], pT[:, n % 2, P * j:P * j + P], qkv[:, kt, c0:c0 + P], j == 0,
                             j == AG * (t + 1) - 1)
                ins.then_inc(made, 1)
        pe.wait_ge(*plan.emptied("pv71"))
        for n in range(2):
            b = fill(f"at{n}")
            for j in range(2):
                for t in range(NT):
                    c = 2 * n + j
                    ins = nc.tensor.transpose(b[:, 256 * j + P * t:256 * j + P * t + P],
                                              arow[:, t, P * c:P * c + P], ident)
            ins.then_inc(made, 1)
        row_block([f"ao{t}{half}" for t in range(NT) for half in range(2)], U_ODO, 4, "at")
        norm_columns("d", 3)
        moe("d", 1)

    @block.vector
    def _(dve):
        counts = {}

        def then(ins, s_=None):
            s_ = s_ or s_dve
            counts[id(s_)] = counts.get(id(s_), 0) + 1
            ins.then_inc(s_, 1)
            dve.wait_ge(s_, counts[id(s_)])

        V = nc.vector

        def take(name):
            dve.wait_ge(made, plan.made(name))
            return psum[:, plan.bank(name), :]

        def tt(o, a, b_, op, s_=None):
            then(V.tensor_tensor(o, a, b_, op), s_)

        def ts(o, a, s1, s2, op0, op1=None, s_=None):
            if op1 is None:
                then(V.tensor_scalar(o, a, s1, None, op0), s_)
            else:
                then(V.tensor_scalar(o, a, s1, s2, op0, op1), s_)

        def stt(o, a, s1, b_, op0, op1, s_=None):
            then(V.scalar_tensor_tensor(out=o, in0=a, scalar=s1, in1=b_, op0=op0, op1=op1), s_)

        def reduce(o, a, op, s_=None):
            then(V.tensor_reduce(o, a, AX.X, op), s_)

        halves = [0]

        def rms_rows(tag, k):
            for t in range(NT):
                dve.wait_ge(rms_ready, NT * k + t + 1)
                then(V.reciprocal(sm["rstd"][:, t:t + 1], sm["rstd"][:, t:t + 1]))
                ts(hn[:, t, :].rearrange("q (c p) -> q p c", c=KC), X[:, t, :].rearrange("q (p c) -> q p c", c=KC),
                   sm["rstd"][:, t:t + 1], None, MUL, s_=hn_ready)
            if tag == "a":
                low_part(0)
            for n in range(4):
                b_ = take(f"{tag}nt{n}")
                halves[0] += 1
                dve.wait_ge(half_done, halves[0])
                for j in range(2):
                    c = 2 * n + j
                    ins = V.scalar_tensor_tensor(out=hTl[:, c, :], in0=b_[:, 256 * j:256 * j + 256],
                                                 scalar=gains[:, k, c:c + 1], in1=hTh[:, c, :].bitcast(F32),
                                                 op0=MUL, op1=SUB)
                then(ins, dve_read)

        def columns_low_of(names):
            for n, name in enumerate(names):
                b_ = take(name)
                halves[0] += 1
                dve.wait_ge(half_done, halves[0])
                v_ = hTh[:, 2 * n:2 * n + 2, :].bitcast(F32)
                then(V.tensor_tensor(hTl[:, 2 * n:2 * n + 2, :], b_.rearrange("p (c n) -> p c n", c=2), v_, SUB),
                     dve_read)

        split = [MOE[0]]

        def low_part(g, i=None):
            s_, v = stream.high(g)
            dve.wait_ge(s_, v if i is None else i * 12 + v)
            V.tensor_tensor(wl[:, stream.slot(g), :], raw[:, stream.slot(g), :],
                            wh[:, stream.slot(g), :].bitcast(F32), SUB).then_inc(low_dve, 1)

        def lows(upto):
            for g in range(split[0], upto):
                if stream.low_by[g] == "dve":
                    low_part(g)
            split[0] = max(split[0], upto)

        rms_rows("a", 0)
        low_part(1)
        b = take("params")
        then(V.tensor_copy(par[:, :], b[:, 0:P_ROWS]), dve_read)
        ts(omka[:, :], par[:, P_KA:P_KA + RT], -1.0, 1.0, MUL, ADD)

        dve.wait_ge(*plan.emptied("loraB"))
        for j, w in ((0, 64), (1, 96)):
            tt(ft[0:w, j, :], rawL[0:w, j, 0:256], rawL[0:w, j, 1:257], SUB)
            stt(fe2[0:w, j, :], ft[0:w, j, :], par[0:w, P_MUL + j:P_MUL + j + 1], rawL[0:w, j, 1:257], MUL, ADD,
                s_=mixl_ready)

        def shift(n, name, dst, mu):
            dve.wait_ge(*plan.emptied(name))
            r_ = rawB[:, 4 * n:4 * n + 4, :]
            tt(ft if n == 0 else fshift, r_[:, :, 0:256], r_[:, :, 1:257], SUB)
            for j in range(4):
                stt(dst[:, j, :], (ft if n == 0 else fshift)[:, j, :], par[:, P_MU + mu + j:P_MU + mu + j + 1],
                    r_[:, j, 1:257], MUL, ADD, s_=fv_ready if name == "v1" and j == 3 else None)

        shift(0, "k1", fk, 4)
        for j in range(RT):
            ts(fkk[:, j, :], fk[:, j, :], par[:, P_KK + j:P_KK + j + 1], None, MUL)
        tt(ft, fkk, fkk, MUL, s_=kksq_ready)
        dve.wait_ge(*plan.emptied("az1"))
        for j in range(RT):
            for c in range(2):
                v = slice(CH * c, CH * c + CH)
                then(V.tensor_tensor_scan(fdx[:, j, v], ones[:, :], fsg[:, j, v], 0.0, MUL, ADD))
        mid = fdx.rearrange("p t (c n) -> p t c n", c=2)
        fsv = sm["fs"].rearrange("p (t o) -> p t o", o=1)
        tt(fsv, mid[:, :, 0, CH - 1:CH], mid[:, :, 0, CH // 2:CH // 2 + 1], SUB)
        tt(fsv, fsv, mid[:, :, 1, CH // 2:CH // 2 + 1], ADD)
        tt(fd.rearrange("p t (c n) -> p t c n", c=2), mid,
           mid[:, :, :, CH // 2:CH // 2 + 1].broadcast_to([P, RT, 2, CH]), SUB)
        tt(fdx, fd, fsg, SUB, s_=decay_in)
        then(V.memset(sm["mark"], 0.0), decay_in)
        shift(1, "r1", fr, 0)
        shift(2, "v1", fv, 8)
        dve.wait_ge(kknorm_done, 1)
        tt(fkk, fkk, ft, MUL)
        tt(ft, fkk, fal, MUL)
        for j in range(RT):
            ts(fal[:, j, :], fal[:, j, :], par[:, P_KA + j:P_KA + j + 1], omka[:, j:j + 1], MUL, ADD)
        tt(fk, fk, fal, MUL)
        dve.wait_ge(decay_out, 3)
        tt(Bt, ft, fd, MUL)
        tt(Kt, fk, fd, MUL)

        def chunks(m):
            return m.rearrange("p t (c n) -> p t c n", c=2)

        tt(AR[:, :, :, 0, :], chunks(fkk), chunks(fdx), MUL)
        tt(AR[:, :, :, 1, :], chunks(fr), chunks(fe2), MUL, s_=cols_ready)
        tt(fr, fr, fk, MUL)
        for j in range(RT):
            ts(fr[:, j, :], fr[:, j, :], par[:, P_RK + j:P_RK + j + 1], None, MUL,
               s_=rkr_ready if j == RT - 1 else None)

        def convolve(n, name, tile0):
            dve.wait_ge(*plan.emptied(name))
            for j in range(4):
                o = conv_out[n][:, j]
                for i in range(CONV):
                    tap = rawA[:, 4 * n + j, i:i + 256].rearrange("p (c n) -> p c n", c=2)
                    wt = par[:, P_CONV + 12 * i + tile0 + j:P_CONV + 12 * i + tile0 + j + 1]
                    last = i == CONV - 1 and j == 3
                    if i == 0:
                        ts(o, tap, wt, None, MUL)
                    else:
                        stt(o, tap, wt, o, MUL, ADD, s_=silu_in if last else None)

        abv = sm["ab"].rearrange("p (c s h) -> p c s h", c=2, s=2)

        def ch(m):
            return m.rearrange("p (c h) -> p c h", c=2)

        dve.wait_ge(d_small, 16 * SMALL_DMAS)
        tt(ch(sm["gx"]), abv[:, :, 0, :], gab[:, 1, :].unsqueeze(1).broadcast_to([P, 2, GH]), ADD)
        stt(sm["gg"], sm["gx"], -1.0, sm["gx"], MUL, MAX, s_=gate_in)
        ts(sm["gx"], sm["gx"], 0.0, None, MAX)
        then(V.tensor_copy(tinv4[:, 16:48], ident.unsqueeze(1).broadcast_to([P, 32, P])))
        convolve(0, "gk1", 4)
        convolve(1, "gq1", 0)
        dve.wait_ge(gate_exp, 3)
        tt(sm["gx"], sm["gx"], sm["ga"], ADD)
        stt(ch(sm["gx"]), ch(sm["gx"]), -1.0, sm["eal"].unsqueeze(1).broadcast_to([P, 2, GH]), MUL, MUL, s_=g_ready)
        dve.wait_ge(made, plan.made("vt1"))
        tt(UG, const("incl").unsqueeze(1).broadcast_to([P, 8, P]), sm["gx"].unsqueeze(2).broadcast_to([P, 8, P]), MUL,
           s_=ug_ready)
        kqf = w_(18432, 2048)
        dve.wait_ge(conv_silu, 2)
        tt(gtmp, kqf, kqf, MUL, s_=gsq_ready)
        b = take("bon")
        then(V.tensor_copy(sm["bonus"], b[:, 0:16]), dve_read)
        then(V.tensor_copy(tinv4[:, 0:16], ident.unsqueeze(1).broadcast_to([P, 16, P])))
        convolve(2, "gv1", 8)
        dve.wait_ge(kqnorm_done, 1)
        inv = gtmp.rearrange("p (h c s n) -> p h c s n", h=GH, c=2, s=2)
        tt(KQ[:, :, :, 0, :], KQ[:, :, :, 0, :], inv[:, :, :, 0, :], MUL)
        stt(KQ[:, :, :, 1, :], KQ[:, :, :, 1, :], float(GD) ** -0.5, inv[:, :, :, 1, :], MUL, MUL, s_=kq_ready)
        b = take("gc")
        then(V.tensor_copy(sm["gc2"], b[:, 0:16]), dve_read)
        tt(sm["kd"], sm["glast"], sm["gc"], SUB)
        for m in range(2):
            b = take(f"gb{m}").rearrange("p (q n) -> p q n", q=4)
            o = GM[:, 4 * m:4 * m + 4, 1, :]
            tt(o, b, sm["gc"][:, 4 * m:4 * m + 4].unsqueeze(2).broadcast_to([P, 4, P]), SUB, s_=dve_read)
            tt(o, o, const("far").unsqueeze(1).broadcast_to([P, 4, P]), ADD, s_=dt_in if m else None)
        for dst, src in ((Bt_odd, Bt), (Kt_odd, Kt)):
            ts(dst, src, const("heads64")[:, RD:RD + 1], None, MUL, s_=odd_heads)
        dve.wait_ge(dt_exp, 1)
        for q in range(8):
            stt(GM[:, q, 0, :], GM[:, q, 1, :], sm["beta"][:, q:q + 1], const("strict"), MUL, MUL)
        dve.wait_ge(gc_exp, 2)
        b = take("gkt")
        tt(kdec.rearrange("p (h n) -> p h n", h=GH), b.rearrange("p (h n) -> p h n", h=GH),
           sm["kd"][:, 0:4].unsqueeze(2).broadcast_to([P, GH, GD]), MUL, s_=dve_read)
        for n in range(4):
            b = take(f"ga{n}")
            gmv = GM[:, 2 * n:2 * n + 2, :, :].rearrange("p q s n -> p (q s n)")
            tt(gmv, gmv, b, MUL, s_=dve_read)
        dve.wait_ge(m4_zero, 2)
        a0 = CP["strict"][0]
        assert CP["incl"][0] == a0 + P
        causal2 = consts[:, a0:a0 + 2 * P].bitcast(U32).unsqueeze(1).broadcast_to([P, 2, 2 * P])
        a0 = CP["level0"][0]
        assert CP["level0t"][0] == a0 + P
        pairs2 = consts[:, a0:a0 + 2 * P].bitcast(U32).unsqueeze(1).broadcast_to([P, 2, 2 * P])
        for kind, q in FORM:
            if kind == "m":
                b = take(f"m{q}")
                o, mask_ = m4[:, q, :].rearrange("p (s n) -> p s n", s=2), causal2
            else:
                b = take(f"i0_{q}")
                o, mask_ = tinv[:, 2 * q:2 * q + 2, :, :].rearrange("p q s n -> p q (s n)"), pairs2
            then(V.copy_predicated(o, mask_, b.rearrange("p (s n) -> p s n", s=2)), dve_read)

        def masked_product(n):
            l, g = INV0[n]
            b_ = take(f"i1_{l}_{g}").rearrange("p (q n) -> p q n", q=4)
            tt(Gb[:, n % 3, :].rearrange("p (q n) -> p q n", q=4), b_,
               const(f"level{l}").unsqueeze(1).broadcast_to([P, 4, P]), MUL, s_=dve_read)

        masked_product(0)
        for n, (l, g) in enumerate(INV0):
            if n + 1 < len(INV0):
                masked_product(n + 1)
            b = take(f"i2_{l}_{g}").rearrange("p (q n) -> p q n", q=4)
            o = tinv[:, 4 * g:4 * g + 4, 0 if l < LEVELS - 1 else 1, :]
            tt(o, o, b, SUB, s_=dve_read)

        def h4(m):
            return m.rearrange("p (h n) -> p h n", h=GH)

        def per_head(m, c):
            return m[:, 4 * c:4 * c + 4].unsqueeze(2).broadcast_to([P, GH, GD])

        b = take("gz0")
        tt(h4(vnew), h4(b), per_head(sm["beta"], 0), MUL, s_=dve_read)
        b = take("st")
        dve.wait_ge(decay_out, 4)
        for j in range(RT):
            stt(state_r[:, j, :], b[:, P * j:P * j + P], sm["fs"][:, j:j + 1], const("heads64"), MUL, MUL,
                s_=dve_read if j == RT - 1 else None)
        b = take("gp1")
        tt(h4(tmpd), h4(b), per_head(sm["egc"], 1), MUL, s_=dve_read)
        tt(r1, gvrow[:, 1, :], tmpd, SUB, s_=r1_ready)

        def h8(m):
            return m.rearrange("p (h n) -> p h n", h=RH)

        def b8(m):
            return m.unsqueeze(2).broadcast_to([P, RH, RD])

        def var(t):
            return sm["var"][:, 12 * t:12 * t + 12]

        def mean_squares(t, last):
            o = ycat[:, t, 0:512]
            tt(tmpd, o, o, MUL)
            reduce(var(t)[:, 0:GH], h4(tmpd), ADD)
            ts(var(t)[:, 0:GH], var(t)[:, 0:GH], 1.0 / GD, RMS_EPS, MUL, ADD, s_=var_ready if last else None)

        def centre(t, last):
            dve.wait_ge(*plan.emptied(f"y{t}"))
            o = ycat[:, t, 512:1024]
            reduce(sm["stat"], h8(o), ADD)
            ts(sm["stat"], sm["stat"], 1.0 / RD, None, MUL)
            tt(h8(o), h8(o), b8(sm["stat"]), SUB)
            tt(tmpd, o, o, MUL)
            reduce(var(t)[:, GH:12], h8(tmpd), ADD)
            ts(var(t)[:, GH:12], var(t)[:, GH:12], 1.0 / RD, LN_EPS, MUL, ADD, s_=var_ready if last else None)

        def rwkv_output(t):
            dve.wait_ge(deviation_ready, t + 1)
            then(V.reciprocal(var(t), var(t)), inverse_ready)
            dve.wait_ge(terms_ready, t + 1)
            o = ycat[:, t, 512:1024]
            tt(h8(o), h8(o), b8(var(t)[:, GH:12]), MUL)
            tt(h4(o), h4(o), lnw, MUL)
            tt(o, o, vb[:, t, :], ADD)
            b_ = take(f"lg{t}")
            tt(o, o, b_, MUL, s_=dve_read)
            then(V.memset(sm["mark"], 0.0), ycat_ready)

        centre(0, False)
        b = take("gz1")
        dve.wait_ge(made, plan.made("go0"))
        tt(h4(vnew), h4(b), per_head(sm["beta"], 1), MUL, s_=dve_read)
        dve.wait_ge(*plan.emptied("go0"))
        mean_squares(0, True)
        b = take("gos")
        tt(h4(tmpd), h4(b), per_head(sm["egc"], 1), MUL, s_=dve_read)
        dve.wait_ge(*plan.emptied("go1"))
        tt(ycat[:, 1, 0:512], ycat[:, 1, 0:512], tmpd, ADD)
        mean_squares(1, False)
        rwkv_output(0)
        centre(1, True)
        rwkv_output(1)

        def add_residual(prefix):
            for t in range(NT):
                for half in range(2):
                    b_ = take(f"{prefix}{t}{half}")
                    o = X[:, t, 512 * half:512 * half + 512]
                    tt(o, o, b_, ADD, s_=dve_read)
                then(V.memset(sm["mark"], 0.0), x_ready)

        columns_low_of([f"yt{n}" for n in range(4)])
        add_residual("op")

        def pairs(m, n=4):
            return m.rearrange("p (t n) -> p t n", t=NT)

        def top(dst, src, best):
            tt(pairs(dst), pairs(src), best.unsqueeze(2).broadcast_to([P, NT, 4]), EQ)
            tt(pairs(dst), pairs(dst), const("rank4").unsqueeze(1).broadcast_to([P, NT, 4]), MUL)
            reduce(sm["gt2"], pairs(dst), MAX)
            tt(pairs(dst), pairs(dst), sm["gt2"].unsqueeze(2).broadcast_to([P, NT, 4]), EQ)

        def route(tag, layer):
            b_ = take(f"{tag}rt")
            then(V.tensor_copy(logitsT[:, :], b_[0:NG + NE, 0:S]), dve_read)
            b_ = take(f"{tag}rl")
            then(V.tensor_copy(sm["logits"], b_[:, 0:40]), dve_read)
            lg = sm["logits"].rearrange("p (t n) -> p t n", t=NT)
            reduce(sm["gm"], lg[:, :, 0:NG], MAX)
            tt(pairs(sm["ge"]), lg[:, :, 0:NG], sm["gm"].unsqueeze(2).broadcast_to([P, NT, NG]), SUB, s_=route_in)
            then(V.tensor_copy(pairs(sm["gt"]), lg[:, :, 0:NG]))
            top(sm["goh"], sm["gt"], sm["gm"])
            lows(MOE[layer] + 4)
            el = lg[:, :, NG:NG + NE].rearrange("p t (g e) -> p t e g", g=NG)
            prod = gates.rearrange("p t (e g) -> p t e g", g=NG)
            tt(prod, el, pairs(sm["goh"]).unsqueeze(2).broadcast_to([P, NT, 4, NG]), MUL)
            reduce(pairs(sm["sel"]), prod, ADD)
            reduce(sm["v1"], pairs(sm["sel"]), MAX)
            top(sm["oh1"], sm["sel"], sm["v1"])
            stt(sm["s2"], sm["oh1"], -3.0e38, sm["sel"], MUL, ADD)
            reduce(sm["v2"], pairs(sm["s2"]), MAX)
            tt(sm["dv"], sm["v2"], sm["v1"], SUB, s_=route_in)
            top(sm["oh2"], sm["s2"], sm["v2"])
            lows(MOE[layer] + 6)
            dve.wait_ge(route_exp, 2 * layer + 2)
            reduce(sm["pg"], pairs(sm["ge"]), ADD)
            then(V.reciprocal(sm["pg"], sm["pg"]))
            ts(sm["i1"], sm["dv"], 1.0, None, ADD)
            then(V.reciprocal(sm["i1"], sm["i1"]))
            tt(sm["i1"], sm["i1"], sm["pg"], MUL)
            tt(sm["i2"], sm["i1"], sm["dv"], MUL)
            tt(pairs(sm["oh1"]), pairs(sm["oh1"]), sm["i1"].unsqueeze(2).broadcast_to([P, NT, 4]), MUL)
            tt(pairs(sm["oh2"]), pairs(sm["oh2"]), sm["i2"].unsqueeze(2).broadcast_to([P, NT, 4]), MUL)
            tt(sm["inn"], sm["oh1"], sm["oh2"], ADD)
            for t in range(NT):
                ins = V.tensor_tensor(gates[:, t, :].rearrange("p (g e) -> p g e", g=NG),
                                      pairs(sm["goh"])[:, t, :].unsqueeze(2).broadcast_to([P, NG, 4]),
                                      pairs(sm["inn"])[:, t, :].unsqueeze(1).broadcast_to([P, NG, 4]), MUL)
                then(ins)

        def moe(tag, layer):
            route(tag, layer)

            def gate(e, i=None):
                v = NE * layer + e + 1
                dve.wait_ge(silu_done, v if i is None else i * 2 + v)
                for t in range(NT):
                    ge = gates[:, t, e:e + 1] if i is None else gates[:, t, bass.ds(i * 2 + e, 1)]
                    ins_ = V.scalar_tensor_tensor(out=moeg[:, t, :], in0=moes[:, t, :], scalar=ge,
                                                  in1=psum[:, 4 + 2 * (e % 2) + t, FF:2 * FF], op0=MUL, op1=MUL)
                ins_.then_inc(g_made, 1)

            def transposed_low(e, i=None):
                v = NE * layer + e + 1
                dve.wait_ge(gT_high, v if i is None else i * 2 + v)
                V.tensor_tensor(moegTl[:, :, :, :].rearrange("p t k n -> p t (k n)"),
                                psum[:, 4 + 2 * (e % 2):6 + 2 * (e % 2), 0:FF],
                                moegTh[:, :, :, :].rearrange("p t k n -> p t (k n)").bitcast(F32),
                                SUB).then_inc(gT_low, 1)

            def dve_step(e, i=None):
                for u in range(3) if e > 1 else (2,):
                    low_part(step_unit(layer, e, u), i)
                transposed_low(e - 1, i)
                for u in range(3, 6):
                    low_part(step_unit(layer, e, u), i)
                gate(e, i)

            gate(0)
            dve_step(1)
            with dve.Fori(0, NE // 2 - 1) as i:
                dve_step(2, i)
                dve_step(3, i)
            split[0] = step_unit(layer, NE, 0)
            transposed_low(NE - 1)
            lows(split[0] + 2)
            for t in range(NT):
                dve.wait_ge(*((y_made, NE * (layer + 1)) if t else (first_sums, layer + 1)))
                for half in range(2):
                    o = X[:, t, 512 * half:512 * half + 512]
                    tt(o, o, psum[:, 2 * t + half, :], ADD, s_=x_ready if half else None)

        rms_rows("b", 1)
        moe("b", 0)
        rms_rows("c", 2)
        half_d = AD // 2
        ang, turns, sin_, cos_ = (trig[:, 64 * n:64 * n + 64] for n in range(4))
        posf = sm["posf"]
        then(V.tensor_copy(posf, possb[:, :]))
        tt(pairs(ang), posf.unsqueeze(2).broadcast_to([P, NT, half_d]),
           const("invf").unsqueeze(1).broadcast_to([P, NT, half_d]), MUL)
        ROUND = 12582912.0
        ts(turns, ang, float(1.0 / (2.0 * np.pi)), None, MUL)
        ts(turns, turns, ROUND, None, ADD)
        ts(turns, turns, ROUND, None, SUB)
        two_pi = 2.0 * np.pi
        p1 = 6.28125
        p2 = float(np.float32(np.round((two_pi - p1) * 2 ** 21) / 2 ** 21))
        p3 = two_pi - p1 - p2
        for part in (p1, p2, p3):
            stt(ang, turns, -part, ang, MUL, ADD)
        ts(sin_, ang, -3.14159, 3.14159, MAX, ALU.min)
        stt(cos_, sin_, -1.0, sin_, MUL, MAX)
        ts(cos_, cos_, -1.0, float(np.pi / 2), MUL, ADD, s_=trig_in)
        dve.wait_ge(trig_done, 1)
        ccos = w_(24704, 128).rearrange("p (t n) -> p t n", t=NT)
        csin = w_(24832, 128).rearrange("p (t n) -> p t n", t=NT)
        for a in range(2):
            then(V.tensor_copy(ccos[:, :, 32 * a:32 * a + 32], pairs(cos_)))
            ts(csin[:, :, 32 * a:32 * a + 32], pairs(sin_), 1.0 if a else -1.0, None, MUL)
        for s in range(6):
            for t in range(NT):
                n = NT * s + t
                lows(U_OD + 4 * s + 4 + Stream.SLOTS)
                b = take(f"s{s}{t}").rearrange("p (h a n) -> p h a n", h=8, a=2)
                if n >= 2:
                    dve.wait_ge(roped, n - 1)
                o = rtmp[:, n % 2, :, 0:512].rearrange("p s (h a n) -> p s h a n", h=8, a=2)
                for a in range(2):
                    cb = ccos[:, t, 32 * a:32 * a + 32].unsqueeze(1).broadcast_to([P, 8, 32])
                    sb_ = csin[:, t, 32 * a:32 * a + 32].unsqueeze(1).broadcast_to([P, 8, 32])
                    then(V.tensor_tensor(o[:, 0, :, a, :], b[:, :, a, :], cb, MUL))
                    ins = V.tensor_tensor(o[:, 1, :, a, :], b[:, :, 1 - a, :], sb_, MUL)
                    if a == 0:
                        then(ins)
                then(ins, dve_read)
                then(V.memset(sm["mark"], 0.0), rope_ready)
        lows(U_ODO + Stream.SLOTS)
        dve.wait_ge(d_mask, 16)

        def masked_scores(n):
            h, t = HT_[n]
            nk = P * (t + 1)
            m0 = 384 * t
            b_ = take(f"sc{h}{t}a")
            w = 384 if t == 0 else 512
            if n >= 2:
                dve.wait_ge(probs_ready, n - 1)
            o = scs[:, n % 2, :]
            stt(o[:, 0:w], b_[:, 0:w], float(AD) ** -0.5, masks[:, m0:m0 + w], MUL, ADD, s_=dve_read)
            if t:
                b_ = take(f"sc{h}{t}b")
                stt(o[:, 512:768], b_[:, 0:256], float(AD) ** -0.5, masks[:, m0 + 512:m0 + 768], MUL, ADD, s_=dve_read)
            v = slice(n % AB, n % AB + 1)
            reduce(sm["mx"][:, v], o[:, 0:AG * nk], MAX)
            ts(sm["nmx"][:, v], sm["mx"][:, v], -1.0, None, MUL, s_=scores_ready)

        for n in range(-AB, len(HT_)):
            if n >= 0:
                dve.wait_ge(probs_ready, n + 1)
                if n >= AB:
                    dve.wait_ge(*plan.emptied("pv%d%d" % HT_[n - AB]))
                v = slice(n % AB, n % AB + 1)
                then(V.reciprocal(sm["rden"][:, v], sm["den"][:, v]), rden_ready)
            if n + AB < len(HT_):
                masked_scores(n + AB)
        columns_low_of([f"at{n}" for n in range(2)])
        lows(MOE[1])
        add_residual("ao")
        rms_rows("d", 3)
        moe("d", 1)
        dve.wait_ge(d_fin, 16)
        for t in range(NT):
            dve.wait_ge(rms_ready, NT * 4 + t + 1)
            then(V.reciprocal(sm["rstd"][:, t:t + 1], sm["rstd"][:, t:t + 1]))
            stt(hn[:, t, :], X[:, t, :], sm["rstd"][:, t:t + 1], w_(0, D), MUL, MUL, s_=out_ready)


_INS = ['x', 'positions', 'ev_norm', 'ev_w_in', 'ev_w_out', 'gdn_conv_w', 'gdn_A_log', 'gdn_dt_bias', 'gdn_norm',
        'rwkv_mu', 'rwkv_w0', 'rwkv_w2', 'rwkv_a0', 'rwkv_a2', 'rwkv_g2', 'rwkv_k_k', 'rwkv_k_a', 'rwkv_r_k',
        'rwkv_ln_w', 'rwkv_ln_b', 'od_norm', 'od_w_in', 'od_w_out', 'ffn_norm', 'moe_w_group', 'moe_w_expert',
        'moe_w1', 'moe_w3', 'moe_w2', 'final_norm']


def kernel(**inputs):
    import numpy as _np
    import concourse.bacc as _bacc
    from concourse import mybir as _mybir
    from concourse.bass_utils import run_bass_kernel_spmd as _run

    nc = _bacc.Bacc("TRN2", target_bir_lowering=False, num_devices=1)
    arrays, args = {}, []
    given = {name: _np.ascontiguousarray(inputs[name]) for name in _INS}
    given["const_mats"], _, given["attn_masks"] = constants()
    for name, a in given.items():
        arrays[f"in_{name}_dram"] = a
        args.append(nc.dram_tensor(f"in_{name}_dram", a.shape, _mybir.dt.from_np(a.dtype), kind="ExternalInput").ap())
    args.append(nc.dram_tensor("out_0_dram", (1, S, D), _mybir.dt.float32, kind="ExternalOutput").ap())
    trunk(nc, *args)
    r = _run(nc, [arrays], core_ids=[0])
    return r.results[0]["out_0_dram"]
```
